# Optimizing a Trainium2 kernel written in Bass

```python
import math
import jax
import jax.numpy as jnp
from jax import lax
import numpy as np

D_MODEL = 1024
BATCH = 1
SEQ = 1024
DEPTH = 1

GRID_W = 64
CTX_LEN = 256
N_HEADS = 8
N_KV_HEADS = 2
HEAD_DIM = 64
GROUP = N_HEADS // N_KV_HEADS
ATTN_W = N_HEADS * HEAD_DIM
KV_W = N_KV_HEADS * HEAD_DIM
WINDOW = 128
BLOCK = 128
HYENA_W = D_MODEL // 2
HYENA_ORDER = 2
FILTER_BANDS = 16
FILTER_EMB = 1 + 2 * FILTER_BANDS
FILTER_HIDDEN = 64
DECAY_TARGET = 1e-2
FAST_DECAY_PCT = 0.3
SLOW_DECAY_PCT = 1.5
ROPE_BASE = 10000.0
AXIS_ROT = HEAD_DIM // 2
N_EXPERTS = 16
EC_CAPACITY = 2
D_FF = 2048
N_BRANCHES = 2
EPS = 1e-6
NEG = -1e30

OFF_Q = 3 * HYENA_W
OFF_K = OFF_Q + ATTN_W
OFF_V = OFF_K + KV_W
OFF_G = OFF_V + KV_W
IN_W = OFF_G + N_BRANCHES * D_MODEL

kernel_name = 'hybrid_hyena_swa_ec_dit_layer'

def _rms(x, g):
    xf = x.astype(jnp.float32)
    y = xf * lax.rsqrt(jnp.mean(xf * xf, axis=-1, keepdims=True) + EPS)
    return (y * g.astype(jnp.float32)).astype(x.dtype)

def _short_conv(u, w, b):
    L = u.shape[1]
    up = jnp.pad(u, ((0, 0), (1, 1), (0, 0)))
    return up[:, :L] * w[0] + up[:, 1:L + 1] * w[1] + up[:, 2:] * w[2] + b

def _hyena_filters(L, fw1, fb1, fw2, fb2, fw3, fb3, ffreq, fout):
    f32 = jnp.float32
    t = jnp.linspace(0.0, 1.0, L, dtype=f32)[:, None]
    w = 2.0 * math.pi * jnp.arange(L, dtype=f32)[:, None] / L
    fr = jnp.linspace(1e-4, FILTER_BANDS - 1, FILTER_BANDS, dtype=f32)[None, :]
    feat = jnp.concatenate([t, jnp.cos(fr * w), -jnp.sin(fr * w)], axis=-1)
    fq = ffreq.astype(f32)
    h = jnp.sin(fq * (feat @ fw1.astype(f32) + fb1.astype(f32)))
    h = jnp.sin(fq * (h @ fw2.astype(f32) + fb2.astype(f32)))
    h = jnp.sin(fq * (h @ fw3.astype(f32) + fb3.astype(f32)))
    h = (h @ fout.astype(f32)).reshape(L, HYENA_ORDER, 2, HYENA_W)
    min_decay = math.log(DECAY_TARGET) / SLOW_DECAY_PCT
    max_decay = math.log(DECAY_TARGET) / FAST_DECAY_PCT
    deltas = jnp.linspace(min_decay, max_decay, HYENA_W, dtype=f32)
    decay = jnp.exp(-t * jnp.abs(deltas))
    h = h * decay[:, None, None, :]
    k = jnp.concatenate([h[:, :, 0], jnp.zeros((1, HYENA_ORDER, HYENA_W), f32), h[:0:-1, :, 1]], axis=0)
    return jnp.fft.rfft(k, axis=0)

def _hyena(u, conv_w, conv_b, kf, hyena_bias):
    L = u.shape[1]
    z = _short_conv(u, conv_w, conv_b)
    v, x1, x2 = jnp.split(z, 3, axis=-1)
    y = v.astype(jnp.float32)
    for o, gate in enumerate((x1, x2)):
        yf = jnp.fft.rfft(y, n=2 * L, axis=1)
        y = jnp.fft.irfft(yf * kf[:, o], n=2 * L, axis=1)[:, :L] + hyena_bias[o].astype(jnp.float32) * y
        y = gate.astype(jnp.float32) * y
    return y.astype(u.dtype)

def _axial_rope(L):
    rows = L // GRID_W
    f32 = jnp.float32
    row = jnp.repeat(jnp.arange(rows, dtype=f32), GRID_W)
    col = jnp.tile(jnp.arange(GRID_W, dtype=f32), rows)
    inv = ROPE_BASE ** (-jnp.arange(0, AXIS_ROT, 2, dtype=f32) / AXIS_ROT)
    ang = jnp.concatenate([row[:, None] * inv, col[:, None] * inv], axis=-1)
    return jnp.cos(ang)[None, :, None, :], jnp.sin(ang)[None, :, None, :]

def _rope(x, cos, sin):
    xf = x.astype(jnp.float32)
    xe, xo = xf[..., 0::2], xf[..., 1::2]
    out = jnp.stack([xe * cos - xo * sin, xe * sin + xo * cos], axis=-1).reshape(x.shape)
    return out.astype(x.dtype)

def _window_attention(q, k, v, kc, vc, sink):
    B, L = q.shape[:2]
    nb = L // BLOCK
    nw = 3 * BLOCK
    nc = kc.shape[1]
    scale = HEAD_DIM ** -0.5
    qb = q.reshape(B, nb, BLOCK, N_KV_HEADS, GROUP, HEAD_DIM)

    def bands(t):
        tp = jnp.pad(t, ((0, 0), (BLOCK, BLOCK), (0, 0), (0, 0))).reshape(B, nb + 2, BLOCK, N_KV_HEADS, HEAD_DIM)
        return jnp.concatenate([tp[:, :-2], tp[:, 1:-1], tp[:, 2:]], axis=2)

    kw, vw = bands(k), bands(v)
    s_win = jnp.einsum('bnqhgd,bnkhd->bnhgqk', qb, kw).astype(jnp.float32) * scale
    rel = jnp.arange(nw)[None, :] - BLOCK - jnp.arange(BLOCK)[:, None]
    kpos = (jnp.arange(nb)[:, None] - 1) * BLOCK + jnp.arange(nw)[None, :]
    mask = (jnp.abs(rel) <= WINDOW)[None] & ((kpos >= 0) & (kpos < L))[:, None, :]
    s_win = jnp.where(mask[None, :, None, None], s_win, NEG)
    s_ctx = jnp.einsum('bnqhgd,bchd->bnhgqc', qb, kc).astype(jnp.float32) * scale
    snk = jnp.broadcast_to(sink.astype(jnp.float32).reshape(N_KV_HEADS, GROUP)[None, None, :, :, None, None],
                           s_win.shape[:-1] + (1,))
    p = jax.nn.softmax(jnp.concatenate([s_win, s_ctx, snk], axis=-1), axis=-1)
    o = (jnp.einsum('bnhgqk,bnkhd->bnqhgd', p[..., :nw].astype(v.dtype), vw)
         + jnp.einsum('bnhgqc,bchd->bnqhgd', p[..., nw:nw + nc].astype(v.dtype), vc))
    return o.reshape(B, L, ATTN_W)

def _ctx_attention(qc, kc, vc, sink):
    B, Lc = qc.shape[:2]
    q = qc.reshape(B, Lc, N_KV_HEADS, GROUP, HEAD_DIM)
    s = jnp.einsum('bqhgd,bkhd->bhgqk', q, kc).astype(jnp.float32) * (HEAD_DIM ** -0.5)
    snk = jnp.broadcast_to(sink.astype(jnp.float32).reshape(N_KV_HEADS, GROUP)[None, :, :, None, None],
                           s.shape[:-1] + (1,))
    p = jax.nn.softmax(jnp.concatenate([s, snk], axis=-1), axis=-1)
    o = jnp.einsum('bhgqk,bkhd->bqhgd', p[..., :Lc].astype(vc.dtype), vc)
    return o.reshape(B, Lc, ATTN_W)

def _merge(y_a, y_b, gate_logits, w_branch_a, w_branch_b, w_out):
    ga, gb = jnp.split(jax.nn.sigmoid(gate_logits), 2, axis=-1)
    return (ga * (y_a @ w_branch_a) + gb * (y_b @ w_branch_b)) @ w_out

def _expert_choice(h, router, w_gate, w_up, w_down):
    B, L, D = h.shape
    cap = EC_CAPACITY * L // N_EXPERTS
    aff = jax.nn.softmax((h @ router).astype(jnp.float32), axis=-1)
    g, idx = lax.top_k(jnp.swapaxes(aff, 1, 2), cap)
    idx_flat = idx.reshape(B, N_EXPERTS * cap)
    bidx = jnp.arange(B)[:, None]
    xin = h[bidx, idx_flat].reshape(B, N_EXPERTS, cap, D)
    a = jnp.einsum('becd,edf->becf', xin, w_gate)
    b = jnp.einsum('becd,edf->becf', xin, w_up)
    y = jnp.einsum('becf,efd->becd', jax.nn.silu(a) * b, w_down)
    y = (y * g[..., None].astype(y.dtype)).reshape(B, N_EXPERTS * cap, D)
    return jnp.zeros_like(h).at[bidx, idx_flat].add(y)

def _layer(x, ctx, mod_x, mod_c, norm1, norm2, w_in, conv_w, conv_b, filt, hyena_bias,
           q_norm, k_norm, attn_sink, w_branch_a, w_branch_b, w_out, router, w_gate, w_up, w_down,
           update_ctx):
    B, L, _ = x.shape
    Lc = ctx.shape[1]
    sh1, sc1, g1, sh2, sc2, g2 = jnp.split(mod_x, 6, axis=-1)
    ch1, cc1, cg1, ch2, cc2, cg2 = jnp.split(mod_c, 6, axis=-1)

    hc = _rms(ctx, norm1) * (1 + cc1) + ch1
    if update_ctx:
        zc = hc @ w_in
        kvc = zc[..., OFF_K:OFF_G]
    else:
        kvc = hc @ w_in[:, OFF_K:OFF_G]
    kc = _rms(kvc[..., :KV_W].reshape(B, Lc, N_KV_HEADS, HEAD_DIM), k_norm)
    vc = kvc[..., KV_W:].reshape(B, Lc, N_KV_HEADS, HEAD_DIM)

    hx = _rms(x, norm1) * (1 + sc1) + sh1
    zx = hx @ w_in
    y_a = _hyena(zx[..., :OFF_Q], conv_w, conv_b, _hyena_filters(L, *filt), hyena_bias)
    cos, sin = _axial_rope(L)
    q = _rope(_rms(zx[..., OFF_Q:OFF_K].reshape(B, L, N_HEADS, HEAD_DIM), q_norm), cos, sin)
    k = _rope(_rms(zx[..., OFF_K:OFF_V].reshape(B, L, N_KV_HEADS, HEAD_DIM), k_norm), cos, sin)
    v = zx[..., OFF_V:OFF_G].reshape(B, L, N_KV_HEADS, HEAD_DIM)
    y_b = _window_attention(q, k, v, kc, vc, attn_sink)
    x_new = x + g1 * _merge(y_a, y_b, zx[..., OFF_G:], w_branch_a, w_branch_b, w_out)
    hx2 = _rms(x_new, norm2) * (1 + sc2) + sh2
    x_new = x_new + g2 * _expert_choice(hx2, router, w_gate, w_up, w_down)

    ctx_new = ctx
    if update_ctx:
        y_ac = _hyena(zc[..., :OFF_Q], conv_w, conv_b, _hyena_filters(Lc, *filt), hyena_bias)
        qc = _rms(zc[..., OFF_Q:OFF_K].reshape(B, Lc, N_HEADS, HEAD_DIM), q_norm)
        y_bc = _ctx_attention(qc, kc, vc, attn_sink)
        ctx_new = ctx + cg1 * _merge(y_ac, y_bc, zc[..., OFF_G:], w_branch_a, w_branch_b, w_out)
        hc2 = _rms(ctx_new, norm2) * (1 + cc2) + ch2
        ctx_new = ctx_new + cg2 * _expert_choice(hc2, router, w_gate, w_up, w_down)
    return x_new, ctx_new

def setup_inputs(seed: int = 0) -> dict:
    key = jax.random.key(seed)
    ks = jax.random.split(key, 32)
    f32 = jnp.float32
    D = D_MODEL

    def nrm(k, shape, scale):
        return jax.random.normal(k, shape, f32) * scale

    return {
        'x': nrm(ks[0], (BATCH, SEQ, D), 1.0),
        'c': nrm(ks[1], (BATCH, D), 1.0),
        'ctx': nrm(ks[2], (BATCH, CTX_LEN, D), 1.0),
        'c_ctx': nrm(ks[3], (D,), 1.0),
        'ada_w': nrm(ks[4], (DEPTH, D, 6 * D), 0.5 * D ** -0.5),
        'ada_b': nrm(ks[5], (DEPTH, 6 * D), 0.02),
        'norm1': 1.0 + nrm(ks[6], (DEPTH, D), 0.02),
        'norm2': 1.0 + nrm(ks[7], (DEPTH, D), 0.02),
        'w_in': nrm(ks[8], (DEPTH, D, IN_W), D ** -0.5),
        'conv_w': nrm(ks[9], (DEPTH, 3, 3 * HYENA_W), 3 ** -0.5),
        'conv_b': nrm(ks[10], (DEPTH, 3 * HYENA_W), 0.02),
        'filt_w1': nrm(ks[11], (DEPTH, FILTER_EMB, FILTER_HIDDEN), FILTER_EMB ** -0.5),
        'filt_b1': nrm(ks[12], (DEPTH, FILTER_HIDDEN), 0.02),
        'filt_w2': nrm(ks[13], (DEPTH, FILTER_HIDDEN, FILTER_HIDDEN), FILTER_HIDDEN ** -0.5),
        'filt_b2': nrm(ks[14], (DEPTH, FILTER_HIDDEN), 0.02),
        'filt_w3': nrm(ks[15], (DEPTH, FILTER_HIDDEN, FILTER_HIDDEN), FILTER_HIDDEN ** -0.5),
        'filt_b3': nrm(ks[16], (DEPTH, FILTER_HIDDEN), 0.02),
        'filt_freq': 1.0 + nrm(ks[17], (DEPTH, FILTER_HIDDEN), 0.02),
        'filt_out': nrm(ks[18], (DEPTH, FILTER_HIDDEN, HYENA_ORDER * 2 * HYENA_W), 0.05 * FILTER_HIDDEN ** -0.5),
        'hyena_bias': nrm(ks[19], (DEPTH, HYENA_ORDER, HYENA_W), 0.5),
        'q_norm': 1.0 + nrm(ks[20], (DEPTH, HEAD_DIM), 0.02),
        'k_norm': 1.0 + nrm(ks[21], (DEPTH, HEAD_DIM), 0.02),
        'attn_sink': nrm(ks[22], (DEPTH, N_HEADS), 0.5),
        'w_branch_a': nrm(ks[23], (DEPTH, HYENA_W, D), HYENA_W ** -0.5),
        'w_branch_b': nrm(ks[24], (DEPTH, ATTN_W, D), ATTN_W ** -0.5),
        'w_out': nrm(ks[25], (DEPTH, D, D), D ** -0.5),
        'router': nrm(ks[26], (DEPTH, D, N_EXPERTS), D ** -0.5),
        'w_gate': nrm(ks[27], (DEPTH, N_EXPERTS, D, D_FF), D ** -0.5),
        'w_up': nrm(ks[28], (DEPTH, N_EXPERTS, D, D_FF), D ** -0.5),
        'w_down': nrm(ks[29], (DEPTH, N_EXPERTS, D_FF, D), D_FF ** -0.5),
    }

def reference(x, c, ctx, c_ctx, ada_w, ada_b, norm1, norm2, w_in, conv_w, conv_b,
              filt_w1, filt_b1, filt_w2, filt_b2, filt_w3, filt_b3, filt_freq, filt_out,
              hyena_bias, q_norm, k_norm, attn_sink, w_branch_a, w_branch_b, w_out,
              router, w_gate, w_up, w_down):
    for l in range(DEPTH):
        mod_x = (jax.nn.silu(c) @ ada_w[l] + ada_b[l])[:, None, :]
        mod_c = (jax.nn.silu(c_ctx) @ ada_w[l] + ada_b[l])[None, None, :]
        filt = (filt_w1[l], filt_b1[l], filt_w2[l], filt_b2[l], filt_w3[l], filt_b3[l], filt_freq[l], filt_out[l])
        x, ctx = _layer(x, ctx, mod_x, mod_c, norm1[l], norm2[l], w_in[l], conv_w[l], conv_b[l], filt,
                        hyena_bias[l], q_norm[l], k_norm[l], attn_sink[l], w_branch_a[l], w_branch_b[l],
                        w_out[l], router[l], w_gate[l], w_up[l], w_down[l], l < DEPTH - 1)
    return x


_drawn_inputs = setup_inputs


def setup_inputs(seed=0):
    import zlib

    import numpy as np

    out = dict(_drawn_inputs(seed))
    spreads = {}
    factors = {'ctx': 5.868,
     'ada_b': 3.804,
     'norm1': 8.0,
     'norm2': 28.031,
     'conv_b': 8.0,
     'filt_b1': 6.303,
     'filt_b2': 5.316,
     'filt_b3': 4.033,
     'filt_freq': 8.0,
     'q_norm': 64.0,
     'k_norm': 64.0,
     'attn_sink': 8.0}
    for name, (base, spread) in spreads.items():
        noise = np.random.default_rng([zlib.crc32(name.encode()), seed]).standard_normal(out[name].shape)
        drawn = base * np.exp(spread * noise) if base else spread * noise
        out[name] = jnp.asarray(drawn.astype(out[name].dtype))
    for name, factor in factors.items():
        out[name] = (out[name] * factor).astype(out[name].dtype)
    return out
```

```python
from contextlib import ExitStack

import numpy as np

import concourse.bass as bass
from concourse import mybir

P = 128
D = 1024
L = 1024
LC = 256
KD = D // P
NT = L // P
NTC = LC // P
NTA = NT + NTC
LA = L + LC
HY = 512
NCH = HY // P
NH = 8
NKV = 2
HD = 64
OFF_Q = 3 * HY
OFF_G = OFF_Q + NH * HD + 2 * NKV * HD
QKV = OFF_G - OFF_Q
NE = 16
CAP = 2 * L // NE
FF = 2048
BANDS = 16
EMB = 1 + 2 * BANDS
FH = 64
EPS = 1e-6
NEG = -1e30
GRID_W = 64
ROT = HD // 2

F32 = mybir.dt.float32
F32R = mybir.dt.float32r
BF16 = mybir.dt.bfloat16
I32 = mybir.dt.int32
U32 = mybir.dt.uint32
ALU = mybir.AluOpType
ACT = mybir.ActivationFunctionType
AX = mybir.AxisListType.X

UW = 256
QKV_UNITS = QKV // UW
HY_UNITS = OFF_Q // UW
G_UNITS = 2 * D // UW
UNITS = QKV_UNITS + HY_UNITS + G_UNITS


def unit_column(u):
    if u < QKV_UNITS:
        return OFF_Q + u * UW
    if u < QKV_UNITS + HY_UNITS:
        return (u - QKV_UNITS) * UW
    return OFF_G + (u - QKV_UNITS - HY_UNITS) * UW


def shape_constants():
    f = np.float32
    t = np.linspace(0.0, 1.0, L, dtype=f)[:, None]
    w = (f(2.0 * np.pi) * np.arange(L, dtype=f)[:, None] / f(L)).astype(f)
    fr = np.linspace(1e-4, BANDS - 1, BANDS, dtype=f)[None, :]
    feat = np.concatenate([t, np.cos((fr * w).astype(f)), -np.sin((fr * w).astype(f))], axis=-1).astype(f)
    lo, hi = np.log(1e-2) / 1.5, np.log(1e-2) / 0.3
    deltas = np.linspace(lo, hi, HY, dtype=f)
    decay = np.exp(-t * np.abs(deltas)).astype(f)
    order = np.concatenate([np.arange(0, L, 2), np.arange(1, L, 2)])
    row = np.repeat(np.arange(L // GRID_W, dtype=f), GRID_W)
    col = np.tile(np.arange(GRID_W, dtype=f), L // GRID_W)
    inv = (f(10000.0) ** (-np.arange(0, ROT, 2, dtype=f) / f(ROT))).astype(f)
    ang = np.concatenate([row[:, None] * inv, col[:, None] * inv], axis=-1).astype(f)
    fq = np.pi * (2 * np.arange(L // 2)[:, None] + 1) / (2 * L)
    j = np.arange(L // 2)[None, :]
    ce, se = np.cos(fq * 2 * j), np.sin(fq * 2 * j)
    co, so = np.cos(fq * (2 * j + 1)), np.sin(fq * (2 * j + 1))
    fourier = np.stack([ce.T, co, se.T, so, ce, se]).astype(f)
    return {
        "feat": np.ascontiguousarray(feat[order].T),
        "decay": np.ascontiguousarray(decay[order] / f(L)),
        "rope_cos": np.cos(ang).astype(f),
        "rope_sin": np.sin(ang).astype(f),
        "fourier": fourier,
    }


def build(nc, A, out):
    root = ExitStack()
    with root:
        def sem(name):
            return root.enter_context(nc.semaphore(name))

        def scope(stack):
            def sb(name, shape, dt=F32):
                return stack.enter_context(nc.sbuf_tensor(name, shape, dt))

            def ps(name, shape, dt=F32):
                return stack.enter_context(nc.psum_tensor(name, shape, dt))
            return sb, ps

        g = {"nc": nc, "sem": sem, "scope": scope, "A": A, "out": out}
        sb, _ = scope(root)
        g["z_dram"] = nc.dram_tensor("z_dram", [OFF_Q, L], F32).ap()
        g["gate_dram"] = nc.dram_tensor("gate_dram", [2 * D, L], F32).ap()
        g["yb_dram"] = nc.dram_tensor("yb_dram", [NH * HD, L], F32).ap()
        g["xn2_dram"] = nc.dram_tensor("xn2_dram", [L, D], F32).ap()
        g["ident"] = sb("ident", [P, P])
        g["ones"] = sb("ones", [P, P])
        g["cols1"] = sb("cols1", [P, 80])
        g["cols2"] = sb("cols2", [P, 56])
        g["A2"] = sb("A2", [P, KD])
        g["mod"] = sb("mod", [P, 48, 2])
        g["g1row"] = sb("g1row", [P, D])
        g["g2row"] = sb("g2row", [P, D])
        g["affT"] = sb("affT", [NE, L])
        with ExitStack() as s12:
            sb12, _ = scope(s12)
            g["qkv"] = sb12("qkv", [P, NTA, QKV])
            with ExitStack() as s:
                sbh, _ = scope(s)
                g["h_hi"] = sbh("h_hi", [P, KD, LA], F32R)
                g["h_lo"] = sbh("h_lo", [P, KD, LA], F32R)
                modulation(g)
                projection(g)
            attention(g)
        with ExitStack() as s:
            sby, _ = scope(s)
            g["ya"] = sby("ya", [P, NCH, L])
            hyena(g)
            merge(g)
        with ExitStack() as s:
            sbe, _ = scope(s)
            g["idx"] = sbe("idx", [P, NE], U32)
            g["gate"] = sbe("gate", [P, NE])
            choice(g)
            experts(g)


def modulation(g):
    nc, sem, A = g["nc"], g["sem"], g["A"]
    ident, ones, cols1, cols2, mod = g["ident"], g["ones"], g["cols1"], g["cols2"], g["mod"]
    h_hi, h_lo = g["h_hi"], g["h_lo"]
    GROUPS = [(h, k) for h in range(3) for k in range(KD)]
    with ExitStack() as s:
        sb, ps = g["scope"](s)
        rows1, rows2 = sb("rows1", [80, P]), sb("rows2", [56, P])
        sil, sig = sb("sil", [P, 2, KD]), sb("sig", [P, 2 * KD])
        ada = sb("ada", [P, 2, KD, 512])
        x = sb("x_in", [P, NTA, D])
        ss, rt, r0, tt = (sb(n, [P, NTA]) for n in ("ss", "rt", "r0", "tt"))
        scale = sb("mod_scale", [P, KD, 2])
        hf = sb("hf", [P, 3, 512])
        junk = hf[:].rearrange("p a n -> p (a n)")[:, 0:D]
        diag = sb("diag", [P, 2, P])
        p_rows = ps("p_rows", [P, 512])
        p_mod = ps("p_mod", [P, 512])
        p_x = ps("p_x", [P, 3, 512])
        p_g = ps("p_g", [P, 2, 512])
        rows_in, rows2_in = sem("rows_in"), sem("rows2_in")
        ada_in = [sem(f"ada_in{i}") for i in range(2)]
        x_in = [sem(f"x_in{t}") for t in range(NTA)]
        consts = sem("consts")
        rows_t, cols_ready = sem("rows_t"), sem("cols_ready")
        sig_ready, sil_ready = sem("sig_ready"), sem("sil_ready")
        section_done = sem("section_done")
        mod_ready = sem("mod_ready")
        ss_ready, root_ready, norm_step, xn_ready = sem("ss_ready"), sem("root_ready"), sem("norm_step"), sem("xn_ready")
        x_t, h_f, hi_ready, lo_ready = sem("x_t"), sem("h_f"), sem("h_hi_ready"), sem("h_lo_ready")
        diag_ready, g_done, g_copied = sem("diag_ready"), sem("g_done"), sem("g_copied")
        SECTIONS = 6 * D // 512

        def tokens(h):
            return (512 * h, 512) if h < 2 else (L, LC)

        with nc.Block() as block:
            @block.sync
            def _(sp):
                at = 0
                for name, n in (("ada_b", 48), ("norm1", 8), ("norm2", 8), ("c", 8)):
                    sp.dma_start(rows1[at:at + n, :], A[name].rearrange("o (j p) -> (o j) p", p=P)).then_inc(rows_in, 16)
                    at += n
                sp.dma_start(rows1[at:at + 8, :], A["c_ctx"].rearrange("(j p) -> j p", p=P)).then_inc(rows_in, 16)
                sp.dma_start(rows2[0:36, :], A["conv_w"].rearrange("o r (j p) -> (o r j) p", p=P)).then_inc(rows2_in, 16)
                sp.dma_start(rows2[36:48, :], A["conv_b"].rearrange("o (j p) -> (o j) p", p=P)).then_inc(rows2_in, 16)
                sp.dma_start(rows2[48:56, :], A["hyena_bias"].rearrange("o r (j p) -> (o r j) p", p=P)).then_inc(rows2_in, 16)
                for s_ in range(SECTIONS):
                    if s_ >= 2:
                        sp.wait_ge(section_done, s_ - 1)
                    sp.dma_start(ada[:, s_ % 2], A["ada_w"][0][:, 512 * s_:512 * s_ + 512]
                                 .rearrange("(k p) n -> p k n", p=P)).then_inc(ada_in[s_ % 2], 16)

            @block.gpsimd
            def _(pool):
                pool.memset(ident[:], 0.0).then_inc(consts, 1)
                pool.memset(ones[:], 1.0).then_inc(consts, 1)
                pool.wait_ge(consts, 2)
                pool.affine_select(out=ident[:], in_=ident[:], compare_op=ALU.not_equal, fill=1.0, base=0,
                                   pattern=[[-1, P]], channel_multiplier=1).then_inc(consts, 1)

            @block.scalar
            def _(act):
                for t in range(NTA):
                    src = A["x"][0, P * t:P * t + P, :] if t < NT else A["ctx"][0, P * (t - NT):P * (t - NT) + P, :]
                    act.dma_start(x[:, t, :], src).then_inc(x_in[t], 16)
                act.wait_ge(cols_ready, 1)
                act.activation(sig[:], cols1[:, 64:80], ACT.Sigmoid).then_inc(sig_ready, 1)
                for t in range(NTA):
                    act.wait_ge(x_in[t], 16)
                    if t:
                        act.wait_ge(ss_ready, t)
                    act.activation(junk, x[:, t, :], ACT.Square, accum_out=ss[:, t:t + 1]).then_inc(ss_ready, 1)
                act.wait_ge(norm_step, 1)
                act.activation(rt[:], ss[:], ACT.Sqrt).then_inc(root_ready, 1)
                for i, (h, k) in enumerate(GROUPS):
                    a, n = tokens(h)
                    act.wait_ge(h_f, i + 1)
                    act.activation(h_hi[:, k, a:a + n], hf[:, i % 3, :n], ACT.Copy).then_inc(hi_ready, 1)

            @block.vector
            def _(dve):
                dve.wait_ge(rows_t, 1)
                dve.tensor_copy(cols1[:], p_rows[:, 0:80]).then_inc(cols_ready, 1)
                dve.tensor_copy(cols2[:], p_rows[:, 80:136]).then_inc(cols_ready, 1)
                dve.wait_ge(sig_ready, 1)
                dve.wait_ge(cols_ready, 2)
                dve.tensor_tensor(sil[:].rearrange("p s k -> p (s k)"), cols1[:, 64:80], sig[:], ALU.mult)\
                   .then_inc(sil_ready, 1)
                dve.wait_ge(ss_ready, NTA)
                dve.tensor_scalar(ss[:], ss[:], 1.0 / D, EPS, ALU.mult, ALU.add).then_inc(norm_step, 1)
                dve.wait_ge(root_ready, 1)
                dve.reciprocal(r0[:], rt[:]).then_inc(norm_step, 1)
                dve.wait_ge(norm_step, 2)
                dve.tensor_tensor(tt[:], r0[:], r0[:], ALU.mult).then_inc(norm_step, 1)
                dve.wait_ge(norm_step, 3)
                dve.tensor_tensor(tt[:], tt[:], ss[:], ALU.mult).then_inc(norm_step, 1)
                dve.wait_ge(norm_step, 4)
                dve.tensor_scalar(tt[:], tt[:], -0.5, 1.5, ALU.mult, ALU.add).then_inc(norm_step, 1)
                dve.wait_ge(norm_step, 5)
                dve.tensor_tensor(r0[:], r0[:], tt[:], ALU.mult).then_inc(norm_step, 1)
                dve.wait_ge(norm_step, 6)
                for t in range(NTA):
                    dve.tensor_scalar(x[:, t, :], x[:, t, :], r0[:, t:t + 1], None, ALU.mult).then_inc(xn_ready, 1)
                dve.wait_ge(section_done, SECTIONS)
                for v in range(2):
                    dve.tensor_tensor(mod[:, :, v], p_mod[:, v:96:2], cols1[:, 0:48], ALU.add).then_inc(mod_ready, 1)
                dve.wait_ge(mod_ready, 2)
                for v in range(2):
                    dve.scalar_tensor_tensor(out=scale[:, :, v], in0=mod[:, 8:16, v], scalar=1.0,
                                             in1=cols1[:, 48:56], op0=ALU.add, op1=ALU.mult).then_inc(mod_ready, 1)
                dve.scalar_tensor_tensor(out=g["A2"][:], in0=mod[:, 32:40, 0], scalar=1.0, in1=cols1[:, 56:64],
                                         op0=ALU.add, op1=ALU.mult).then_inc(mod_ready, 1)
                dve.wait_ge(mod_ready, 5)

                def modulate(i):
                    h, k = GROUPS[i]
                    v, n = int(h == 2), tokens(h)[1]
                    dve.wait_ge(x_t, i + 1)
                    if i >= 3:
                        dve.wait_ge(lo_ready, i - 2)
                    dve.tensor_scalar(hf[:, i % 3, :n], p_x[:, i % 3, :n], scale[:, k, v:v + 1], mod[:, k, v:v + 1],
                                      ALU.mult, ALU.add).then_inc(h_f, 1)

                def low_part(i):
                    h, k = GROUPS[i]
                    a, n = tokens(h)
                    dve.wait_ge(hi_ready, i + 1)
                    dve.tensor_tensor(h_lo[:, k, a:a + n], hf[:, i % 3, :n], h_hi[:, k, a:a + n].bitcast(F32),
                                      ALU.subtract).then_inc(lo_ready, 1)

                for i in range(len(GROUPS)):
                    modulate(i)
                    if i:
                        low_part(i - 1)
                low_part(len(GROUPS) - 1)
                for i in range(2 * KD):
                    if i >= 2:
                        dve.wait_ge(g_done, i - 1)
                    c = (16 if i < KD else 40) + i % KD
                    dve.tensor_scalar(diag[:, i % 2, :], ident[:], mod[:, c, 0:1], None, ALU.mult).then_inc(diag_ready, 1)
                    if i % 4 == 3:
                        row = g["g1row"] if i < KD else g["g2row"]
                        dve.wait_ge(g_done, i + 1)
                        q = i // 4
                        dve.tensor_copy(row[:, 512 * (q % 2):512 * (q % 2) + 512], p_g[:, q % 2, :]).then_inc(g_copied, 1)

            @block.tensor
            def _(pe):
                pe.wait_ge(consts, 3)
                pe.wait_ge(rows_in, 80)
                pe.wait_ge(rows2_in, 48)
                pe.transpose(p_rows[:, 0:80], rows1[:], ident[0:80, 0:80])
                pe.transpose(p_rows[:, 80:136], rows2[:], ident[0:56, 0:56]).then_inc(rows_t, 1)
                pe.wait_ge(sil_ready, 1)
                for s_ in range(SECTIONS):
                    pe.wait_ge(ada_in[s_ % 2], 16 * (s_ // 2 + 1))
                    for j in range(4):
                        for k in range(KD):
                            mm = pe.matmul(p_mod[:, 2 * (4 * s_ + j):2 * (4 * s_ + j) + 2],
                                           ada[:, s_ % 2, k, P * j:P * j + P], sil[:, :, k],
                                           start=k == 0, stop=k == KD - 1)
                    mm.then_inc(section_done, 1)
                for i, (h, k) in enumerate(GROUPS):
                    if i >= 3:
                        pe.wait_ge(h_f, i - 2)
                    tiles = range(4 * h, min(4 * h + 4, NTA))
                    pe.wait_ge(xn_ready, tiles[-1] + 1)
                    for n, t in enumerate(tiles):
                        mm = pe.transpose(p_x[:, i % 3, P * n:P * n + P], x[:, t, P * k:P * k + P], ident[:])
                    mm.then_inc(x_t, 1)
                for i in range(2 * KD):
                    pe.wait_ge(diag_ready, i + 1)
                    if i >= 8 and i % 4 == 0:
                        pe.wait_ge(g_copied, i // 4 - 1)
                    pe.matmul(p_g[:, (i // 4) % 2, P * (i % 4):P * (i % 4) + P], ones[:], diag[:, i % 2, :],
                              start=True, stop=True).then_inc(g_done, 1)


def three(pe, out, a_hi, a_lo, b_hi, b_lo, start, stop):
    pe.matmul(out, a_hi, b_hi, start=start, stop=False)
    pe.matmul(out, a_hi, b_lo, start=False, stop=False)
    return pe.matmul(out, a_lo, b_hi, start=False, stop=stop)


def projection(g):
    nc, sem, A = g["nc"], g["sem"], g["A"]
    h_hi, h_lo, qkv, cols2 = g["h_hi"], g["h_lo"], g["qkv"], g["cols2"]
    groups = []
    for u in range(UNITS):
        if u < QKV_UNITS:
            groups += [(u, t, None) for t in range(NTA if u == QKV_UNITS - 1 else NT)]
        else:
            groups += [(u, c, h) for c in range(2) for h in range(2)]
    first = {}
    for i, (u, _, _) in enumerate(groups):
        first.setdefault(u, i)
    first[UNITS] = len(groups)
    BANKS = 6
    with ExitStack() as s:
        sb, ps = g["scope"](s)
        w = sb("w_raw", [P, 2, KD, UW])
        w_hi = sb("w_hi", [P, 2, KD, UW], F32R)
        w_lo = sb("w_lo", [P, 2, KD, UW], F32R)
        ub = sb("ub", [P, 2, L + 2])
        t1 = sb("conv_t", [P, L])
        zs = sb("zs", [P, 2, L])
        gs = sb("gs", [P, 2, L])
        pz = ps("p_z", [P, BANKS, 512])
        w_in = [sem(f"w_in{i}") for i in range(2)]
        w_hi_ready, w_lo_ready = sem("w_hi_ready"), sem("w_lo_ready")
        group_done, evacuated = sem("group_done"), sem("evacuated")
        padded, conv_step, z_ready = sem("padded"), sem("conv_step"), sem("z_ready")
        z_stored = [sem(f"z_stored{i}") for i in range(2)]
        g_stored = [sem(f"g_stored{i}") for i in range(2)]
        NZ, NG = 2 * HY_UNITS, 2 * G_UNITS

        with nc.Block() as block:
            @block.sync
            def _(sp):
                def load(u):
                    if u >= 2:
                        sp.wait_ge(w_lo_ready, u - 1)
                    c = unit_column(u)
                    sp.dma_start(w[:, u % 2], A["w_in"][0][:, c:c + UW].rearrange("(k p) n -> p k n", p=P))\
                      .then_inc(w_in[u % 2], 16)
                load(0)
                load(1)
                for u in range(UNITS):
                    if u + 2 < UNITS:
                        load(u + 2)
                    if QKV_UNITS <= u < QKV_UNITS + HY_UNITS:
                        for c in range(2):
                            i = 2 * (u - QKV_UNITS) + c
                            sp.wait_ge(z_ready, i + 1)
                            sp.dma_start(g["z_dram"][P * i:P * i + P, :], zs[:, i % 2, :]).then_inc(z_stored[i % 2], 16)
                for i in range(2):
                    sp.wait_ge(z_stored[i], 16 * (NZ // 2))

            @block.scalar
            def _(act):
                def high_part(u):
                    act.wait_ge(w_in[u % 2], 16 * (u // 2 + 1))
                    if u >= 2:
                        act.wait_ge(group_done, first[u - 1])
                    act.activation(w_hi[:, u % 2], w[:, u % 2], ACT.Copy).then_inc(w_hi_ready, 1)

                high_part(0)
                act.wait_ge(padded, 1)
                for u in range(UNITS):
                    if u + 1 < UNITS:
                        high_part(u + 1)
                    for i in range(first[u], first[u + 1]):
                        _, c, h = groups[i]
                        act.wait_ge(group_done, i + 1)
                        src = pz[:, i % BANKS, :]
                        if u < QKV_UNITS:
                            act.activation(qkv[:, c, UW * u:UW * u + UW], src[:, 0:UW], ACT.Copy).then_inc(evacuated, 1)
                        elif u < QKV_UNITS + HY_UNITS:
                            n = 2 * (u - QKV_UNITS) + c
                            if n >= 2:
                                act.wait_ge(z_ready, n - 1)
                            act.activation(ub[:, n % 2, 1 + 512 * h:513 + 512 * h], src, ACT.Copy).then_inc(evacuated, 1)
                        else:
                            n = 2 * (u - QKV_UNITS - HY_UNITS) + c
                            if n >= 2 and h == 0:
                                act.wait_ge(g_stored[n % 2], 16 * (n // 2))
                            act.activation(gs[:, n % 2, 512 * h:512 * h + 512], src, ACT.Sigmoid).then_inc(evacuated, 1)
                            if h == 1:
                                act.wait_ge(evacuated, i + 1)
                                act.dma_start(g["gate_dram"][P * n:P * n + P, :], gs[:, n % 2, :])\
                                   .then_inc(g_stored[n % 2], 16)
                for i in range(2):
                    act.wait_ge(g_stored[i], 16 * (NG // 2))

            @block.vector
            def _(dve):
                def low_part(u):
                    dve.wait_ge(w_hi_ready, u + 1)
                    dve.tensor_tensor(w_lo[:, u % 2], w[:, u % 2], w_hi[:, u % 2].bitcast(F32), ALU.subtract)\
                       .then_inc(w_lo_ready, 1)

                dve.memset(ub[:], 0.0).then_inc(padded, 1)
                low_part(0)
                for u in range(UNITS):
                    if u + 1 < UNITS:
                        low_part(u + 1)
                    if not QKV_UNITS <= u < QKV_UNITS + HY_UNITS:
                        continue
                    for c in range(2):
                        n = 2 * (u - QKV_UNITS) + c
                        b = ub[:, n % 2, :]
                        dve.wait_ge(evacuated, first[u] + 2 * c + 2)
                        if n >= 2:
                            dve.wait_ge(z_stored[n % 2], 16 * (n // 2))
                        if n:
                            dve.wait_ge(z_ready, n)
                        dve.tensor_scalar(t1[:], b[:, 1:L + 1], cols2[:, 12 + n:13 + n], cols2[:, 36 + n:37 + n],
                                          ALU.mult, ALU.add).then_inc(conv_step, 1)
                        dve.wait_ge(conv_step, 2 * n + 1)
                        dve.scalar_tensor_tensor(out=t1[:], in0=b[:, 0:L], scalar=cols2[:, n:n + 1], in1=t1[:],
                                                 op0=ALU.mult, op1=ALU.add).then_inc(conv_step, 1)
                        dve.wait_ge(conv_step, 2 * n + 2)
                        dve.scalar_tensor_tensor(out=zs[:, n % 2, :], in0=b[:, 2:L + 2], scalar=cols2[:, 24 + n:25 + n],
                                                 in1=t1[:], op0=ALU.mult, op1=ALU.add).then_inc(z_ready, 1)

            @block.tensor
            def _(pe):
                for u in range(UNITS):
                    pe.wait_ge(w_lo_ready, u + 1)
                    b = u % 2
                    for i in range(first[u], first[u + 1]):
                        _, c, h = groups[i]
                        if i >= BANKS:
                            pe.wait_ge(evacuated, i - BANKS + 1)
                        for k in range(KD):
                            if h is None:
                                mm = three(pe, pz[:, i % BANKS, 0:UW],
                                           h_hi[:, k, P * c:P * c + P], h_lo[:, k, P * c:P * c + P],
                                           w_hi[:, b, k, :], w_lo[:, b, k, :], k == 0, k == KD - 1)
                            else:
                                mm = three(pe, pz[:, i % BANKS, :],
                                           w_hi[:, b, k, P * c:P * c + P], w_lo[:, b, k, P * c:P * c + P],
                                           h_hi[:, k, 512 * h:512 * h + 512], h_lo[:, k, 512 * h:512 * h + 512],
                                           k == 0, k == KD - 1)
                        mm.then_inc(group_done, 1)


def inverse_root(dve, act_root, step, at, v, root, r, tmp):
    dve.wait_ge(act_root, 1)
    dve.reciprocal(r, root).then_inc(step, 1)
    dve.wait_ge(step, at + 1)
    dve.tensor_tensor(tmp, r, r, ALU.mult).then_inc(step, 1)
    dve.wait_ge(step, at + 2)
    dve.tensor_tensor(tmp, tmp, v, ALU.mult).then_inc(step, 1)
    dve.wait_ge(step, at + 3)
    dve.tensor_scalar(tmp, tmp, -0.5, 1.5, ALU.mult, ALU.add).then_inc(step, 1)
    dve.wait_ge(step, at + 4)
    dve.tensor_tensor(r, r, tmp, ALU.mult).then_inc(step, 1)
    dve.wait_ge(step, at + 5)


def attention(g):
    nc, sem, A = g["nc"], g["sem"], g["A"]
    qkv, ident = g["qkv"], g["ident"]
    NG = NH + NKV
    W = NG * HD
    GRP = NH // NKV
    U = NT * NH
    SC = HD ** -0.5
    with ExitStack() as s:
        sb, ps = g["scope"](s)
        wrow = sb("wrow", [P, NG, HD])
        nsink = sb("nsink", [P, NH])
        cos, sin = sb("cos", [P, NT, ROT]), sb("sin", [P, NT, ROT])
        sq = sb("sq", [P, W])
        ssq, root, rstd, tmp = (sb(n, [P, NTA, NG]) for n in ("ssq", "q_root", "rstd", "q_tmp"))
        xn = sb("xn", [P, NG, HD])
        r1, r2 = sb("r1", [P, NG, ROT]), sb("r2", [P, NG, ROT])
        r3, r4 = sb("r3", [P, NG, ROT]), sb("r4", [P, NG, ROT])
        qn = sb("qn", [P, 2, NG, HD])
        qT = sb("qT", [P, GRP, L])
        kT = sb("kT", [P, LA])
        negI, m_prev, m_next = (sb(n, [P, P], BF16) for n in ("negI", "m_prev", "m_next"))
        mx, nm, rs = (sb(n, [P, U]) for n in ("mx", "nm", "rs"))
        es0, es, r = sb("es0", [P, NH]), sb("es", [P, NH]), sb("r_sum", [P, NH])
        probs = sb("probs", [P, 3, 640])
        probsT = sb("probsT", [P, 2, 640])
        yb = sb("yb", [P, NH, HD])
        yt = sb("yt", [P, 2, NCH, P])
        p_s = ps("p_s", [P, 2, 1024])
        p_pt = ps("p_pt", [P, 1024])
        p_o = ps("p_o", [P, 512])
        p_y = ps("p_y", [P, 512])
        small_in, masks, mask_step = sem("small_in"), sem("masks"), sem("mask_step")
        w_ready, sq_ready, ssq_ready = sem("w_ready"), sem("sq_ready"), sem("ssq_ready")
        q_root, q_step, rope_step = sem("q_root_ready"), sem("q_step"), sem("rope_step")
        qn_ready, qk_t, qk_copied = sem("qn_ready"), sem("qk_t"), sem("qk_copied")
        s_done, max_ready, shift_ready, exp_ready = sem("s_done"), sem("max_ready"), sem("shift_ready"), sem("exp_ready")
        pt_done, pt_copied, pv_done = sem("pt_done"), sem("pt_copied"), sem("pv_done")
        es0_ready, es_ready, norm_step, yb_ready = sem("es0_ready"), sem("es_ready"), sem("o_step"), sem("yb_ready")
        y_t, y_copied = sem("y_t"), sem("y_copied")
        y_stored = [sem(f"y_stored{i}") for i in range(2)]

        def blocks(n):
            return list(range(max(0, n - 1), min(NT - 1, n + 1) + 1))

        def width(u):
            return LC + P * len(blocks(u // NH))

        with nc.Block() as block:
            @block.sync
            def _(sp):
                for i in range(NG):
                    w = A["q_norm"] if i < NH else A["k_norm"]
                    sp.dma_start(wrow[:, i, :], w[0, :].partition_broadcast(P)).then_inc(small_in, 16)
                sp.dma_start(nsink[:], A["attn_sink"][0, :].partition_broadcast(P)).then_inc(small_in, 16)
                sp.dma_start(cos[:], A["rope_cos"].rearrange("(t p) d -> p t d", p=P)).then_inc(small_in, 16)
                sp.dma_start(sin[:], A["rope_sin"].rearrange("(t p) d -> p t d", p=P)).then_inc(small_in, 16)
                for n in range(NT):
                    sp.wait_ge(y_copied, n + 1)
                    sp.dma_start(g["yb_dram"][:, P * n:P * n + P].rearrange("(c p) t -> p c t", p=P), yt[:, n % 2])\
                      .then_inc(y_stored[n % 2], 16)
                for i in range(2):
                    sp.wait_ge(y_stored[i], 16 * (NT // 2))

            @block.gpsimd
            def _(pool):
                pool.memset(negI[:], 0.0).then_inc(mask_step, 1)
                pool.memset(m_prev[:], 0.0).then_inc(mask_step, 1)
                pool.memset(m_next[:], 0.0).then_inc(mask_step, 1)
                pool.wait_ge(mask_step, 3)
                pool.affine_select(out=negI[:], in_=negI[:], compare_op=ALU.not_equal, fill=NEG, base=0,
                                   pattern=[[-1, P]], channel_multiplier=1).then_inc(masks, 1)
                pool.affine_select(out=m_prev[:], in_=m_prev[:], compare_op=ALU.is_ge, fill=1.0, base=0,
                                   pattern=[[1, P]], channel_multiplier=-1).then_inc(masks, 1)
                pool.affine_select(out=m_next[:], in_=m_next[:], compare_op=ALU.is_ge, fill=1.0, base=0,
                                   pattern=[[-1, P]], channel_multiplier=1).then_inc(masks, 1)

            @block.scalar
            def _(act):
                act.wait_ge(q_step, 1)
                act.activation(root[:], ssq[:], ACT.Sqrt).then_inc(q_root, 1)
                for i in range(NTA):
                    act.wait_ge(qk_t, i + 1)
                    if i < NT:
                        act.activation(qT[:, :, P * i:P * i + P], p_s[:, i % 2, 0:512].rearrange("p (g t) -> p g t", g=GRP),
                                       ACT.Copy)
                    at = LC + P * i if i < NT else P * (i - NT)
                    act.activation(kT[:, at:at + P], p_s[:, i % 2, 512:640], ACT.Copy).then_inc(qk_copied, 1)

                def copy_y(n):
                    act.wait_ge(y_t, n + 1)
                    if n >= 2:
                        act.wait_ge(y_stored[n % 2], 16 * (n // 2))
                    act.activation(yt[:, n % 2].rearrange("p c t -> p (c t)"), p_y[:], ACT.Copy).then_inc(y_copied, 1)

                for u in range(U):
                    n, w = u // NH, width(u)
                    act.wait_ge(shift_ready, u + 1)
                    if u >= 3:
                        act.wait_ge(pt_done, u - 2)
                    act.activation(probs[:, u % 3, :w], p_s[:, u % 2, :w], ACT.Exp, bias=nm[:, u:u + 1], scale=SC,
                                   accum_out=rs[:, u:u + 1]).then_inc(exp_ready, 1)
                    if u % NH == NH - 1:
                        act.wait_ge(es0_ready, n + 1)
                        act.activation(es[:], es0[:], ACT.Exp).then_inc(es_ready, 1)
                    if u % NH == 3 and n >= 1:
                        copy_y(n - 1)
                copy_y(NT - 1)

            @block.vector
            def _(dve):
                dve.wait_ge(small_in, 16 * (NG + 3))
                dve.tensor_scalar(nsink[:], nsink[:], -1.0, None, ALU.mult).then_inc(w_ready, 1)
                dve.memset(ssq[:], 1.0).then_inc(ssq_ready, 1)
                dve.wait_ge(ssq_ready, 1)
                for i in range(NTA):
                    a = 0 if i < NT else NH
                    w = (NG - a) * HD
                    src = qkv[:, i, HD * a:HD * a + w]
                    if i:
                        dve.wait_ge(ssq_ready, i + 1)
                    dve.tensor_tensor(sq[:, 0:w], src, src, ALU.mult).then_inc(sq_ready, 1)
                    dve.wait_ge(sq_ready, i + 1)
                    dve.tensor_reduce(ssq[:, i, a:NG], sq[:, 0:w].rearrange("p (h d) -> p h d", d=HD), AX, ALU.add)\
                       .then_inc(ssq_ready, 1)
                dve.wait_ge(ssq_ready, NTA + 1)
                dve.tensor_scalar(ssq[:], ssq[:], 1.0 / HD, EPS, ALU.mult, ALU.add).then_inc(q_step, 1)
                inverse_root(dve, q_root, q_step, 1, ssq[:], root[:], rstd[:], tmp[:])
                dve.wait_ge(w_ready, 1)
                ropes = 0
                for i in range(NTA):
                    a = 0 if i < NT else NH
                    if i >= 2:
                        dve.wait_ge(qk_t, i - 1)
                    x = qkv[:, i, 0:W].rearrange("p (h d) -> p h d", d=HD)
                    r_ = rstd[:, i, :].unsqueeze(2).broadcast_to([P, NG, HD])
                    if i:
                        dve.wait_ge(qn_ready, i)
                    if i < NT:
                        def pairs(t, spec):
                            return t[:, 0:NH].rearrange(spec, s=NKV, g=GRP)
                        dve.tensor_tensor(pairs(xn, "p (g s) d -> p s g d"), pairs(x, "p (s g) d -> p s g d"),
                                          pairs(r_, "p (s g) d -> p s g d"), ALU.mult)
                    dve.tensor_tensor(xn[:, NH:], x[:, NH:], r_[:, NH:], ALU.mult).then_inc(rope_step, 1)
                    ropes += 1
                    dve.wait_ge(rope_step, ropes)
                    if i >= NT:
                        dve.tensor_tensor(qn[:, i % 2, a:], xn[:, a:], wrow[:, a:], ALU.mult).then_inc(qn_ready, 1)
                        continue
                    dve.tensor_tensor(xn[:], xn[:], wrow[:], ALU.mult).then_inc(rope_step, 1)
                    ropes += 1
                    dve.wait_ge(rope_step, ropes)
                    c = cos[:, i, :].unsqueeze(1).broadcast_to([P, NG, ROT])
                    s_ = sin[:, i, :].unsqueeze(1).broadcast_to([P, NG, ROT])
                    even, odd = xn[:, :, 0:HD:2], xn[:, :, 1:HD:2]
                    dve.tensor_tensor(r1[:], even, c, ALU.mult).then_inc(rope_step, 1)
                    dve.tensor_tensor(r2[:], odd, s_, ALU.mult).then_inc(rope_step, 1)
                    dve.tensor_tensor(r3[:], even, s_, ALU.mult).then_inc(rope_step, 1)
                    dve.tensor_tensor(r4[:], odd, c, ALU.mult).then_inc(rope_step, 1)
                    ropes += 4
                    dve.wait_ge(rope_step, ropes)
                    dve.tensor_tensor(qn[:, i % 2, :, 0:HD:2], r1[:], r2[:], ALU.subtract)
                    dve.tensor_tensor(qn[:, i % 2, :, 1:HD:2], r3[:], r4[:], ALU.add).then_inc(qn_ready, 1)

                def copy_probs(u):
                    dve.wait_ge(pt_done, u + 1)
                    if u >= 2:
                        dve.wait_ge(pv_done, u - 1)
                    dve.tensor_copy(probsT[:, u % 2, :width(u)], p_pt[:, :width(u)]).then_inc(pt_copied, 1)

                def normalise(n):
                    dve.wait_ge(es_ready, n + 1)
                    dve.wait_ge(exp_ready, NH * (n + 1))
                    dve.tensor_tensor(r[:], rs[:, NH * n:NH * n + NH], es[:], ALU.add).then_inc(norm_step, 1)
                    dve.wait_ge(norm_step, 2 * n + 1)
                    dve.reciprocal(r[:], r[:]).then_inc(norm_step, 1)
                    dve.wait_ge(norm_step, 2 * n + 2)
                    dve.wait_ge(pv_done, NH * (n + 1))
                    if n:
                        dve.wait_ge(y_t, n)
                    dve.tensor_tensor(yb[:], p_o[:].rearrange("p (h d) -> p h d", d=HD),
                                      r[:].unsqueeze(2).broadcast_to([P, NH, HD]), ALU.mult).then_inc(yb_ready, 1)

                for u in range(U):
                    n = u // NH
                    dve.wait_ge(s_done, u + 1)
                    dve.reduce_max(mx[:, u:u + 1], p_s[:, u % 2, :width(u)], AX).then_inc(max_ready, 1)
                    dve.wait_ge(max_ready, u + 1)
                    dve.tensor_scalar(nm[:, u:u + 1], mx[:, u:u + 1], -SC, nsink[:, u % NH:u % NH + 1],
                                      ALU.mult, ALU.min).then_inc(shift_ready, 1)
                    if u % NH == NH - 1:
                        dve.wait_ge(shift_ready, u + 1)
                        if n:
                            dve.wait_ge(es_ready, n)
                        dve.tensor_tensor(es0[:], nm[:, NH * n:NH * n + NH], nsink[:], ALU.subtract)\
                           .then_inc(es0_ready, 1)
                    if u:
                        copy_probs(u - 1)
                    if u % NH == 0 and n:
                        normalise(n - 1)
                copy_probs(U - 1)
                normalise(NT - 1)

            @block.tensor
            def _(pe):
                for i in range(NTA):
                    pe.wait_ge(qn_ready, i + 1)
                    if i >= 2:
                        pe.wait_ge(qk_copied, i - 1)
                    if i < NT:
                        q = qn[:, i % 2].rearrange("p h d -> p (h d)")
                        for j in range(GRP):
                            pe.transpose(p_s[:, i % 2, P * j:P * j + P], q[:, P * j:P * j + P], ident[:])
                    pe.transpose(p_s[:, i % 2, 512:640], qn[:, i % 2, NH:NG, :].rearrange("p s d -> p (s d)"), ident[:])\
                      .then_inc(qk_t, 1)
                pe.wait_ge(qk_copied, NTA)
                pe.wait_ge(masks, 3)

                def scores(u):
                    n, h = divmod(u, NH)
                    kv, j = divmod(h, GRP)
                    at = slice(HD * kv, HD * kv + HD)
                    bank, b = p_s[:, u % 2], blocks(n)
                    q = qT[at, j, P * n:P * n + P]
                    if u >= 2:
                        pe.wait_ge(exp_ready, u - 1)
                    pe.matmul(bank[:, 0:LC], q, kT[at, 0:LC], start=True, stop=True)
                    for i, w in enumerate(b):
                        out = bank[:, LC + P * i:LC + P * i + P]
                        mask = {-1: m_prev, 0: None, 1: m_next}[w - n]
                        mm = pe.matmul(out, q, kT[at, LC + P * w:LC + P * w + P], start=True, stop=mask is None)
                        if mask is not None:
                            mm = pe.matmul(out, negI[:], mask[:], start=False, stop=True)
                    mm.then_inc(s_done, 1)

                def transpose_probs(u):
                    pe.wait_ge(exp_ready, u + 1)
                    if u:
                        pe.wait_ge(pt_copied, u)
                    for c in range(width(u) // P):
                        mm = pe.transpose(p_pt[:, P * c:P * c + P], probs[:, u % 3, P * c:P * c + P], ident[:])
                    mm.then_inc(pt_done, 1)

                def values(u):
                    n, h = divmod(u, NH)
                    kv = h // GRP
                    pe.wait_ge(pt_copied, u + 1)
                    if h == 0 and n:
                        pe.wait_ge(yb_ready, n)
                    tiles = [NT, NT + 1] + blocks(n)
                    for c, t in enumerate(tiles):
                        v = qkv[:, t, HD * (NG + kv):HD * (NG + kv) + HD]
                        mm = pe.matmul(p_o[:, HD * h:HD * h + HD], probsT[:, u % 2, P * c:P * c + P], v,
                                       start=c == 0, stop=c == len(tiles) - 1)
                    mm.then_inc(pv_done, 1)

                def transpose_y(n):
                    pe.wait_ge(yb_ready, n + 1)
                    if n:
                        pe.wait_ge(y_copied, n)
                    y = yb[:].rearrange("p h d -> p (h d)")
                    for c in range(NCH):
                        mm = pe.transpose(p_y[:, P * c:P * c + P], y[:, P * c:P * c + P], ident[:])
                    mm.then_inc(y_t, 1)

                scores(0)
                for u in range(U):
                    if u + 1 < U:
                        scores(u + 1)
                    transpose_probs(u)
                    if u:
                        values(u - 1)
                    if u % NH == 2 and u > NH:
                        transpose_y(u // NH - 1)
                values(U - 1)
                transpose_y(NT - 1)


def hyena(g):
    nc, sem, A = g["nc"], g["sem"], g["A"]
    ident, cols2, ya = g["ident"], g["cols2"], g["ya"]
    T = L // P
    HT = T // 2
    FC = L // 2 // P
    ORD = 2
    TWO_PI = 2.0 * np.pi
    C1 = 6.28125
    C2 = TWO_PI - C1
    MAGIC = 1.5 * 2.0 ** 23
    with ExitStack() as outer:
        sbo, _ = g["scope"](outer)
        hid = sbo("hid", [FH, L])
        fpm = sbo("fpm", [FH, ORD, 2, HY])
        with ExitStack() as s:
            sb, ps = g["scope"](s)
            feat = sb("feat", [EMB, L])
            w1, w2, w3 = sb("fw1", [EMB, FH]), sb("fw2", [FH, FH]), sb("fw3", [FH, FH])
            vec = sb("fvec", [FH, 4])
            fout = sb("fout", [FH, ORD, 2, HY])
            un, kn = sb("un", [FH, L]), sb("kn", [FH, L])
            p_f = ps("p_f", [FH, 2, 512])
            f_in, fz_ready, f_step, sin_ready, fpm_ready = sem("f_in"), sem("fz_ready"), sem("f_step"), sem("sin_ready"), sem("fpm_ready")
            with nc.Block() as block:
                @block.sync
                def _(sp):
                    sp.dma_start(feat[:], A["feat"]).then_inc(f_in, 16)
                    for t, n in ((w1, "filt_w1"), (w2, "filt_w2"), (w3, "filt_w3")):
                        sp.dma_start(t[:], A[n][0]).then_inc(f_in, 16)
                    for i, n in enumerate(("filt_b1", "filt_b2", "filt_b3", "filt_freq")):
                        sp.dma_start(vec[:, i:i + 1], A[n].rearrange("o h -> h o")).then_inc(f_in, 16)
                    sp.dma_start(fout[:].rearrange("h a b c -> h (a b c)"), A["filt_out"][0]).then_inc(f_in, 16)

                @block.tensor
                def _(pe):
                    pe.wait_ge(f_in, 16 * 9)
                    for layer, (w, src) in enumerate(((w1, feat), (w2, hid), (w3, hid))):
                        if layer:
                            pe.wait_ge(sin_ready, layer)
                        for h in range(2):
                            mm = pe.matmul(p_f[:, h, :], w[:], src[:, 512 * h:512 * h + 512], start=True, stop=True)
                        mm.then_inc(fz_ready, 1)

                @block.vector
                def _(dve):
                    dve.wait_ge(f_in, 16 * 9)
                    dve.tensor_tensor(fpm[:, :, 0, :], fout[:, :, 0, :], fout[:, :, 1, :], ALU.add).then_inc(fpm_ready, 1)
                    dve.tensor_tensor(fpm[:, :, 1, :], fout[:, :, 0, :], fout[:, :, 1, :], ALU.subtract).then_inc(fpm_ready, 1)
                    n = 0
                    for layer in range(3):
                        dve.wait_ge(fz_ready, layer + 1)
                        if layer:
                            dve.wait_ge(sin_ready, layer)
                        for op in (
                            lambda: dve.tensor_scalar(un[:], p_f[:].rearrange("h a n -> h (a n)"), vec[:, layer:layer + 1],
                                                      vec[:, 3:4], ALU.add, ALU.mult),
                            lambda: dve.tensor_scalar(kn[:], un[:], 1.0 / TWO_PI, MAGIC, ALU.mult, ALU.add),
                            lambda: dve.tensor_scalar(kn[:], kn[:], -MAGIC, None, ALU.add),
                            lambda: dve.scalar_tensor_tensor(out=un[:], in0=kn[:], scalar=-C1, in1=un[:],
                                                             op0=ALU.mult, op1=ALU.add),
                            lambda: dve.scalar_tensor_tensor(out=un[:], in0=kn[:], scalar=-C2, in1=un[:],
                                                             op0=ALU.mult, op1=ALU.add),
                            lambda: dve.tensor_scalar(un[:], un[:], 3.1415925, -3.1415925, ALU.min, ALU.max),
                        ):
                            op().then_inc(f_step, 1)
                            n += 1
                            dve.wait_ge(f_step, n)

                @block.scalar
                def _(act):
                    for layer in range(3):
                        act.wait_ge(f_step, 6 * (layer + 1))
                        act.activation(hid[:], un[:], ACT.Sin).then_inc(sin_ready, 1)

        with ExitStack() as s:
            sb, ps = g["scope"](s)
            four = sb("four", [P, 4, FC, 512])
            pm = sb("pm", [P, 2, T, HY])
            ut = sb("ut", [P, T, HY])
            spec = sb("spec", [P, 4, FC, HY])
            gate = sb("gate_in", [P, 2, L])
            decay = sb("decay_in", [P, 2, HY])
            cp = sb("cp", [P, 4, HY])
            KX = sb("kx", [P, 8, HY])
            Y = sb("yspec", [P, 4, HY])
            t_a, t_b = sb("t_a", [P, 2, HY]), sb("t_b", [P, 2, HY])
            pj = ps("p_j", [P, 4, 2, 512])
            v_in, four_in, four2_in = sem("v_in"), sem("four_in"), sem("four2_in")
            four_back_in = sem("four_back_in")
            decay_in = [sem(f"decay_in{i}") for i in range(2)]
            gate_in = [sem(f"gate_in{i}") for i in range(2)]
            job, a_done, v_done = sem("job"), sem("act_read"), sem("dve_read")
            step = sem("spectral_step")
            jobs = []
            for o in range(ORD):
                jobs += [("filter", o, c) for c in range(T)]
                jobs += [("turn", o, c) for c in range(HT)]
                jobs += [(k, o, c) for c in range(FC) for k in ("Kc", "Ks", "Xc", "Xs")]
                jobs += [("back", o, c) for c in range(NCH)]
            n_job = {j: i for i, j in enumerate(jobs)}
            acts = {j: i + 1 for i, j in enumerate([j for j in jobs if j[0] not in ("filter", "back")])}
            dves = {j: i + 1 for i, j in enumerate([j for j in jobs if j[0] != "turn"])}

            def spectral_steps(o):
                return (o + 1) * (3 + FC * (4 + 10)) + o * 2 * NCH

            def free(pe, i):
                if i >= 4:
                    j = jobs[i - 4]
                    pe.wait_ge(*((a_done, acts[j]) if j[0] == "turn" else (v_done, dves[j])))

            with nc.Block() as block:
                @block.sync
                def _(sp):
                    sp.dma_start(ya[:], g["z_dram"][0:HY, :].rearrange("(c p) t -> p c t", p=P)).then_inc(v_in, 16)

                    def load_decay(i):
                        c = i % T
                        if i >= 2:
                            sp.wait_ge(v_done, dves[("filter", (i - 2) // T, (i - 2) % T)])
                        sp.dma_start(decay[:, i % 2], A["decay"][P * c:P * c + P, :]).then_inc(decay_in[i % 2], 16)

                    def load_gate(i):
                        o, c = divmod(i, NCH)
                        if i >= 2:
                            sp.wait_ge(v_done, dves[("back", (i - 2) // NCH, (i - 2) % NCH)])
                        at = HY * (o + 1) + P * c
                        sp.dma_start(gate[:, i % 2], g["z_dram"][at:at + P, :]).then_inc(gate_in[i % 2], 16)

                    def load_fourier(rows, s_):
                        for to, m in rows:
                            sp.dma_start(four[:, to], A["fourier"][m].rearrange("(c p) n -> p c n", p=P)).then_inc(s_, 16)

                    load_decay(0)
                    load_decay(1)
                    load_fourier(((0, 0), (1, 1), (2, 2), (3, 3)), four_in)
                    load_gate(0)
                    load_gate(1)
                    for o in range(ORD):
                        for c in range(T):
                            if o * T + c >= 2:
                                load_decay(o * T + c)
                        sp.wait_ge(job, n_job[("Xs", o, FC - 1)] + 1)
                        load_fourier(((0, 4), (2, 5)), four_back_in)
                        for c in range(NCH):
                            if o * NCH + c >= 2:
                                load_gate(o * NCH + c)
                        if o + 1 < ORD:
                            sp.wait_ge(job, n_job[("back", o, NCH - 1)] + 1)
                            load_fourier(((0, 0), (2, 2)), four2_in)

                @block.scalar
                def _(act):
                    for i, j in enumerate(jobs):
                        kind, o, c = j
                        if kind in ("filter", "back"):
                            continue
                        act.wait_ge(job, i + 1)
                        b = pj[:, i % 4]
                        if kind == "turn":
                            act.activation(ut[:, c:T:HT, :], b, ACT.Copy).then_inc(a_done, 1)
                        else:
                            q = ("Kc", "Ks", "Xc", "Xs").index(kind)
                            if o or c:
                                before = (kind, o, c - 1) if c else (kind, o - 1, FC - 1)
                                act.wait_ge(v_done, dves[before])
                            act.activation(cp[:, q], b[:, 0, :], ACT.Copy).then_inc(a_done, 1)

                @block.vector
                def _(dve):
                    steps = 0

                    def done(*instructions):
                        nonlocal steps
                        for i in instructions:
                            i.then_inc(step, 1)
                        steps += len(instructions)
                        dve.wait_ge(step, steps)

                    def tt(out, a, b, op):
                        return dve.tensor_tensor(out, a, b, op)

                    for i, j in enumerate(jobs):
                        kind, o, c = j
                        b = pj[:, i % 4]
                        if kind == "filter":
                            n = o * T + c
                            dve.wait_ge(job, i + 1)
                            dve.wait_ge(decay_in[n % 2], 16 * (n // 2 + 1))
                            if c == 0:
                                done(tt(pm[:, 0, c], b[:, 0], decay[:, n % 2], ALU.mult),
                                     tt(pm[:, 1, c], b[:, 1], decay[:, n % 2], ALU.mult))
                                done(tt(t_a[0:1, 0], pm[0:1, 0, 0], pm[0:1, 1, 0], ALU.add))
                                dve.tensor_scalar(pm[0:1, 0, 0], t_a[0:1, 0], 0.5, None, ALU.mult).then_inc(v_done, 1)
                            else:
                                tt(pm[:, 0, c], b[:, 0], decay[:, n % 2], ALU.mult)
                                tt(pm[:, 1, c], b[:, 1], decay[:, n % 2], ALU.mult).then_inc(v_done, 1)
                        elif kind == "back":
                            n = o * NCH + c
                            dve.wait_ge(job, i + 1)
                            dve.wait_ge(gate_in[n % 2], 16 * (n // 2 + 1))
                            bias = cols2[:, 48 + 4 * o + c:49 + 4 * o + c]
                            y = [ya[:, c, q:L:2] for q in range(2)]
                            done(*[dve.scalar_tensor_tensor(out=y[q], in0=y[q], scalar=bias, in1=b[:, q],
                                                            op0=ALU.mult, op1=ALU.add) for q in range(2)])
                            tt(ya[:, c, :], ya[:, c, :], gate[:, n % 2, :], ALU.mult).then_inc(v_done, 1)
                        elif kind in ("Kc", "Ks", "Xc", "Xs"):
                            q = ("Kc", "Ks", "Xc", "Xs").index(kind)
                            dve.wait_ge(a_done, acts[j])
                            even, odd = cp[:, q], b[:, 1]
                            tt(KX[:, 2 * q], even, odd, ALU.add).then_inc(step, 1)
                            if kind[1] == "c":
                                tt(KX[:, 2 * q + 1], even, odd, ALU.subtract).then_inc(v_done, 1)
                            else:
                                tt(KX[:, 2 * q + 1], odd, even, ALU.subtract).then_inc(v_done, 1)
                            steps += 1
                            if kind == "Xs":
                                dve.wait_ge(step, steps)
                                dve.wait_ge(v_done, dves[j])
                                kr, ki, xr, xi = (KX[:, 2 * z:2 * z + 2] for z in range(4))
                                yr, yi = Y[:, 0:2], Y[:, 2:4]
                                done(tt(t_a[:], xr, kr, ALU.mult), tt(t_b[:], xi, ki, ALU.mult))
                                done(tt(yr, t_a[:], t_b[:], ALU.subtract))
                                done(tt(t_a[:], xr, ki, ALU.mult), tt(t_b[:], xi, kr, ALU.mult))
                                done(tt(yi, t_a[:], t_b[:], ALU.add))
                                done(tt(spec[:, 0, c], Y[:, 0], Y[:, 1], ALU.add),
                                     tt(spec[:, 1, c], Y[:, 2], Y[:, 3], ALU.subtract),
                                     tt(spec[:, 2, c], Y[:, 0], Y[:, 1], ALU.subtract),
                                     tt(spec[:, 3, c], Y[:, 2], Y[:, 3], ALU.add))

                @block.tensor
                def _(pe):
                    for i, j in enumerate(jobs):
                        kind, o, c = j
                        b = pj[:, i % 4]
                        free(pe, i)
                        if kind == "filter":
                            for m in range(2):
                                mm = pe.matmul(b[:, m], hid[:, P * c:P * c + P], fpm[:, o, m, :], start=True, stop=True)
                        elif kind == "turn":
                            if c == 0:
                                if o == 0:
                                    pe.wait_ge(v_in, 16)
                                else:
                                    pe.wait_ge(v_done, dves[("back", o - 1, NCH - 1)])
                            for m in range(2):
                                at = 2 * P * c + m
                                for h in range(NCH):
                                    mm = pe.transpose(b[:, m, P * h:P * h + P], ya[:, h, at:at + 2 * P - 1:2], ident[:])
                        elif kind == "back":
                            if c == 0:
                                pe.wait_ge(four_back_in, 32 * (o + 1))
                                pe.wait_ge(step, spectral_steps(o))
                            for m in range(2):
                                for z in range(2):
                                    for f in range(FC):
                                        mm = pe.matmul(b[:, m], spec[:, 2 * m + z, f, P * c:P * c + P],
                                                       four[:, 2 * z + m, f, :], start=z == 0 and f == 0,
                                                       stop=z == 1 and f == FC - 1)
                        else:
                            if c == 0 and kind == "Kc":
                                if o == 0:
                                    pe.wait_ge(four_in, 64)
                                else:
                                    pe.wait_ge(four2_in, 32 * o)
                                pe.wait_ge(v_done, dves[("filter", o, T - 1)])
                            if c == 0 and kind == "Xc":
                                pe.wait_ge(a_done, acts[("turn", o, HT - 1)])
                            z = int(kind[1] == "s")
                            for m in range(2):
                                src = pm[:, z] if kind[0] == "K" else ut
                                for t in range(HT):
                                    mm = pe.matmul(b[:, m], four[:, 2 * z + m, t, P * c:P * c + P],
                                                   src[:, HT * m + t, :], start=t == 0, stop=t == HT - 1)
                        mm.then_inc(job, 1)


def merge(g):
    nc, sem, A = g["nc"], g["sem"], g["A"]
    ya, ident, mod, A2 = g["ya"], g["ident"], g["mod"], g["A2"]
    with ExitStack() as s:
        sb, ps = g["scope"](s)
        wa, wb = sb("wa", [P, NCH, D]), sb("wb", [P, NCH, D])
        yb = sb("yb_in", [P, NCH, L])
        wo = sb("wo", [P, KD, D])
        gates = sb("gates_in", [P, 2, 2, 512])
        mT = sb("mT", [P, KD, L])
        ta, tb = sb("m_a", [P, 2, 512]), sb("m_b", [P, 2, 512])
        x = sb("x_res", [P, 2, D])
        xn = sb("x_new", [P, NT, D])
        ss, rt, rs, tmp = (sb(n, [P, NT]) for n in ("ss2", "rt2", "rs2", "tmp2"))
        router = sb("router_w", [P, KD, NE])
        h2 = sb("h2", [P, 2, KD, P])
        junk = h2[:, 0].rearrange("p k t -> p (k t)")
        lg, ex = sb("lg", [P, NT, NE]), sb("ex", [P, NT, NE])
        mxl, sm = sb("mxl", [P, NT]), sb("sml", [P, NT])
        pj = ps("p_m", [P, 4, 2, 512])
        a_in, b_in, o_in, r_in = sem("wa_in"), sem("wb_in"), sem("wo_in"), sem("router_in")
        gates_in = [sem(f"gates_in{i}") for i in range(2)]
        xr_in = [sem(f"xr_in{i}") for i in range(2)]
        job, read = sem("m_job"), sem("m_read")
        mul, mt_ready = sem("m_mul"), sem("mt_ready")
        xg_ready, xnew_ready, sq_ready = sem("xg_ready"), sem("xnew_ready"), sem("sq2_ready")
        v_step, rt_ready, xn_ready = sem("v2_step"), sem("rt2_ready"), sem("xn2_ready")
        h_ready = sem("h2_ready")
        sm_step, exp_done = sem("sm_step"), sem("ex_ready")
        aff_t, aff_ready = sem("aff_t"), sem("aff_ready")
        x_stored, xn_stored = sem("x_stored"), sem("xn_stored")
        jobs = [("m", j, h) for j in range(KD) for h in range(2)] + [("o", t, 0) for t in range(NT)] \
            + [("h", t, 0) for t in range(NT)]
        M, O = 2 * KD, 2 * KD + NT

        with nc.Block() as block:
            @block.sync
            def _(sp):
                sp.dma_start(yb[:], g["yb_dram"].rearrange("(c p) t -> p c t", p=P)).then_inc(b_in, 16)
                sp.dma_start(wa[:], A["w_branch_a"][0].rearrange("(c p) n -> p c n", p=P)).then_inc(a_in, 16)
                sp.dma_start(wb[:], A["w_branch_b"][0].rearrange("(c p) n -> p c n", p=P)).then_inc(b_in, 16)
                for i in range(M):
                    if i >= 2:
                        sp.wait_ge(mt_ready, i - 1)
                    j, h = divmod(i, 2)
                    sp.dma_start(gates[:, i % 2], g["gate_dram"][:, 512 * h:512 * h + 512]
                                 .rearrange("(v c p) t -> c p v t", v=2, p=P)[j]).then_inc(gates_in[i % 2], 16)
                    if i == 1:
                        sp.dma_start(wo[:], A["w_out"][0].rearrange("(c p) n -> p c n", p=P)).then_inc(o_in, 16)
                        sp.dma_start(router[:], A["router"][0].rearrange("(c p) n -> p c n", p=P)).then_inc(r_in, 16)
                for t in range(NT):
                    if t >= 2:
                        sp.wait_ge(xnew_ready, t - 1)
                    sp.dma_start(x[:, t % 2], A["x"][0, P * t:P * t + P, :]).then_inc(xr_in[t % 2], 16)
                for t in range(NT):
                    sp.wait_ge(xnew_ready, t + 1)
                    sp.dma_start(g["out"][0, P * t:P * t + P, :], xn[:, t, :]).then_inc(x_stored, 16)
                sp.wait_ge(x_stored, 16 * NT)
                for t in range(NT):
                    sp.wait_ge(xn_ready, t + 1)
                    sp.dma_start(g["xn2_dram"][P * t:P * t + P, :], xn[:, t, :]).then_inc(xn_stored, 16)
                sp.wait_ge(xn_stored, 16 * NT)

            @block.tensor
            def _(pe):
                pe.wait_ge(a_in, 16)
                pe.wait_ge(b_in, 32)

                def logits(t):
                    pe.wait_ge(h_ready, KD * (t + 1))
                    for k in range(KD):
                        mm = pe.matmul(pj[:, (O + NT) % 4, 0, NE * t:NE * t + NE], h2[:, t % 2, k, :], router[:, k, :],
                                       start=k == 0, stop=k == KD - 1)
                    mm.then_inc(job, 1)

                for i, (kind, j, h) in enumerate(jobs):
                    q = i % 4 if kind != "h" else (O + 1 + j % 3) % 4
                    b = pj[:, q]
                    if kind != "h" and i >= 4:
                        pe.wait_ge(read, i - 3)
                    if kind == "h":
                        pe.wait_ge(read, O if j < 3 else O + j - 2)
                    if kind == "m":
                        for br, (w, y) in enumerate(((wa, ya), (wb, yb))):
                            for c in range(NCH):
                                mm = pe.matmul(b[:, br], w[:, c, P * j:P * j + P], y[:, c, 512 * h:512 * h + 512],
                                               start=c == 0, stop=c == NCH - 1)
                    elif kind == "o":
                        if j == 0:
                            pe.wait_ge(o_in, 16)
                            pe.wait_ge(mt_ready, M)
                        for h_ in range(2):
                            for k in range(KD):
                                mm = pe.matmul(b[:, h_], mT[:, k, P * j:P * j + P], wo[:, k, 512 * h_:512 * h_ + 512],
                                               start=k == 0, stop=k == KD - 1)
                    else:
                        pe.wait_ge(xn_ready, j + 1)
                        for k in range(KD):
                            mm = pe.transpose(b[:, k // 4, P * (k % 4):P * (k % 4) + P], xn[:, j, P * k:P * k + P],
                                              ident[:])
                    mm.then_inc(job, 1)
                    if kind == "h":
                        if j == 0:
                            pe.wait_ge(r_in, 16)
                        logits(j)
                pe.wait_ge(sm_step, 6)
                for t in range(NT):
                    mm = pe.transpose(pj[0:NE, (O + 1) % 4, t // 4, P * (t % 4):P * (t % 4) + P], ex[:, t, :], ident[:])
                mm.then_inc(aff_t, 1)

            @block.scalar
            def _(act):
                for t in range(NT):
                    act.wait_ge(xnew_ready, t + 1)
                    if t:
                        act.wait_ge(sq_ready, t)
                    act.activation(junk, xn[:, t, :], ACT.Square, accum_out=ss[:, t:t + 1]).then_inc(sq_ready, 1)
                act.wait_ge(v_step, 1)
                act.activation(rt[:], ss[:], ACT.Sqrt).then_inc(rt_ready, 1)
                act.wait_ge(sm_step, 3)
                act.activation(ex[:], lg[:], ACT.Exp).then_inc(exp_done, 1)

            @block.vector
            def _(dve):
                for i in range(M):
                    j, h = divmod(i, 2)
                    b = pj[:, i % 4]
                    dve.wait_ge(job, i + 1)
                    dve.wait_ge(gates_in[i % 2], 16 * (i // 2 + 1))
                    part = slice(512 * h, 512 * h + 512)
                    if i >= 2:
                        dve.wait_ge(mt_ready, i - 1)
                    dve.tensor_tensor(ta[:, i % 2], gates[:, i % 2, 0], b[:, 0], ALU.mult).then_inc(mul, 1)
                    dve.tensor_tensor(tb[:, i % 2], gates[:, i % 2, 1], b[:, 1], ALU.mult).then_inc(read, 1)
                    dve.wait_ge(mul, i + 1)
                    dve.wait_ge(read, i + 1)
                    dve.tensor_tensor(mT[:, j, part], ta[:, i % 2], tb[:, i % 2], ALU.add).then_inc(mt_ready, 1)
                for t in range(NT):
                    i = M + t
                    dve.wait_ge(job, i + 1)
                    dve.tensor_tensor(xn[:, t, :], pj[:, i % 4].rearrange("p a n -> p (a n)"), g["g1row"][:], ALU.mult)\
                       .then_inc(read, 1)
                    dve.wait_ge(read, i + 1)
                    dve.wait_ge(xr_in[t % 2], 16 * (t // 2 + 1))
                    dve.tensor_tensor(xn[:, t, :], xn[:, t, :], x[:, t % 2], ALU.add).then_inc(xnew_ready, 1)
                dve.wait_ge(sq_ready, NT)
                dve.tensor_scalar(ss[:], ss[:], 1.0 / D, EPS, ALU.mult, ALU.add).then_inc(v_step, 1)
                inverse_root(dve, rt_ready, v_step, 1, ss[:], rt[:], rs[:], tmp[:])
                dve.wait_ge(x_stored, 16 * NT)
                for t in range(NT):
                    dve.tensor_scalar(xn[:, t, :], xn[:, t, :], rs[:, t:t + 1], None, ALU.mult).then_inc(xn_ready, 1)
                for t in range(NT):
                    b = pj[:, (O + 1 + t % 3) % 4]
                    dve.wait_ge(job, O + 2 * t + 1)
                    if t >= 2:
                        dve.wait_ge(job, O + 2 * (t - 1))
                    for k in range(KD):
                        ins = dve.tensor_scalar(h2[:, t % 2, k, :], b[:, k // 4, P * (k % 4):P * (k % 4) + P],
                                                A2[:, k:k + 1], mod[:, 24 + k, 0:1], ALU.mult, ALU.add)
                        ins.then_inc(h_ready, 1)
                        if k == KD - 1:
                            dve.wait_ge(h_ready, KD * (t + 1))
                            dve.tensor_copy(tmp[:, 0:1], rs[:, 0:1]).then_inc(read, 1)
                dve.wait_ge(job, O + 2 * NT)
                lp = pj[:, (O + NT) % 4, 0, 0:NT * NE].rearrange("p (t e) -> p t e", e=NE)
                dve.tensor_reduce(mxl[:], lp, AX, ALU.max).then_inc(sm_step, 1)
                dve.wait_ge(sm_step, 1)
                dve.tensor_copy(lg[:], lp).then_inc(sm_step, 1)
                dve.wait_ge(sm_step, 2)
                dve.tensor_tensor(lg[:], lg[:], mxl[:].unsqueeze(2).broadcast_to([P, NT, NE]), ALU.subtract)\
                   .then_inc(sm_step, 1)
                dve.wait_ge(exp_done, 1)
                dve.tensor_reduce(sm[:], ex[:], AX, ALU.add).then_inc(sm_step, 1)
                dve.wait_ge(sm_step, 4)
                dve.reciprocal(sm[:], sm[:]).then_inc(sm_step, 1)
                dve.wait_ge(sm_step, 5)
                dve.tensor_tensor(ex[:], ex[:], sm[:].unsqueeze(2).broadcast_to([P, NT, NE]), ALU.mult)\
                   .then_inc(sm_step, 1)
                dve.wait_ge(aff_t, 1)
                dve.tensor_copy(g["affT"][:], pj[0:NE, (O + 1) % 4].rearrange("p a n -> p (a n)")).then_inc(aff_ready, 1)


def choice(g):
    nc, sem = g["nc"], g["sem"]
    aff, ident = g["affT"], g["ident"]
    R = CAP // 8
    with ExitStack() as s:
        sb, ps = g["scope"](s)
        vals, idx = sb("vals", [NE, CAP]), sb("idx_rows", [NE, CAP], U32)
        idx_f = sb("idx_f", [NE, CAP])
        p_c = ps("p_c", [P, 2, 512])
        best, found, gone = sem("best"), sem("found"), sem("gone")
        as_float, turned, kept = sem("as_float"), sem("turned"), sem("kept")

        with nc.Block() as block:
            @block.vector
            def _(dve):
                for r in range(R):
                    at = slice(8 * r, 8 * r + 8)
                    if r:
                        dve.wait_ge(gone, r)
                    dve.max(vals[:, at], aff[:]).then_inc(best, 1)
                    dve.wait_ge(best, r + 1)
                    dve.max_index(idx[:, at], vals[:, at], aff[:]).then_inc(found, 1)
                    dve.wait_ge(found, r + 1)
                    dve.match_replace(aff[:], vals[:, at], aff[:], -1.0).then_inc(gone, 1)
                dve.tensor_copy(idx_f[:], idx[:]).then_inc(as_float, 1)
                dve.wait_ge(turned, 1)
                dve.tensor_copy(g["gate"][:], p_c[:, 0, 0:NE]).then_inc(kept, 1)
                dve.tensor_copy(g["idx"][:], p_c[:, 1, 0:NE]).then_inc(kept, 1)
                dve.wait_ge(kept, 2)

            @block.tensor
            def _(pe):
                pe.wait_ge(as_float, 1)
                pe.transpose(p_c[:, 0, 0:NE], vals[:], ident[0:NE, 0:NE])
                pe.transpose(p_c[:, 1, 0:NE], idx_f[:], ident[0:NE, 0:NE]).then_inc(turned, 1)


FQ = FF // 512
EU = 4 * FQ + 2 * FQ
RAW, PARTS = 6, 4
AHEAD = 3
TURNS = FQ + 2
TURN_AT = {5: 0, 9: 1, 13: 2, 16: (3, 4), 17: 5}


def experts(g):
    nc, sem, A = g["nc"], g["sem"], g["A"]
    ident, A2, mod, g2row = g["ident"], g["A2"], g["mod"], g["g2row"]
    idx, gate = g["idx"], g["gate"]
    with ExitStack() as s:
        sb, ps = g["scope"](s)
        ring = sb("ring", [P, RAW, 2048])
        r_hi, r_lo = sb("r_hi", [P, PARTS, 2048], F32R), sb("r_lo", [P, PARTS, 2048], F32R)
        xe = sb("xe", [P, D])
        xf = sb("xf", [P, 2, 4, P])
        x_hi, x_lo = sb("x_hi", [P, KD, P], F32R), sb("x_lo", [P, KD, P], F32R)
        sg, au = sb("sg", [P, 512]), sb("au", [P, 512])
        a_hi, a_lo = sb("a_hi", [P, FF // P, P], F32R), sb("a_lo", [P, FF // P, P], F32R)
        ys, yo = sb("ys", [P, D]), sb("yo", [P, 2, D])
        idx_e = sb("idx_e", [P, 1], U32)
        idx_s = sb("idx_s", [P, 2], U32)
        gate_e = sb("gate_e", [P, 1])
        p_a = ps("p_a", [P, 2, 512])
        p_b = ps("p_b", [P, 512])
        p_y = ps("p_y2", [P, D])
        p_t = ps("p_t2", [P, 2, 512])
        raw_in = [sem(f"raw_in{i}") for i in range(RAW)]
        hi_ready, lo_ready, unit_done = sem("hi_ready"), sem("lo_ready"), sem("unit_done")
        idx_ready, gathered, gate_ready = sem("idx_ready"), sem("gathered"), sem("gate_ready")
        turn, turn_f, turn_hi, turn_lo = sem("turn"), sem("turn_f"), sem("turn_hi"), sem("turn_lo")
        sg_ready, au_step, au_ready = sem("sg_ready"), sem("au_step"), sem("au_ready")
        ys_ready, yo_ready, added = sem("ys_ready"), sem("yo_ready"), sem("added")
        pool_passed = sem("pool_passed")

        def source(e, i):
            if i < 4 * FQ:
                c, q = divmod(i, 4)
                w = A["w_gate"] if q < 2 else A["w_up"]
                return w[0][bass.ds(e, 1), 512 * (q % 2):512 * (q % 2) + 512, 512 * c:512 * c + 512]\
                    .rearrange("e (k p) n -> p (e k) n", p=P)
            j = i - 4 * FQ
            return A["w_down"][0][bass.ds(e, 1), 256 * j:256 * j + 256, :].rearrange("e (k p) n -> p (e k) n", p=P)

        def each_expert(eng, body, first=True, last=True):
            body(0, True, False)
            with eng.Fori(1, NE - 1) as e:
                body(e, False, False)
            body(NE - 1, False, True)

        with nc.Block() as block:
            @block.sync
            def _(sp):
                def body(e, first, last):
                    for i in range(EU):
                        if not (first and i < RAW):
                            sp.wait_ge(lo_ready, EU * e + i - RAW + 1)
                        n = 4 if i < 4 * FQ else 2
                        sp.dma_start(ring[:, i % RAW].rearrange("p (k n) -> p k n", k=n), source(e, i))\
                          .then_inc(raw_in[i % RAW], 16)
                each_expert(sp, body)

            @block.gpsimd
            def _(pool):
                def gather(e):
                    pool.wait_ge(idx_ready, e + 1)
                    pool.sem_inc(pool_passed, 1)
                    pool.indirect_dma_start(out=xe[:], out_offset=None, in_=g["xn2_dram"][:, :],
                                            in_offset=bass.IndirectOffsetOnAxis(ap=idx_e[:, 0:1], axis=0))\
                        .then_inc(gathered, 16)

                def body(e, first, last):
                    if not last:
                        gather(e + 1)
                    pool.wait_ge(yo_ready, e + 1)
                    if not first:
                        pool.wait_ge(added, 16 * e)
                    pool.sem_inc(pool_passed, 1)
                    pool.indirect_dma_start(out=g["out"][0], in_=yo[:, 0], in_offset=None,
                                            out_offset=bass.IndirectOffsetOnAxis(ap=idx_s[:, 0:1], axis=0),
                                            compute_op=ALU.add).then_inc(added, 16)
                gather(0)
                each_expert(pool, body)
                pool.wait_ge(added, 16 * NE)

            @block.scalar
            def _(act):
                def high_part(e, i, before=None):
                    act.wait_ge(raw_in[i % RAW], 16 * (EU // RAW * e + i // RAW + 1))
                    if not before:
                        act.wait_ge(unit_done, EU * e + i - PARTS + 1)
                    act.activation(r_hi[:, i % PARTS], ring[:, i % RAW], ACT.Copy).then_inc(hi_ready, 1)

                def turn_x(e, q):
                    act.wait_ge(turn_f, 2 * e + q + 1)
                    act.activation(x_hi[:, 4 * q:4 * q + 4, :], xf[:, q], ACT.Copy).then_inc(turn_hi, 1)

                def body(e, first, last):
                    for i in range(EU):
                        if not (last and i + AHEAD >= EU):
                            high_part(e, i + AHEAD, first and i + AHEAD < PARTS)
                        if i < 4 * FQ and i % 4 == 3:
                            c = i // 4
                            act.wait_ge(unit_done, EU * e + i - 1)
                            if not (first and c == 0):
                                act.wait_ge(au_step, 2 * (FQ * e + c))
                            act.activation(sg[:], p_a[:, c % 2], ACT.Sigmoid).then_inc(sg_ready, 1)
                        for q in np.atleast_1d(TURN_AT.get(i, [])).astype(int).tolist():
                            if q in (3, 4):
                                if not last:
                                    turn_x(e + 1, q - 3)
                                continue
                            c = min(q, 3)
                            act.wait_ge(turn, turns(e, q, last))
                            act.activation(a_hi[:, 4 * c:4 * c + 4, :].rearrange("p k m -> p (k m)"), p_t[:, q % 2],
                                           ACT.Copy).then_inc(turn_hi, 1)
                        if i == EU - 1:
                            act.wait_ge(unit_done, EU * e + EU)
                            act.wait_ge(gate_ready, e + 1)
                            if not first:
                                act.wait_ge(yo_ready, e)
                            act.activation(ys[:], p_y[:], ACT.Copy, scale=gate_e[:, 0:1]).then_inc(ys_ready, 1)
                for i in range(AHEAD):
                    high_part(0, i, True)
                for q in range(2):
                    turn_x(0, q)
                each_expert(act, body)

            @block.vector
            def _(dve):
                def low_part(e, i):
                    dve.wait_ge(hi_ready, EU * e + i + 1)
                    dve.tensor_tensor(r_lo[:, i % PARTS], ring[:, i % RAW], r_hi[:, i % PARTS].bitcast(F32),
                                      ALU.subtract).then_inc(lo_ready, 1)

                def take_index(e, first):
                    if not first:
                        dve.wait_ge(gathered, 16 * e)
                    dve.tensor_copy(idx_e[:, 0:1], idx[:, bass.ds(e, 1)]).then_inc(idx_ready, 1)

                def turn_x(e, q, n, bank):
                    dve.wait_ge(turn, n + 1)
                    for k in range(4):
                        ins = dve.tensor_scalar(xf[:, q, k, :], p_t[:, bank, P * k:P * k + P],
                                                A2[:, 4 * q + k:4 * q + k + 1], mod[:, 24 + 4 * q + k, 0:1],
                                                ALU.mult, ALU.add)
                    ins.then_inc(turn_f, 1)
                    dve.wait_ge(turn_hi, n + 1)
                    dve.tensor_tensor(x_lo[:, 4 * q:4 * q + 4, :], xf[:, q], x_hi[:, 4 * q:4 * q + 4, :].bitcast(F32),
                                      ALU.subtract).then_inc(turn_lo, 1)

                def body(e, first, last):
                    for i in range(EU):
                        if not (last and i + AHEAD >= EU):
                            low_part(e, i + AHEAD)
                        if i == 0 and not last:
                            take_index(e + 1, False)
                        if i == 1:
                            if not first:
                                dve.wait_ge(ys_ready, e)
                                dve.wait_ge(added, 16 * e)
                            dve.tensor_copy(gate_e[:, 0:1], gate[:, bass.ds(e, 1)]).then_inc(gate_ready, 1)
                            dve.tensor_copy(idx_s[:, 0:1], idx[:, bass.ds(e, 1)])
                        if i < 4 * FQ and i % 4 == 3:
                            c = i // 4
                            dve.wait_ge(sg_ready, FQ * e + c + 1)
                            if not (first and c == 0):
                                dve.wait_ge(turn, turns(e, c - 1, last) if c else turns_before(e))
                            dve.tensor_tensor(au[:], sg[:], p_a[:, c % 2], ALU.mult).then_inc(au_step, 1)
                            dve.wait_ge(au_step, 2 * (FQ * e + c) + 1)
                            dve.wait_ge(unit_done, EU * e + i + 1)
                            dve.tensor_tensor(au[:], au[:], p_b[:], ALU.mult).then_inc(au_step, 1)
                        for q in np.atleast_1d(TURN_AT.get(i, [])).astype(int).tolist():
                            if q in (3, 4):
                                if not last:
                                    turn_x(e + 1, q - 3, turns(e, q, last) - 1, q % 2)
                                continue
                            c = min(q, 3)
                            n = turns(e, q, last)
                            dve.wait_ge(turn_hi, n)
                            dve.tensor_tensor(a_lo[:, 4 * c:4 * c + 4, :].rearrange("p k m -> p (k m)"), p_t[:, q % 2],
                                              a_hi[:, 4 * c:4 * c + 4, :].rearrange("p k m -> p (k m)").bitcast(F32),
                                              ALU.subtract).then_inc(turn_lo, 1)
                        if i == EU - 1:
                            dve.wait_ge(ys_ready, e + 1)
                            dve.tensor_tensor(yo[:, 0], ys[:], g2row[:], ALU.mult).then_inc(yo_ready, 1)
                take_index(0, True)
                for i in range(AHEAD):
                    low_part(0, i)
                for q in range(2):
                    turn_x(0, q, q, q)
                each_expert(dve, body)

            @block.tensor
            def _(pe):
                def turn_x(e, q, n, bank):
                    if q == 0:
                        pe.wait_ge(gathered, 16 * (e + 1))
                    if not (isinstance(n, int) and n < 2):
                        pe.wait_ge(turn_lo, n - 1)
                    for k in range(4):
                        mm = pe.transpose(p_t[:, bank, P * k:P * k + P], xe[:, P * (4 * q + k):P * (4 * q + k) + P],
                                          ident[:])
                    mm.then_inc(turn, 1)

                def turn_a(e, q, n):
                    c = min(q, 3)
                    pe.wait_ge(au_step, 2 * (FQ * e + c + 1))
                    pe.wait_ge(turn_lo, n - 1)
                    for k in range(4):
                        mm = pe.transpose(p_t[:, q % 2, P * k:P * k + P], au[:, P * k:P * k + P], ident[:])
                    mm.then_inc(turn, 1)

                def body(e, first, last):
                    for i in range(EU):
                        pe.wait_ge(lo_ready, EU * e + i + 1)
                        hi, lo = r_hi[:, i % PARTS], r_lo[:, i % PARTS]
                        if i < 4 * FQ:
                            c, q = divmod(i, 4)
                            out = p_a[:, c % 2] if q < 2 else p_b[:]
                            if i == 0:
                                pe.wait_ge(turn_lo, turns_before(e))
                            if q == 0 and not (first and c < 2):
                                pe.wait_ge(au_step, 2 * (FQ * e + c - 1))
                            if q == 2 and not (first and c == 0):
                                pe.wait_ge(au_step, 2 * (FQ * e + c))
                            for k in range(4):
                                kk = 4 * (q % 2) + k
                                mm = three(pe, out, x_hi[:, kk, :], x_lo[:, kk, :], hi[:, 512 * k:512 * k + 512],
                                           lo[:, 512 * k:512 * k + 512], kk == 0, kk == KD - 1)
                        else:
                            j = i - 4 * FQ
                            if j == 0 and not first:
                                pe.wait_ge(ys_ready, e)
                            if j % 2 == 0:
                                c = j // 2
                                pe.wait_ge(turn_lo, turns(e, c if c < 3 else 5, last))
                            for k in range(2):
                                kk = 2 * j + k
                                for h in range(2):
                                    at = slice(D * k + 512 * h, D * k + 512 * h + 512)
                                    mm = three(pe, p_y[:, 512 * h:512 * h + 512], a_hi[:, kk, :], a_lo[:, kk, :],
                                               hi[:, at], lo[:, at], kk == 0, kk == FF // P - 1)
                        mm.then_inc(unit_done, 1)
                        for q in np.atleast_1d(TURN_AT.get(i, [])).astype(int).tolist():
                            n = turns(e, q, last) - 1
                            if q in (3, 4):
                                if not last:
                                    turn_x(e + 1, q - 3, n, q % 2)
                            else:
                                turn_a(e, q, n)
                for q in range(2):
                    turn_x(0, q, q, q)
                each_expert(pe, body)


def turns_before(e):
    return TURNS * e + 2


def turns(e, q, last):
    return TURNS * e + q + 3 - (2 if last and q == 5 else 0)


INPUTS = ["x", "c", "ctx", "c_ctx", "ada_w", "ada_b", "norm1", "norm2", "w_in", "conv_w", "conv_b", "filt_w1",
          "filt_b1", "filt_w2", "filt_b2", "filt_w3", "filt_b3", "filt_freq", "filt_out", "hyena_bias", "q_norm",
          "k_norm", "attn_sink", "w_branch_a", "w_branch_b", "w_out", "router", "w_gate", "w_up", "w_down"]


def kernel(**inputs):
    from concourse import bacc
    from concourse.bass_utils import run_bass_kernel_spmd

    nc = bacc.Bacc("TRN2", target_bir_lowering=False, num_devices=1)
    arrays = {f"in_{n}": np.ascontiguousarray(inputs[n]) for n in INPUTS}
    arrays.update({f"in_{n}": a for n, a in shape_constants().items()})
    A = {n[3:]: nc.dram_tensor(n, a.shape, mybir.dt.from_np(a.dtype), kind="ExternalInput").ap()
         for n, a in arrays.items()}
    out = nc.dram_tensor("out_x", (1, L, D), F32, kind="ExternalOutput").ap()
    build(nc, A, out)
    r = run_bass_kernel_spmd(nc, [arrays], core_ids=[0])
    return r.results[0]["out_x"]
```

```python
from contextlib import ExitStack

import numpy as np

import concourse.bass as bass
from concourse import mybir

P = 128
D = 1024
L = 1024
LC = 256
KD = D // P
NT = L // P
NTC = LC // P
NTA = NT + NTC
LA = L + LC
HY = 512
NCH = HY // P
NH = 8
NKV = 2
HD = 64
OFF_Q = 3 * HY
OFF_G = OFF_Q + NH * HD + 2 * NKV * HD
QKV = OFF_G - OFF_Q
NE = 16
CAP = 2 * L // NE
FF = 2048
BANDS = 16
EMB = 1 + 2 * BANDS
FH = 64
EPS = 1e-6
NEG = -1e30
GRID_W = 64
NG = NH + NKV
GRP = NH // NKV
ROT = HD // 2

F32 = mybir.dt.float32
F32R = mybir.dt.float32r
BF16 = mybir.dt.bfloat16
I32 = mybir.dt.int32
U32 = mybir.dt.uint32
ALU = mybir.AluOpType
ACT = mybir.ActivationFunctionType
AX = mybir.AxisListType.X

UW = 256
QKV_UNITS = QKV // UW
HY_UNITS = OFF_Q // UW
G_UNITS = 2 * D // UW
UNITS = QKV_UNITS + HY_UNITS + G_UNITS


def unit_column(u):
    if u < QKV_UNITS:
        return OFF_Q + u * UW
    if u < QKV_UNITS + HY_UNITS:
        return (u - QKV_UNITS) * UW
    return OFF_G + (u - QKV_UNITS - HY_UNITS) * UW


def shape_constants():
    f = np.float32
    t = np.linspace(0.0, 1.0, L, dtype=f)[:, None]
    w = (f(2.0 * np.pi) * np.arange(L, dtype=f)[:, None] / f(L)).astype(f)
    fr = np.linspace(1e-4, BANDS - 1, BANDS, dtype=f)[None, :]
    feat = np.concatenate([t, np.cos((fr * w).astype(f)), -np.sin((fr * w).astype(f))], axis=-1).astype(f)
    lo, hi = np.log(1e-2) / 1.5, np.log(1e-2) / 0.3
    deltas = np.linspace(lo, hi, HY, dtype=f)
    decay = np.exp(-t * np.abs(deltas)).astype(f)
    order = np.concatenate([np.arange(0, L, 2), np.arange(1, L, 2)])
    row = np.repeat(np.arange(L // GRID_W, dtype=f), GRID_W)
    col = np.tile(np.arange(GRID_W, dtype=f), L // GRID_W)
    inv = (f(10000.0) ** (-np.arange(0, ROT, 2, dtype=f) / f(ROT))).astype(f)
    ang = np.concatenate([row[:, None] * inv, col[:, None] * inv], axis=-1).astype(f)
    fq = np.pi * (2 * np.arange(L // 2)[:, None] + 1) / (2 * L)
    j = np.arange(L // 2)[None, :]
    ce, se = np.cos(fq * 2 * j), np.sin(fq * 2 * j)
    co, so = np.cos(fq * (2 * j + 1)), np.sin(fq * (2 * j + 1))
    fourier = np.stack([ce.T, co, se.T, so, ce, se]).astype(f)
    return {
        "feat": np.ascontiguousarray(feat[order].T),
        "decay": np.ascontiguousarray(decay[order] / f(L)),
        "rope_cos": np.cos(ang).astype(f),
        "rope_sin": np.sin(ang).astype(f),
        "fourier": fourier,
    }


def build(nc, A, out):
    root = ExitStack()
    with root:
        def sem(name):
            return root.enter_context(nc.semaphore(name))

        def scope(stack):
            def sb(name, shape, dt=F32):
                return stack.enter_context(nc.sbuf_tensor(name, shape, dt))

            def ps(name, shape, dt=F32):
                return stack.enter_context(nc.psum_tensor(name, shape, dt))
            return sb, ps

        g = {"nc": nc, "sem": sem, "scope": scope, "A": A, "out": out}
        sb, _ = scope(root)
        g["z_dram"] = nc.dram_tensor("z_dram", [OFF_Q, L], F32).ap()
        g["gate_dram"] = nc.dram_tensor("gate_dram", [2 * D, L], F32).ap()
        g["yb_dram"] = nc.dram_tensor("yb_dram", [NH * HD, L], F32).ap()
        g["xn2_dram"] = nc.dram_tensor("xn2_dram", [L, D], F32).ap()
        g["ident"] = sb("ident", [P, P])
        g["ones"] = sb("ones", [P, P])
        g["cols1"] = sb("cols1", [P, 80])
        g["cols2"] = sb("cols2", [P, 56])
        g["A2"] = sb("A2", [P, KD])
        g["mod"] = sb("mod", [P, 48, 2])
        g["g1row"] = sb("g1row", [P, D])
        g["g2row"] = sb("g2row", [P, D])
        with ExitStack() as s12:
            sb12, _ = scope(s12)
            g["qkv"] = sb12("qkv", [P, NTA, QKV])
            g["sil"] = sb12("sil", [P, 2, KD])
            with ExitStack() as s:
                sbh, _ = scope(s)
                g["h_hi"] = sbh("h_hi", [P, KD, LA], F32R)
                g["h_lo"] = sbh("h_lo", [P, KD, LA], F32R)
                modulation(g)
                projection(g)
            attention(g)
        g["affT"] = sb("affT", [NE, L])
        with ExitStack() as s:
            sby, _ = scope(s)
            g["ya"] = sby("ya", [P, NCH, L])
            hyena(g)
            merge(g)
        with ExitStack() as s:
            sbe, _ = scope(s)
            g["idx"] = sbe("idx", [P, NE], U32)
            g["gate"] = sbe("gate", [P, NE])
            choice(g)
            experts(g)


def modulation(g):
    nc, sem, A = g["nc"], g["sem"], g["A"]
    ident, ones, cols1, cols2, mod = g["ident"], g["ones"], g["cols1"], g["cols2"], g["mod"]
    h_hi, h_lo, sil = g["h_hi"], g["h_lo"], g["sil"]
    GROUPS = [(h, k) for h in range(3) for k in range(KD)]
    SECTIONS = 2 * D // 512
    with ExitStack() as s:
        sb, ps = g["scope"](s)
        rows1, rows2 = sb("rows1", [80, P]), sb("rows2", [56, P])
        sig = sb("sig", [P, 2 * KD])
        ada = sb("ada", [P, 2, KD, 512])
        mod_rows = sb("mod_rows", [2, SECTIONS, 512])
        x = sb("x_in", [P, NTA, D])
        ss, rt, r0, tt = (sb(n, [P, NTA]) for n in ("ss", "rt", "r0", "tt"))
        scale = sb("mod_scale", [P, KD, 2])
        hf = sb("hf", [P, 3, 512])
        junk = hf[:].rearrange("p a n -> p (a n)")[:, 0:D]
        p_rows = ps("p_rows", [P, 512])
        p_mod = ps("p_mod", [P, 512])
        p_x = ps("p_x", [P, 3, 512])
        p_sec = ps("p_sec", [P, 2, 512])
        rows_in, rows2_in = sem("rows_in"), sem("rows2_in")
        ada_in = [sem(f"ada_in{i}") for i in range(2)]
        x_in = [sem(f"x_in{t}") for t in range(NTA)]
        consts = sem("consts")
        rows_t, cols_ready = sem("rows_t"), sem("cols_ready")
        sig_ready, sil_ready = sem("sig_ready"), sem("sil_ready")
        section_done, section_copied, mod_t = sem("section_done"), sem("section_copied"), sem("mod_t")
        mod_ready = sem("mod_ready")
        ss_ready, root_ready, norm_step, xn_ready = sem("ss_ready"), sem("root_ready"), sem("norm_step"), sem("xn_ready")
        x_t, h_f, hi_ready, lo_ready = sem("x_t"), sem("h_f"), sem("h_hi_ready"), sem("h_lo_ready")

        def tokens(h):
            return (512 * h, 512) if h < 2 else (L, LC)

        with nc.Block() as block:
            @block.sync
            def _(sp):
                at = 0
                for name, n in (("ada_b", 48), ("norm1", 8), ("norm2", 8), ("c", 8)):
                    sp.dma_start(rows1[at:at + n, :], A[name].rearrange("o (j p) -> (o j) p", p=P)).then_inc(rows_in, 16)
                    at += n
                sp.dma_start(rows1[at:at + 8, :], A["c_ctx"].rearrange("(j p) -> j p", p=P)).then_inc(rows_in, 16)
                sp.dma_start(rows2[0:36, :], A["conv_w"].rearrange("o r (j p) -> (o r j) p", p=P)).then_inc(rows2_in, 16)
                sp.dma_start(rows2[36:48, :], A["conv_b"].rearrange("o (j p) -> (o j) p", p=P)).then_inc(rows2_in, 16)
                sp.dma_start(rows2[48:56, :], A["hyena_bias"].rearrange("o r (j p) -> (o r j) p", p=P)).then_inc(rows2_in, 16)
                for s_ in range(SECTIONS):
                    if s_ >= 2:
                        sp.wait_ge(section_done, s_ - 1)
                    sp.dma_start(ada[:, s_ % 2], A["ada_w"][0][:, 512 * s_:512 * s_ + 512]
                                 .rearrange("(k p) n -> p k n", p=P)).then_inc(ada_in[s_ % 2], 16)

            @block.gpsimd
            def _(pool):
                pool.memset(ident[:], 0.0).then_inc(consts, 1)
                pool.memset(ones[:], 1.0).then_inc(consts, 1)
                pool.wait_ge(consts, 2)
                pool.affine_select(out=ident[:], in_=ident[:], compare_op=ALU.not_equal, fill=1.0, base=0,
                                   pattern=[[-1, P]], channel_multiplier=1).then_inc(consts, 1)

            @block.scalar
            def _(act):
                for t in range(NTA):
                    src = A["x"][0, P * t:P * t + P, :] if t < NT else A["ctx"][0, P * (t - NT):P * (t - NT) + P, :]
                    act.dma_start(x[:, t, :], src).then_inc(x_in[t], 16)
                act.wait_ge(cols_ready, 1)
                act.activation(sig[:], cols1[:, 64:80], ACT.Sigmoid).then_inc(sig_ready, 1)
                for t in range(NTA):
                    act.wait_ge(x_in[t], 16)
                    if t:
                        act.wait_ge(ss_ready, t)
                    act.activation(junk, x[:, t, :], ACT.Square, accum_out=ss[:, t:t + 1]).then_inc(ss_ready, 1)
                act.wait_ge(norm_step, 1)
                act.activation(rt[:], ss[:], ACT.Sqrt).then_inc(root_ready, 1)
                for s_ in range(SECTIONS):
                    act.wait_ge(section_done, s_ + 1)
                    act.activation(mod_rows[:, s_, :], p_sec[0:2, s_ % 2, :], ACT.Copy).then_inc(section_copied, 1)
                for i, (h, k) in enumerate(GROUPS):
                    a, n = tokens(h)
                    act.wait_ge(h_f, i + 1)
                    act.activation(h_hi[:, k, a:a + n], hf[:, i % 3, :n], ACT.Copy).then_inc(hi_ready, 1)

            @block.vector
            def _(dve):
                dve.wait_ge(rows_t, 1)
                dve.tensor_copy(cols1[:], p_rows[:, 0:80]).then_inc(cols_ready, 1)
                dve.tensor_copy(cols2[:], p_rows[:, 80:136]).then_inc(cols_ready, 1)
                dve.wait_ge(sig_ready, 1)
                dve.wait_ge(cols_ready, 2)
                dve.tensor_tensor(sil[:].rearrange("p s k -> p (s k)"), cols1[:, 64:80], sig[:], ALU.mult)\
                   .then_inc(sil_ready, 1)
                dve.wait_ge(ss_ready, NTA)
                dve.tensor_scalar(ss[:], ss[:], 1.0 / D, EPS, ALU.mult, ALU.add).then_inc(norm_step, 1)
                inverse_root(dve, root_ready, norm_step, 1, ss[:], rt[:], r0[:], tt[:])
                for t in range(NTA):
                    dve.tensor_scalar(x[:, t, :], x[:, t, :], r0[:, t:t + 1], None, ALU.mult).then_inc(xn_ready, 1)
                dve.wait_ge(mod_t, 1)
                for v in range(2):
                    dve.tensor_tensor(mod[:, 0:16, v], p_mod[:, v:32:2], cols1[:, 0:16], ALU.add).then_inc(mod_ready, 1)
                dve.wait_ge(mod_ready, 2)
                for v in range(2):
                    dve.scalar_tensor_tensor(out=scale[:, :, v], in0=mod[:, 8:16, v], scalar=1.0,
                                             in1=cols1[:, 48:56], op0=ALU.add, op1=ALU.mult).then_inc(mod_ready, 1)
                dve.wait_ge(mod_ready, 4)

                def modulate(i):
                    h, k = GROUPS[i]
                    v, n = int(h == 2), tokens(h)[1]
                    dve.wait_ge(x_t, i + 1)
                    if i >= 3:
                        dve.wait_ge(lo_ready, i - 2)
                    dve.tensor_scalar(hf[:, i % 3, :n], p_x[:, i % 3, :n], scale[:, k, v:v + 1], mod[:, k, v:v + 1],
                                      ALU.mult, ALU.add).then_inc(h_f, 1)

                def low_part(i):
                    h, k = GROUPS[i]
                    a, n = tokens(h)
                    dve.wait_ge(hi_ready, i + 1)
                    dve.tensor_tensor(h_lo[:, k, a:a + n], hf[:, i % 3, :n], h_hi[:, k, a:a + n].bitcast(F32),
                                      ALU.subtract).then_inc(lo_ready, 1)

                for i in range(len(GROUPS)):
                    modulate(i)
                    if i:
                        low_part(i - 1)
                low_part(len(GROUPS) - 1)

            @block.tensor
            def _(pe):
                pe.wait_ge(consts, 3)
                pe.wait_ge(rows_in, 80)
                pe.wait_ge(rows2_in, 48)
                pe.transpose(p_rows[:, 0:80], rows1[:], ident[0:80, 0:80])
                pe.transpose(p_rows[:, 80:136], rows2[:], ident[0:56, 0:56]).then_inc(rows_t, 1)
                pe.wait_ge(sil_ready, 1)
                for s_ in range(SECTIONS):
                    pe.wait_ge(ada_in[s_ % 2], 16 * (s_ // 2 + 1))
                    if s_ >= 2:
                        pe.wait_ge(section_copied, s_ - 1)
                    for k in range(KD):
                        mm = pe.matmul(p_sec[0:2, s_ % 2, :], sil[:, :, k], ada[:, s_ % 2, k, :],
                                       start=k == 0, stop=k == KD - 1)
                    mm.then_inc(section_done, 1)
                pe.wait_ge(section_copied, SECTIONS)
                for c in range(4 * SECTIONS):
                    mm = pe.transpose(p_mod[:, 2 * c:2 * c + 2], mod_rows[:, c // 4, P * (c % 4):P * (c % 4) + P],
                                      ident[0:2, 0:2])
                mm.then_inc(mod_t, 1)
                for i, (h, k) in enumerate(GROUPS):
                    if i >= 3:
                        pe.wait_ge(h_f, i - 2)
                    tiles = range(4 * h, min(4 * h + 4, NTA))
                    pe.wait_ge(xn_ready, tiles[-1] + 1)
                    for n, t in enumerate(tiles):
                        mm = pe.transpose(p_x[:, i % 3, P * n:P * n + P], x[:, t, P * k:P * k + P], ident[:])
                    mm.then_inc(x_t, 1)


def three(pe, out, a_hi, a_lo, b_hi, b_lo, start, stop):
    pe.matmul(out, a_hi, b_hi, start=start, stop=False)
    pe.matmul(out, a_hi, b_lo, start=False, stop=False)
    return pe.matmul(out, a_lo, b_hi, start=False, stop=stop)


def projection(g):
    nc, sem, A = g["nc"], g["sem"], g["A"]
    h_hi, h_lo, qkv, cols2 = g["h_hi"], g["h_lo"], g["qkv"], g["cols2"]
    ident, ones, sil, mod, cols1 = g["ident"], g["ones"], g["sil"], g["mod"], g["cols1"]
    groups = []
    for u in range(UNITS):
        if u < QKV_UNITS:
            groups += [(u, t, None) for t in range(NTA if u == QKV_UNITS - 1 else NT)]
        else:
            groups += [(u, c, h) for c in range(2) for h in range(2)]
    first = {}
    for i, (u, _, _) in enumerate(groups):
        first.setdefault(u, i)
    first[UNITS] = len(groups)
    BANKS = 6
    with ExitStack() as s:
        sb, ps = g["scope"](s)
        w = sb("w_raw", [P, 2, KD, UW])
        w_hi = sb("w_hi", [P, 2, KD, UW], F32R)
        w_lo = sb("w_lo", [P, 2, KD, UW], F32R)
        ub = sb("ub", [P, L + 2])
        work = sb("work", [P, 4 * NG * ROT])
        t1 = work[:, 0:L]
        zs = sb("zs", [P, 2, L])
        gs = zs
        ada = sb("ada_rest", [P, KD, UW])
        acc = sb("ada_acc", [P, 2, UW])
        diag = sb("diag", [P, 2, P])
        wrow = sb("wrow", [P, NG, HD])
        cos, sin = sb("cos", [P, NT, ROT]), sb("sin", [P, NT, ROT])
        sq = work[:, 0:NG * HD]
        ssq, root, rstd, tmp = (sb(n, [P, NTA, NG]) for n in ("ssq", "q_root", "rstd", "q_tmp"))
        xn = sb("xn", [P, NG, HD])
        rope = [work[:, NG * ROT * i:NG * ROT * (i + 1)].rearrange("p (h d) -> p h d", d=ROT) for i in range(4)]
        p_mod = ps("p_mod2", [P, 512])
        p_g = ps("p_g", [P, 512])
        pz = ps("p_z", [P, BANKS, 512])
        w_in = [sem(f"w_in{i}") for i in range(2)]
        w_hi_ready, w_lo_ready = sem("w_hi_ready"), sem("w_lo_ready")
        group_done, evacuated = sem("group_done"), sem("evacuated")
        ada_in, acc_step, acc_ready, sums_done = sem("ada2_in"), sem("acc_step"), sem("acc_ready"), sem("sums_done")
        mod_ready, diag_ready, g_done, g_copied = sem("mod2_ready"), sem("diag_ready"), sem("g_done"), sem("g_copied")
        small_in, sq_ready, ssq_ready = sem("small_in"), sem("sq_ready"), sem("ssq_ready")
        q_root, q_step, rope_step, qn_ready = sem("q_root_ready"), sem("q_step"), sem("rope_step"), sem("qn_ready")
        padded, conv_step, z_ready = sem("padded"), sem("conv_step"), sem("z_ready")
        z_stored = [sem(f"z_stored{i}") for i in range(2)]
        g_stored = [sem(f"g_stored{i}") for i in range(2)]
        NZ, NGT = 2 * HY_UNITS, 2 * G_UNITS
        ADA = 4 * D // UW

        with nc.Block() as block:
            @block.sync
            def _(sp):
                def load(u):
                    if u >= 2:
                        sp.wait_ge(w_lo_ready, u - 1)
                    c = unit_column(u)
                    sp.dma_start(w[:, u % 2], A["w_in"][0][:, c:c + UW].rearrange("(k p) n -> p k n", p=P))\
                      .then_inc(w_in[u % 2], 16)
                load(0)
                load(1)
                for i in range(NG):
                    w_ = A["q_norm"] if i < NH else A["k_norm"]
                    sp.dma_start(wrow[:, i, :], w_[0, :].partition_broadcast(P)).then_inc(small_in, 16)
                sp.dma_start(cos[:], A["rope_cos"].rearrange("(t p) d -> p t d", p=P)).then_inc(small_in, 16)
                sp.dma_start(sin[:], A["rope_sin"].rearrange("(t p) d -> p t d", p=P)).then_inc(small_in, 16)
                for u in range(UNITS):
                    if u + 2 < UNITS:
                        load(u + 2)
                    if u < ADA:
                        if u:
                            sp.wait_ge(acc_ready, u)
                        c = 2 * D + UW * u
                        sp.dma_start(ada[:], A["ada_w"][0][:, c:c + UW].rearrange("(k p) n -> p k n", p=P))\
                          .then_inc(ada_in, 16)
                    if QKV_UNITS <= u < QKV_UNITS + HY_UNITS:
                        for c in range(2):
                            i = 2 * (u - QKV_UNITS) + c
                            sp.wait_ge(z_ready, i + 1)
                            sp.dma_start(g["z_dram"][P * i:P * i + P, :], zs[:, i % 2, :]).then_inc(z_stored[i % 2], 16)
                for i in range(2):
                    sp.wait_ge(z_stored[i], 16 * (NZ // 2))

            @block.scalar
            def _(act):
                def high_part(u):
                    act.wait_ge(w_in[u % 2], 16 * (u // 2 + 1))
                    if u >= 2:
                        act.wait_ge(group_done, first[u - 1])
                    act.activation(w_hi[:, u % 2], w[:, u % 2], ACT.Copy).then_inc(w_hi_ready, 1)

                high_part(0)
                act.wait_ge(padded, 1)
                for u in range(UNITS):
                    if u + 1 < UNITS:
                        high_part(u + 1)
                    if u == QKV_UNITS + 1:
                        act.wait_ge(q_step, 1)
                        act.activation(root[:], ssq[:], ACT.Sqrt).then_inc(q_root, 1)
                    for i in range(first[u], first[u + 1]):
                        _, c, h = groups[i]
                        act.wait_ge(group_done, i + 1)
                        src = pz[:, i % BANKS, :]
                        if u < QKV_UNITS:
                            act.activation(qkv[:, c, UW * u:UW * u + UW], src[:, 0:UW], ACT.Copy).then_inc(evacuated, 1)
                        elif u < QKV_UNITS + HY_UNITS:
                            n = 2 * (u - QKV_UNITS) + c
                            if n:
                                act.wait_ge(z_ready, n)
                            act.activation(ub[:, 1 + 512 * h:513 + 512 * h], src, ACT.Copy).then_inc(evacuated, 1)
                        else:
                            n = 2 * (u - QKV_UNITS - HY_UNITS) + c
                            if n < 2 and h == 0:
                                act.wait_ge(z_stored[n % 2], 16 * (NZ // 2))
                            if n >= 2 and h == 0:
                                act.wait_ge(g_stored[n % 2], 16 * (n // 2))
                            act.activation(gs[:, n % 2, 512 * h:512 * h + 512], src, ACT.Sigmoid).then_inc(evacuated, 1)
                            if h == 1:
                                act.wait_ge(evacuated, i + 1)
                                act.dma_start(g["gate_dram"][P * n:P * n + P, :], gs[:, n % 2, :])\
                                   .then_inc(g_stored[n % 2], 16)
                for i in range(2):
                    act.wait_ge(g_stored[i], 16 * (NGT // 2))

            @block.vector
            def _(dve):
                def low_part(u):
                    dve.wait_ge(w_hi_ready, u + 1)
                    dve.tensor_tensor(w_lo[:, u % 2], w[:, u % 2], w_hi[:, u % 2].bitcast(F32), ALU.subtract)\
                       .then_inc(w_lo_ready, 1)

                def ada_part(m):
                    dve.wait_ge(ada_in, 16 * (m + 1))
                    if m >= 2:
                        dve.wait_ge(sums_done, m - 1)
                    a = acc[:, m % 2]
                    dve.tensor_scalar(a, ada[:, 0, :], sil[:, 0, 0:1], None, ALU.mult).then_inc(acc_step, 1)
                    for k in range(1, KD):
                        dve.wait_ge(acc_step, (KD - 1) * m + k)
                        dve.scalar_tensor_tensor(out=a, in0=ada[:, k, :], scalar=sil[:, 0, k:k + 1], in1=a,
                                                 op0=ALU.mult, op1=ALU.add)\
                           .then_inc(acc_step if k < KD - 1 else acc_ready, 1)

                def head_squares(i):
                    a = 0 if i < NT else NH
                    w_ = (NG - a) * HD
                    src = qkv[:, i, HD * a:HD * NG]
                    if i:
                        dve.wait_ge(ssq_ready, i + 1)
                    dve.tensor_tensor(sq[:, 0:w_], src, src, ALU.mult).then_inc(sq_ready, 1)
                    dve.wait_ge(sq_ready, i + 1)
                    dve.tensor_reduce(ssq[:, i, a:NG], sq[:, 0:w_].rearrange("p (h d) -> p h d", d=HD), AX, ALU.add)\
                       .then_inc(ssq_ready, 1)

                rope_steps = 0

                def norm_heads(i):
                    nonlocal rope_steps
                    x = qkv[:, i, 0:NG * HD].rearrange("p (h d) -> p h d", d=HD)
                    r_ = rstd[:, i, :].unsqueeze(2).broadcast_to([P, NG, HD])
                    if i:
                        dve.wait_ge(qn_ready, i)
                    if i < NT:
                        def pairs(t, spec):
                            return t[:, 0:NH].rearrange(spec, s=NKV, g=GRP)
                        dve.tensor_tensor(pairs(xn, "p (g s) d -> p s g d"), pairs(x, "p (s g) d -> p s g d"),
                                          pairs(r_, "p (s g) d -> p s g d"), ALU.mult)
                    dve.tensor_tensor(xn[:, NH:], x[:, NH:], r_[:, NH:], ALU.mult).then_inc(rope_step, 1)
                    rope_steps += 1
                    dve.wait_ge(rope_step, rope_steps)
                    if i >= NT:
                        dve.tensor_tensor(x[:, NH:], xn[:, NH:], wrow[:, NH:], ALU.mult).then_inc(qn_ready, 1)
                        return
                    dve.tensor_tensor(xn[:], xn[:], wrow[:], ALU.mult).then_inc(rope_step, 1)
                    rope_steps += 1
                    dve.wait_ge(rope_step, rope_steps)
                    dve.wait_ge(z_ready, min(2 * (i + 1), NZ))
                    c = cos[:, i, :].unsqueeze(1).broadcast_to([P, NG, ROT])
                    s_ = sin[:, i, :].unsqueeze(1).broadcast_to([P, NG, ROT])
                    even, odd = xn[:, :, 0:HD:2], xn[:, :, 1:HD:2]
                    for r, a, b in zip(rope, (even, odd, even, odd), (c, s_, s_, c)):
                        dve.tensor_tensor(r, a, b, ALU.mult).then_inc(rope_step, 1)
                    rope_steps += 4
                    dve.wait_ge(rope_step, rope_steps)
                    dve.tensor_tensor(x[:, :, 0:HD:2], rope[0], rope[1], ALU.subtract)
                    dve.tensor_tensor(x[:, :, 1:HD:2], rope[2], rope[3], ALU.add).then_inc(qn_ready, 1)

                dve.memset(ub[:], 0.0).then_inc(padded, 1)
                dve.memset(ssq[:], 1.0).then_inc(ssq_ready, 1)
                dve.wait_ge(ssq_ready, 1)
                low_part(0)
                for u in range(UNITS):
                    if u + 1 < UNITS:
                        low_part(u + 1)
                    if u < ADA:
                        ada_part(u)
                    if u == QKV_UNITS:
                        dve.wait_ge(small_in, 16 * (NG + 2))
                        dve.wait_ge(evacuated, first[QKV_UNITS])
                        for i in range(NTA):
                            head_squares(i)
                        dve.wait_ge(ssq_ready, NTA + 1)
                        dve.tensor_scalar(ssq[:], ssq[:], 1.0 / HD, EPS, ALU.mult, ALU.add).then_inc(q_step, 1)
                    if u == QKV_UNITS + 1:
                        inverse_root(dve, q_root, q_step, 1, ssq[:], root[:], rstd[:], tmp[:])
                    if QKV_UNITS < u <= QKV_UNITS + NTA:
                        norm_heads(u - QKV_UNITS - 1)
                    if not QKV_UNITS <= u < QKV_UNITS + HY_UNITS:
                        continue
                    for c in range(2):
                        n = 2 * (u - QKV_UNITS) + c
                        b = ub[:]
                        dve.wait_ge(evacuated, first[u] + 2 * c + 2)
                        if n >= 2:
                            dve.wait_ge(z_stored[n % 2], 16 * (n // 2))
                        if n:
                            dve.wait_ge(z_ready, n)
                        if n >= 2:
                            dve.wait_ge(qn_ready, min(u - QKV_UNITS, NT))
                        dve.tensor_scalar(t1, b[:, 1:L + 1], cols2[:, 12 + n:13 + n], cols2[:, 36 + n:37 + n],
                                          ALU.mult, ALU.add).then_inc(conv_step, 1)
                        dve.wait_ge(conv_step, 2 * n + 1)
                        dve.scalar_tensor_tensor(out=t1, in0=b[:, 0:L], scalar=cols2[:, n:n + 1], in1=t1,
                                                 op0=ALU.mult, op1=ALU.add).then_inc(conv_step, 1)
                        dve.wait_ge(conv_step, 2 * n + 2)
                        dve.scalar_tensor_tensor(out=zs[:, n % 2, :], in0=b[:, 2:L + 2], scalar=cols2[:, 24 + n:25 + n],
                                                 in1=t1, op0=ALU.mult, op1=ALU.add).then_inc(z_ready, 1)
                dve.wait_ge(sums_done, ADA)
                dve.tensor_tensor(mod[:, 16:48, 0], p_mod[:, 0:32], cols1[:, 16:48], ALU.add).then_inc(mod_ready, 1)
                dve.wait_ge(mod_ready, 1)
                dve.scalar_tensor_tensor(out=g["A2"][:], in0=mod[:, 32:40, 0], scalar=1.0, in1=cols1[:, 56:64],
                                         op0=ALU.add, op1=ALU.mult).then_inc(mod_ready, 1)
                for i in range(2 * KD):
                    if i >= 2:
                        dve.wait_ge(g_done, i - 1)
                    c = (16 if i < KD else 40) + i % KD
                    dve.tensor_scalar(diag[:, i % 2, :], ident[:], mod[:, c, 0:1], None, ALU.mult).then_inc(diag_ready, 1)
                    if i % 4 == 3:
                        row = g["g1row"] if i < KD else g["g2row"]
                        dve.wait_ge(g_done, i + 1)
                        q = i // 4
                        dve.tensor_copy(row[:, 512 * (q % 2):512 * (q % 2) + 512], p_g[:]).then_inc(g_copied, 1)

            @block.tensor
            def _(pe):
                def column_sums(m):
                    pe.wait_ge(acc_ready, m + 1)
                    for c in range(2):
                        mm = pe.matmul(p_mod[:, 2 * m + c:2 * m + c + 1], acc[:, m % 2, P * c:P * c + P], ones[:, 0:1],
                                       start=True, stop=True)
                    mm.then_inc(sums_done, 1)

                for u in range(UNITS):
                    if 1 <= u <= ADA:
                        column_sums(u - 1)
                    pe.wait_ge(w_lo_ready, u + 1)
                    b = u % 2
                    for i in range(first[u], first[u + 1]):
                        _, c, h = groups[i]
                        if i >= BANKS:
                            pe.wait_ge(evacuated, i - BANKS + 1)
                        for k in range(KD):
                            if h is None:
                                mm = three(pe, pz[:, i % BANKS, 0:UW],
                                           h_hi[:, k, P * c:P * c + P], h_lo[:, k, P * c:P * c + P],
                                           w_hi[:, b, k, :], w_lo[:, b, k, :], k == 0, k == KD - 1)
                            else:
                                mm = three(pe, pz[:, i % BANKS, :],
                                           w_hi[:, b, k, P * c:P * c + P], w_lo[:, b, k, P * c:P * c + P],
                                           h_hi[:, k, 512 * h:512 * h + 512], h_lo[:, k, 512 * h:512 * h + 512],
                                           k == 0, k == KD - 1)
                        mm.then_inc(group_done, 1)
                for i in range(2 * KD):
                    pe.wait_ge(diag_ready, i + 1)
                    if i >= 4 and i % 4 == 0:
                        pe.wait_ge(g_copied, i // 4)
                    pe.matmul(p_g[:, P * (i % 4):P * (i % 4) + P], ones[:], diag[:, i % 2, :], start=True, stop=True)\
                      .then_inc(g_done, 1)


def inverse_root(dve, act_root, step, at, v, root, r, tmp):
    dve.wait_ge(act_root, 1)
    dve.reciprocal(r, root).then_inc(step, 1)
    dve.wait_ge(step, at + 1)
    dve.tensor_tensor(tmp, r, r, ALU.mult).then_inc(step, 1)
    dve.wait_ge(step, at + 2)
    dve.tensor_tensor(tmp, tmp, v, ALU.mult).then_inc(step, 1)
    dve.wait_ge(step, at + 3)
    dve.tensor_scalar(tmp, tmp, -0.5, 1.5, ALU.mult, ALU.add).then_inc(step, 1)
    dve.wait_ge(step, at + 4)
    dve.tensor_tensor(r, r, tmp, ALU.mult).then_inc(step, 1)
    dve.wait_ge(step, at + 5)


def attention(g):
    nc, sem, A = g["nc"], g["sem"], g["A"]
    qkv, ident, ones = g["qkv"], g["ident"], g["ones"]
    U = NT * NH
    G = NT * NKV
    SC = HD ** -0.5
    QB = 3
    with ExitStack() as s:
        sb, ps = g["scope"](s)
        nsink = sb("nsink", [P, NH])
        q_hi, q_lo = (sb(n, [P, QB, NKV, GRP, P], F32R) for n in ("q_hi", "q_lo"))
        k_hi, k_lo = (sb(n, [P, LA], F32R) for n in ("k_hi", "k_lo"))
        v_hi, v_lo = (sb(n, [P, NTA, P], F32R) for n in ("v_hi", "v_lo"))
        negI, m_prev, m_next = (sb(n, [P, P], BF16) for n in ("negI", "m_prev", "m_next"))
        mx, nm, rs = (sb(n, [P, U]) for n in ("mx", "nm", "rs"))
        es0, es, r = (sb(n, [P, 2, GRP]) for n in ("es0", "es", "r_sum"))
        probs = sb("probs", [P, 3, 640])
        pT_hi, pT_lo = (sb(n, [P, 2, 5, GRP, P], F32R) for n in ("pT_hi", "pT_lo"))
        diag = sb("r_diag", [P, GRP, P])
        o_raw = sb("o_raw", [P, 2, 512])
        yb = sb("yb", [P, 2, 512])
        p_s = ps("p_s", [P, 2, 1024])
        p_pt = ps("p_pt", [P, 1024])
        p_o = ps("p_o", [P, 512])
        p_r = ps("p_r", [P, 512])
        small_in, masks, mask_step = sem("sink_in"), sem("masks"), sem("mask_step")
        w_ready, v_hi_ready, v_lo_ready = sem("sink_ready"), sem("v_hi_ready"), sem("v_lo_ready")
        q_lo_zero = sem("q_lo_zero")
        qk_t, qk_hi, qk_lo = sem("qk_t"), sem("qk_hi"), sem("qk_lo")
        s_done, max_ready, shift_ready, exp_ready = sem("s_done"), sem("max_ready"), sem("shift_ready"), sem("exp_ready")
        pt_done, pt_hi, pt_lo, pv_done = sem("pt_done"), sem("pt_hi"), sem("pt_lo"), sem("pv_done")
        es0_ready, es_ready, r_step = sem("es0_ready"), sem("es_ready"), sem("r_step")
        diag_ready, r_done, o_copied, yb_ready = sem("r_diag_ready"), sem("r_done"), sem("o_copied"), sem("yb_ready")
        y_stored = [sem(f"y_stored{i}") for i in range(2)]
        ORDER = [NT, NT + 1] + list(range(NT))

        def blocks(n):
            return list(range(max(0, n - 1), min(NT - 1, n + 1) + 1))

        def window(n):
            return 512 - P * len(blocks(n)), 512

        def chunks(n):
            a = window(n)[0]
            return [(a + P * i, w) for i, w in enumerate(blocks(n))] + [(512, NT), (512 + P, NT + 1)]

        with nc.Block() as block:
            @block.sync
            def _(sp):
                sp.dma_start(nsink[:], A["attn_sink"][0, :].partition_broadcast(P)).then_inc(small_in, 16)
                for G_ in range(G):
                    n, kv = divmod(G_, NKV)
                    sp.wait_ge(yb_ready, G_ + 1)
                    at = slice(HD * kv, HD * kv + HD)
                    dst = g["yb_dram"][HD * GRP * kv:HD * GRP * (kv + 1), P * n:P * n + P]
                    sp.dma_start(dst.rearrange("(j d) t -> d j t", d=HD),
                                 yb[at, G_ % 2].rearrange("d (j t) -> d j t", j=GRP)).then_inc(y_stored[G_ % 2], 16)
                for i in range(2):
                    sp.wait_ge(y_stored[i], 16 * (G // 2))

            @block.gpsimd
            def _(pool):
                pool.memset(q_hi[:].rearrange("p b s j t -> p (b s j t)").bitcast(F32), 0.0).then_inc(mask_step, 1)
                pool.memset(negI[:], 0.0).then_inc(mask_step, 1)
                pool.memset(m_prev[:], 0.0).then_inc(mask_step, 1)
                pool.memset(m_next[:], 0.0).then_inc(mask_step, 1)
                pool.wait_ge(mask_step, 4)
                pool.affine_select(out=negI[:], in_=negI[:], compare_op=ALU.not_equal, fill=NEG, base=0,
                                   pattern=[[-1, P]], channel_multiplier=1).then_inc(masks, 1)
                pool.affine_select(out=m_prev[:], in_=m_prev[:], compare_op=ALU.is_ge, fill=1.0, base=0,
                                   pattern=[[1, P]], channel_multiplier=-1).then_inc(masks, 1)
                pool.affine_select(out=m_next[:], in_=m_next[:], compare_op=ALU.is_ge, fill=1.0, base=0,
                                   pattern=[[-1, P]], channel_multiplier=1).then_inc(masks, 1)

            def at_unit(u):
                n, h = divmod(u, NH)
                return n + 4 if h == 1 and n + 4 < NTA else None

            def key_columns(t):
                return slice(P * t, P * t + P)

            @block.scalar
            def _(act):
                def high_qk(i):
                    t = ORDER[i]
                    act.wait_ge(qk_t, i + 1)
                    src = p_pt[:]
                    if t < NT:
                        if t >= QB:
                            act.wait_ge(s_done, NH * (t - QB + 1))
                        for kv in range(NKV):
                            at = slice(HD * kv, HD * kv + HD)
                            act.activation(q_hi[at, t % QB, kv], src[at, 0:512].rearrange("p (j t) -> p j t", j=GRP), ACT.Copy)
                    act.activation(k_hi[:, key_columns(t)], src[:, 512:640], ACT.Copy).then_inc(qk_hi, 1)

                act.activation(v_hi[:], qkv[:, :, HD * NG:], ACT.Copy).then_inc(v_hi_ready, 1)
                for i in range(4):
                    if i == 2:
                        act.wait_ge(mask_step, 4)
                    high_qk(i)

                def high_probs(u):
                    n, h = divmod(u, NH)
                    act.wait_ge(pt_done, u + 1)
                    if u >= 2 * GRP and u % GRP == 0:
                        act.wait_ge(pv_done, u // GRP - 1)
                    c = len(chunks(n))
                    act.activation(pT_hi[:, (u // GRP) % 2, 0:c, h % GRP, :],
                                   p_pt[:, 0:P * c].rearrange("p (c t) -> p c t", t=P), ACT.Copy).then_inc(pt_hi, 1)

                def sink_term(G_):
                    act.wait_ge(es0_ready, G_ + 1)
                    act.activation(es[:, G_ % 2], es0[:, G_ % 2], ACT.Exp).then_inc(es_ready, 1)

                def copy_output(G_):
                    at = slice(HD * (G_ % NKV), HD * (G_ % NKV) + HD)
                    act.wait_ge(pv_done, G_ + 1)
                    if G_ >= 2:
                        act.wait_ge(yb_ready, G_ - 1)
                    act.activation(o_raw[at, G_ % 2], p_o[at, :], ACT.Copy).then_inc(o_copied, 1)

                for u in range(U):
                    n = u // NH
                    a = window(n)[0]
                    if u:
                        high_probs(u - 1)
                    act.wait_ge(shift_ready, u + 1)
                    if u >= 3:
                        act.wait_ge(pt_done, u - 2)
                    act.activation(probs[:, u % 3, 0:768 - a], p_s[:, u % 2, a:768], ACT.Exp, bias=nm[:, u:u + 1],
                                   scale=SC, accum_out=rs[:, u:u + 1]).then_inc(exp_ready, 1)
                    if (i := at_unit(u)) is not None:
                        high_qk(i)
                    if u % GRP == GRP - 1:
                        sink_term(u // GRP)
                    if u % GRP == 2 and u > GRP:
                        copy_output(u // GRP - 1)
                high_probs(U - 1)
                copy_output(G - 1)

            @block.vector
            def _(dve):
                dve.memset(q_lo[:].rearrange("p b s j t -> p (b s j t)").bitcast(F32), 0.0).then_inc(q_lo_zero, 1)
                dve.wait_ge(small_in, 16)
                dve.tensor_scalar(nsink[:], nsink[:], -1.0, None, ALU.mult).then_inc(w_ready, 1)
                dve.wait_ge(v_hi_ready, 1)
                dve.tensor_tensor(v_lo[:], qkv[:, :, HD * NG:], v_hi[:].bitcast(F32), ALU.subtract).then_inc(v_lo_ready, 1)
                dve.wait_ge(q_lo_zero, 1)

                def low_qk(i):
                    t = ORDER[i]
                    dve.wait_ge(qk_hi, i + 1)
                    if t < NT:
                        for kv in range(NKV):
                            at = slice(HD * kv, HD * kv + HD)
                            dve.tensor_tensor(q_lo[at, t % QB, kv], p_pt[at, 0:512].rearrange("p (j t) -> p j t", j=GRP),
                                              q_hi[at, t % QB, kv].bitcast(F32), ALU.subtract)
                    dve.tensor_tensor(k_lo[:, key_columns(t)], p_pt[:, 512:640], k_hi[:, key_columns(t)].bitcast(F32),
                                      ALU.subtract).then_inc(qk_lo, 1)

                for i in range(4):
                    low_qk(i)
                dve.wait_ge(w_ready, 1)

                def low_probs(u):
                    n, h = divmod(u, NH)
                    c = len(chunks(n))
                    dve.wait_ge(pt_hi, u + 1)
                    dve.tensor_tensor(pT_lo[:, (u // GRP) % 2, 0:c, h % GRP, :],
                                      p_pt[:, 0:P * c].rearrange("p (c t) -> p c t", t=P),
                                      pT_hi[:, (u // GRP) % 2, 0:c, h % GRP, :].bitcast(F32), ALU.subtract).then_inc(pt_lo, 1)

                def divide_1(G_):
                    dve.wait_ge(es_ready, G_ + 1)
                    dve.tensor_tensor(r[:, G_ % 2], rs[:, GRP * G_:GRP * G_ + GRP], es[:, G_ % 2], ALU.add).then_inc(r_step, 1)
                    dve.wait_ge(r_step, 2 * G_ + 1)
                    dve.reciprocal(r[:, G_ % 2], r[:, G_ % 2]).then_inc(r_step, 1)
                    dve.wait_ge(r_step, 2 * G_ + 2)
                    if G_:
                        dve.wait_ge(r_done, G_)
                    dve.tensor_tensor(diag[:], ident[:].unsqueeze(1).broadcast_to([P, GRP, P]),
                                      r[:, G_ % 2].unsqueeze(2).broadcast_to([P, GRP, P]), ALU.mult).then_inc(diag_ready, 1)

                def divide_2(G_):
                    at = slice(HD * (G_ % NKV), HD * (G_ % NKV) + HD)
                    dve.wait_ge(r_done, G_ + 1)
                    dve.wait_ge(o_copied, G_ + 1)
                    if G_ >= 2:
                        dve.wait_ge(y_stored[G_ % 2], 16 * (G_ // 2))
                    dve.tensor_tensor(yb[at, G_ % 2], o_raw[at, G_ % 2], p_r[at, :], ALU.mult).then_inc(yb_ready, 1)

                def shift(u):
                    n, h = divmod(u, NH)
                    dve.wait_ge(s_done, u + 1)
                    dve.reduce_max(mx[:, u:u + 1], p_s[:, u % 2, window(n)[0]:768], AX).then_inc(max_ready, 1)
                    dve.wait_ge(max_ready, u + 1)
                    dve.tensor_scalar(nm[:, u:u + 1], mx[:, u:u + 1], -SC, nsink[:, h:h + 1], ALU.mult, ALU.min)\
                       .then_inc(shift_ready, 1)

                shift(0)
                for u in range(U):
                    if u:
                        low_probs(u - 1)
                    if (i := at_unit(u)) is not None:
                        low_qk(i)
                    if u + 1 < U:
                        shift(u + 1)
                    if u % GRP == GRP - 1:
                        G_ = u // GRP
                        at = GRP * (G_ % NKV)
                        dve.wait_ge(shift_ready, u + 1)
                        if G_ >= 2:
                            dve.wait_ge(es_ready, G_ - 1)
                        dve.tensor_tensor(es0[:, G_ % 2], nm[:, GRP * G_:GRP * G_ + GRP], nsink[:, at:at + GRP],
                                          ALU.subtract).then_inc(es0_ready, 1)
                    if u % GRP == 1 and u > GRP:
                        divide_1(u // GRP - 1)
                    if u % GRP == 3 and u > GRP:
                        divide_2(u // GRP - 1)
                low_probs(U - 1)
                divide_1(G - 1)
                divide_2(G - 1)

            @block.tensor
            def _(pe):
                def turn_qk(i, units):
                    t = ORDER[i]
                    if i:
                        pe.wait_ge(qk_lo, i)
                    if units:
                        pe.wait_ge(pt_lo, units)
                    q = qkv[:, t, 0:HD * NG]
                    if t < NT:
                        for j in range(GRP):
                            pe.transpose(p_pt[:, P * j:P * j + P], q[:, P * j:P * j + P], ident[:])
                    pe.transpose(p_pt[:, 512:640], q[:, 512:640], ident[:]).then_inc(qk_t, 1)

                for i in range(4):
                    turn_qk(i, 0)
                pe.wait_ge(qk_lo, 4)
                pe.wait_ge(masks, 3)

                def scores(u):
                    n, h = divmod(u, NH)
                    kv, j = divmod(h, GRP)
                    bank, b, (a, _) = p_s[:, u % 2], blocks(n), window(n)
                    qh, ql = q_hi[:, n % QB, kv, j, :], q_lo[:, n % QB, kv, j, :]
                    if h == 0:
                        pe.wait_ge(qk_lo, min(n + 4, NTA))
                    if u >= 2:
                        pe.wait_ge(exp_ready, u - 1)
                    ks = slice(P * b[0], P * b[-1] + P)
                    three(pe, bank[:, a:512], qh, ql, k_hi[:, ks], k_lo[:, ks], True, False)
                    if b[0] < n:
                        pe.matmul(bank[:, a:a + P], negI[:], m_prev[:], start=False, stop=b[-1] == n)
                    if b[-1] > n:
                        pe.matmul(bank[:, 512 - P:512], negI[:], m_next[:], start=False, stop=True)
                    three(pe, bank[:, 512:768], qh, ql, k_hi[:, L:], k_lo[:, L:], True, True).then_inc(s_done, 1)

                def transpose_probs(u):
                    n = u // NH
                    a = window(n)[0]
                    pe.wait_ge(exp_ready, u + 1)
                    if u:
                        pe.wait_ge(pt_lo, u)
                    for i, (c, _) in enumerate(chunks(n)):
                        mm = pe.transpose(p_pt[:, P * i:P * i + P], probs[:, u % 3, c - a:c - a + P], ident[:])
                    mm.then_inc(pt_done, 1)

                def values(G_):
                    n = G_ // NKV
                    pe.wait_ge(pt_lo, GRP * (G_ + 1))
                    if G_ == 0:
                        pe.wait_ge(v_lo_ready, 1)
                    else:
                        pe.wait_ge(o_copied, G_)
                    cs = chunks(n)
                    for i, (_, t) in enumerate(cs):
                        mm = three(pe, p_o[:], v_hi[:, t, :], v_lo[:, t, :],
                                   pT_hi[:, G_ % 2, i].rearrange("p j t -> p (j t)"),
                                   pT_lo[:, G_ % 2, i].rearrange("p j t -> p (j t)"), i == 0, i == len(cs) - 1)
                    mm.then_inc(pv_done, 1)

                def spread(G_):
                    pe.wait_ge(diag_ready, G_ + 1)
                    if G_:
                        pe.wait_ge(yb_ready, G_)
                    pe.matmul(p_r[:], ones[:], diag[:].rearrange("p j t -> p (j t)"), start=True, stop=True)\
                      .then_inc(r_done, 1)

                scores(0)
                for u in range(U):
                    if u + 1 < U:
                        scores(u + 1)
                    if (i := at_unit(u)) is not None:
                        turn_qk(i, u)
                        pe.wait_ge(qk_lo, i + 1)
                    transpose_probs(u)
                    if u % GRP == 0 and u:
                        values(u // GRP - 1)
                    if u % GRP == 2 and u > GRP:
                        spread(u // GRP - 1)
                values(G - 1)
                spread(G - 1)


def hyena(g):
    nc, sem, A = g["nc"], g["sem"], g["A"]
    ident, cols2, ya = g["ident"], g["cols2"], g["ya"]
    T = L // P
    HT = T // 2
    FC = L // 2 // P
    ORD = 2
    TWO_PI = 2.0 * np.pi
    C1 = 6.28125
    C2 = TWO_PI - C1
    MAGIC = 1.5 * 2.0 ** 23
    with ExitStack() as outer:
        sbo, _ = g["scope"](outer)
        hid = sbo("hid", [FH, L])
        fpm = sbo("fpm", [FH, ORD, 2, HY])
        with ExitStack() as s:
            sb, ps = g["scope"](s)
            feat = sb("feat", [EMB, L])
            w1, w2, w3 = sb("fw1", [EMB, FH]), sb("fw2", [FH, FH]), sb("fw3", [FH, FH])
            vec = sb("fvec", [FH, 4])
            fout = sb("fout", [FH, ORD, 2, HY])
            un, kn = sb("un", [FH, L]), sb("kn", [FH, L])
            p_f = ps("p_f", [FH, 2, 512])
            f_in, fz_ready, f_step, sin_ready, fpm_ready = sem("f_in"), sem("fz_ready"), sem("f_step"), sem("sin_ready"), sem("fpm_ready")
            with nc.Block() as block:
                @block.sync
                def _(sp):
                    sp.dma_start(feat[:], A["feat"]).then_inc(f_in, 16)
                    for t, n in ((w1, "filt_w1"), (w2, "filt_w2"), (w3, "filt_w3")):
                        sp.dma_start(t[:], A[n][0]).then_inc(f_in, 16)
                    for i, n in enumerate(("filt_b1", "filt_b2", "filt_b3", "filt_freq")):
                        sp.dma_start(vec[:, i:i + 1], A[n].rearrange("o h -> h o")).then_inc(f_in, 16)
                    sp.dma_start(fout[:].rearrange("h a b c -> h (a b c)"), A["filt_out"][0]).then_inc(f_in, 16)

                @block.tensor
                def _(pe):
                    pe.wait_ge(f_in, 16 * 9)
                    for layer, (w, src) in enumerate(((w1, feat), (w2, hid), (w3, hid))):
                        if layer:
                            pe.wait_ge(sin_ready, layer)
                        for h in range(2):
                            mm = pe.matmul(p_f[:, h, :], w[:], src[:, 512 * h:512 * h + 512], start=True, stop=True)
                        mm.then_inc(fz_ready, 1)

                @block.vector
                def _(dve):
                    dve.wait_ge(f_in, 16 * 9)
                    dve.tensor_tensor(fpm[:, :, 0, :], fout[:, :, 0, :], fout[:, :, 1, :], ALU.add).then_inc(fpm_ready, 1)
                    dve.tensor_tensor(fpm[:, :, 1, :], fout[:, :, 0, :], fout[:, :, 1, :], ALU.subtract).then_inc(fpm_ready, 1)
                    n = 0
                    for layer in range(3):
                        dve.wait_ge(fz_ready, layer + 1)
                        if layer:
                            dve.wait_ge(sin_ready, layer)
                        for op in (
                            lambda: dve.tensor_scalar(un[:], p_f[:].rearrange("h a n -> h (a n)"), vec[:, layer:layer + 1],
                                                      vec[:, 3:4], ALU.add, ALU.mult),
                            lambda: dve.tensor_scalar(kn[:], un[:], 1.0 / TWO_PI, MAGIC, ALU.mult, ALU.add),
                            lambda: dve.tensor_scalar(kn[:], kn[:], -MAGIC, None, ALU.add),
                            lambda: dve.scalar_tensor_tensor(out=un[:], in0=kn[:], scalar=-C1, in1=un[:],
                                                             op0=ALU.mult, op1=ALU.add),
                            lambda: dve.scalar_tensor_tensor(out=un[:], in0=kn[:], scalar=-C2, in1=un[:],
                                                             op0=ALU.mult, op1=ALU.add),
                            lambda: dve.tensor_scalar(un[:], un[:], 3.1415925, -3.1415925, ALU.min, ALU.max),
                        ):
                            op().then_inc(f_step, 1)
                            n += 1
                            dve.wait_ge(f_step, n)

                @block.scalar
                def _(act):
                    for layer in range(3):
                        act.wait_ge(f_step, 6 * (layer + 1))
                        act.activation(hid[:], un[:], ACT.Sin).then_inc(sin_ready, 1)

        with ExitStack() as s:
            sb, ps = g["scope"](s)
            four = sb("four", [P, 4, FC, 512])
            pm = sb("pm", [P, 2, T, HY])
            ut = sb("ut", [P, T, HY])
            spec = sb("spec", [P, 4, FC, HY])
            gate = sb("gate_in", [P, 2, L])
            decay = sb("decay_in", [P, 2, HY])
            cp = sb("cp", [P, 4, HY])
            KX = sb("kx", [P, 8, HY])
            Y = sb("yspec", [P, 4, HY])
            t_a, t_b = sb("t_a", [P, 2, HY]), sb("t_b", [P, 2, HY])
            pj = ps("p_j", [P, 4, 2, 512])
            v_in, four_in, four2_in = sem("v_in"), sem("four_in"), sem("four2_in")
            four_back_in = sem("four_back_in")
            decay_in = [sem(f"decay_in{i}") for i in range(2)]
            gate_in = [sem(f"gate_in{i}") for i in range(2)]
            job, a_done, v_done = sem("job"), sem("act_read"), sem("dve_read")
            step = sem("spectral_step")
            jobs = []
            for o in range(ORD):
                jobs += [("filter", o, c) for c in range(T)]
                jobs += [("turn", o, c) for c in range(HT)]
                jobs += [(k, o, c) for c in range(FC) for k in ("Kc", "Ks", "Xc", "Xs")]
                jobs += [("back", o, c) for c in range(NCH)]
            n_job = {j: i for i, j in enumerate(jobs)}
            acts = {j: i + 1 for i, j in enumerate([j for j in jobs if j[0] not in ("filter", "back")])}
            dves = {j: i + 1 for i, j in enumerate([j for j in jobs if j[0] != "turn"])}

            def spectral_steps(o):
                return (o + 1) * (3 + FC * (4 + 10)) + o * 2 * NCH

            def free(pe, i):
                if i >= 4:
                    j = jobs[i - 4]
                    pe.wait_ge(*((a_done, acts[j]) if j[0] == "turn" else (v_done, dves[j])))

            with nc.Block() as block:
                @block.sync
                def _(sp):
                    sp.dma_start(ya[:], g["z_dram"][0:HY, :].rearrange("(c p) t -> p c t", p=P)).then_inc(v_in, 16)

                    def load_decay(i):
                        c = i % T
                        if i >= 2:
                            sp.wait_ge(v_done, dves[("filter", (i - 2) // T, (i - 2) % T)])
                        sp.dma_start(decay[:, i % 2], A["decay"][P * c:P * c + P, :]).then_inc(decay_in[i % 2], 16)

                    def load_gate(i):
                        o, c = divmod(i, NCH)
                        if i >= 2:
                            sp.wait_ge(v_done, dves[("back", (i - 2) // NCH, (i - 2) % NCH)])
                        at = HY * (o + 1) + P * c
                        sp.dma_start(gate[:, i % 2], g["z_dram"][at:at + P, :]).then_inc(gate_in[i % 2], 16)

                    def load_fourier(rows, s_):
                        for to, m in rows:
                            sp.dma_start(four[:, to], A["fourier"][m].rearrange("(c p) n -> p c n", p=P)).then_inc(s_, 16)

                    load_decay(0)
                    load_decay(1)
                    load_fourier(((0, 0), (1, 1), (2, 2), (3, 3)), four_in)
                    load_gate(0)
                    load_gate(1)
                    for o in range(ORD):
                        for c in range(T):
                            if o * T + c >= 2:
                                load_decay(o * T + c)
                        sp.wait_ge(job, n_job[("Xs", o, FC - 1)] + 1)
                        load_fourier(((0, 4), (2, 5)), four_back_in)
                        for c in range(NCH):
                            if o * NCH + c >= 2:
                                load_gate(o * NCH + c)
                        if o + 1 < ORD:
                            sp.wait_ge(job, n_job[("back", o, NCH - 1)] + 1)
                            load_fourier(((0, 0), (2, 2)), four2_in)

                @block.scalar
                def _(act):
                    for i, j in enumerate(jobs):
                        kind, o, c = j
                        if kind in ("filter", "back"):
                            continue
                        act.wait_ge(job, i + 1)
                        b = pj[:, i % 4]
                        if kind == "turn":
                            act.activation(ut[:, c:T:HT, :], b, ACT.Copy).then_inc(a_done, 1)
                        else:
                            q = ("Kc", "Ks", "Xc", "Xs").index(kind)
                            if o or c:
                                before = (kind, o, c - 1) if c else (kind, o - 1, FC - 1)
                                act.wait_ge(v_done, dves[before])
                            act.activation(cp[:, q], b[:, 0, :], ACT.Copy).then_inc(a_done, 1)

                @block.vector
                def _(dve):
                    steps = 0

                    def done(*instructions):
                        nonlocal steps
                        for i in instructions:
                            i.then_inc(step, 1)
                        steps += len(instructions)
                        dve.wait_ge(step, steps)

                    def tt(out, a, b, op):
                        return dve.tensor_tensor(out, a, b, op)

                    for i, j in enumerate(jobs):
                        kind, o, c = j
                        b = pj[:, i % 4]
                        if kind == "filter":
                            n = o * T + c
                            dve.wait_ge(job, i + 1)
                            dve.wait_ge(decay_in[n % 2], 16 * (n // 2 + 1))
                            if c == 0:
                                done(tt(pm[:, 0, c], b[:, 0], decay[:, n % 2], ALU.mult),
                                     tt(pm[:, 1, c], b[:, 1], decay[:, n % 2], ALU.mult))
                                done(tt(t_a[0:1, 0], pm[0:1, 0, 0], pm[0:1, 1, 0], ALU.add))
                                dve.tensor_scalar(pm[0:1, 0, 0], t_a[0:1, 0], 0.5, None, ALU.mult).then_inc(v_done, 1)
                            else:
                                tt(pm[:, 0, c], b[:, 0], decay[:, n % 2], ALU.mult)
                                tt(pm[:, 1, c], b[:, 1], decay[:, n % 2], ALU.mult).then_inc(v_done, 1)
                        elif kind == "back":
                            n = o * NCH + c
                            dve.wait_ge(job, i + 1)
                            dve.wait_ge(gate_in[n % 2], 16 * (n // 2 + 1))
                            bias = cols2[:, 48 + 4 * o + c:49 + 4 * o + c]
                            y = [ya[:, c, q:L:2] for q in range(2)]
                            done(*[dve.scalar_tensor_tensor(out=y[q], in0=y[q], scalar=bias, in1=b[:, q],
                                                            op0=ALU.mult, op1=ALU.add) for q in range(2)])
                            tt(ya[:, c, :], ya[:, c, :], gate[:, n % 2, :], ALU.mult).then_inc(v_done, 1)
                        elif kind in ("Kc", "Ks", "Xc", "Xs"):
                            q = ("Kc", "Ks", "Xc", "Xs").index(kind)
                            dve.wait_ge(a_done, acts[j])
                            even, odd = cp[:, q], b[:, 1]
                            tt(KX[:, 2 * q], even, odd, ALU.add).then_inc(step, 1)
                            if kind[1] == "c":
                                tt(KX[:, 2 * q + 1], even, odd, ALU.subtract).then_inc(v_done, 1)
                            else:
                                tt(KX[:, 2 * q + 1], odd, even, ALU.subtract).then_inc(v_done, 1)
                            steps += 1
                            if kind == "Xs":
                                dve.wait_ge(step, steps)
                                dve.wait_ge(v_done, dves[j])
                                kr, ki, xr, xi = (KX[:, 2 * z:2 * z + 2] for z in range(4))
                                yr, yi = Y[:, 0:2], Y[:, 2:4]
                                done(tt(t_a[:], xr, kr, ALU.mult), tt(t_b[:], xi, ki, ALU.mult))
                                done(tt(yr, t_a[:], t_b[:], ALU.subtract))
                                done(tt(t_a[:], xr, ki, ALU.mult), tt(t_b[:], xi, kr, ALU.mult))
                                done(tt(yi, t_a[:], t_b[:], ALU.add))
                                done(tt(spec[:, 0, c], Y[:, 0], Y[:, 1], ALU.add),
                                     tt(spec[:, 1, c], Y[:, 2], Y[:, 3], ALU.subtract),
                                     tt(spec[:, 2, c], Y[:, 0], Y[:, 1], ALU.subtract),
                                     tt(spec[:, 3, c], Y[:, 2], Y[:, 3], ALU.add))

                @block.tensor
                def _(pe):
                    for i, j in enumerate(jobs):
                        kind, o, c = j
                        b = pj[:, i % 4]
                        free(pe, i)
                        if kind == "filter":
                            for m in range(2):
                                mm = pe.matmul(b[:, m], hid[:, P * c:P * c + P], fpm[:, o, m, :], start=True, stop=True)
                        elif kind == "turn":
                            if c == 0:
                                if o == 0:
                                    pe.wait_ge(v_in, 16)
                                else:
                                    pe.wait_ge(v_done, dves[("back", o - 1, NCH - 1)])
                            for m in range(2):
                                at = 2 * P * c + m
                                for h in range(NCH):
                                    mm = pe.transpose(b[:, m, P * h:P * h + P], ya[:, h, at:at + 2 * P - 1:2], ident[:])
                        elif kind == "back":
                            if c == 0:
                                pe.wait_ge(four_back_in, 32 * (o + 1))
                                pe.wait_ge(step, spectral_steps(o))
                            for m in range(2):
                                for z in range(2):
                                    for f in range(FC):
                                        mm = pe.matmul(b[:, m], spec[:, 2 * m + z, f, P * c:P * c + P],
                                                       four[:, 2 * z + m, f, :], start=z == 0 and f == 0,
                                                       stop=z == 1 and f == FC - 1)
                        else:
                            if c == 0 and kind == "Kc":
                                if o == 0:
                                    pe.wait_ge(four_in, 64)
                                else:
                                    pe.wait_ge(four2_in, 32 * o)
                                pe.wait_ge(v_done, dves[("filter", o, T - 1)])
                            if c == 0 and kind == "Xc":
                                pe.wait_ge(a_done, acts[("turn", o, HT - 1)])
                            z = int(kind[1] == "s")
                            for m in range(2):
                                src = pm[:, z] if kind[0] == "K" else ut
                                for t in range(HT):
                                    mm = pe.matmul(b[:, m], four[:, 2 * z + m, t, P * c:P * c + P],
                                                   src[:, HT * m + t, :], start=t == 0, stop=t == HT - 1)
                        mm.then_inc(job, 1)


def merge(g):
    nc, sem, A = g["nc"], g["sem"], g["A"]
    ya, ident, mod, A2 = g["ya"], g["ident"], g["mod"], g["A2"]
    with ExitStack() as s:
        sb, ps = g["scope"](s)
        wa, wb = sb("wa", [P, NCH, D]), sb("wb", [P, NCH, D])
        yb = sb("yb_in", [P, NCH, L])
        wo = sb("wo", [P, KD, D])
        gates = sb("gates_in", [P, 2, 2, 512])
        mT = sb("mT", [P, KD, L])
        ta, tb = sb("m_a", [P, 2, 512]), sb("m_b", [P, 2, 512])
        x = sb("x_res", [P, 2, D])
        xn = sb("x_new", [P, NT, D])
        ss, rt, rs, tmp = (sb(n, [P, NT]) for n in ("ss2", "rt2", "rs2", "tmp2"))
        router = sb("router_w", [P, KD, NE])
        h2 = sb("h2", [P, 2, KD, P])
        junk = h2[:, 0].rearrange("p k t -> p (k t)")
        lg, ex = sb("lg", [P, NT, NE]), sb("ex", [P, NT, NE])
        mxl, sm = sb("mxl", [P, NT]), sb("sml", [P, NT])
        pj = ps("p_m", [P, 4, 2, 512])
        a_in, b_in, o_in, r_in = sem("wa_in"), sem("wb_in"), sem("wo_in"), sem("router_in")
        gates_in = [sem(f"gates_in{i}") for i in range(2)]
        xr_in = [sem(f"xr_in{i}") for i in range(2)]
        job, read = sem("m_job"), sem("m_read")
        mul, mt_ready = sem("m_mul"), sem("mt_ready")
        xg_ready, xnew_ready, sq_ready = sem("xg_ready"), sem("xnew_ready"), sem("sq2_ready")
        v_step, rt_ready, xn_ready = sem("v2_step"), sem("rt2_ready"), sem("xn2_ready")
        h_ready = sem("h2_ready")
        sm_step, exp_done = sem("sm_step"), sem("ex_ready")
        aff_t, aff_ready = sem("aff_t"), sem("aff_ready")
        x_stored, xn_stored = sem("x_stored"), sem("xn_stored")
        jobs = [("m", j, h) for j in range(KD) for h in range(2)] + [("o", t, 0) for t in range(NT)] \
            + [("h", t, 0) for t in range(NT)]
        M, O = 2 * KD, 2 * KD + NT

        with nc.Block() as block:
            @block.sync
            def _(sp):
                sp.dma_start(yb[:], g["yb_dram"].rearrange("(c p) t -> p c t", p=P)).then_inc(b_in, 16)
                sp.dma_start(wa[:], A["w_branch_a"][0].rearrange("(c p) n -> p c n", p=P)).then_inc(a_in, 16)
                sp.dma_start(wb[:], A["w_branch_b"][0].rearrange("(c p) n -> p c n", p=P)).then_inc(b_in, 16)
                for i in range(M):
                    if i >= 2:
                        sp.wait_ge(mt_ready, i - 1)
                    j, h = divmod(i, 2)
                    sp.dma_start(gates[:, i % 2], g["gate_dram"][:, 512 * h:512 * h + 512]
                                 .rearrange("(v c p) t -> c p v t", v=2, p=P)[j]).then_inc(gates_in[i % 2], 16)
                    if i == 1:
                        sp.dma_start(wo[:], A["w_out"][0].rearrange("(c p) n -> p c n", p=P)).then_inc(o_in, 16)
                        sp.dma_start(router[:], A["router"][0].rearrange("(c p) n -> p c n", p=P)).then_inc(r_in, 16)
                for t in range(NT):
                    if t >= 2:
                        sp.wait_ge(xnew_ready, t - 1)
                    sp.dma_start(x[:, t % 2], A["x"][0, P * t:P * t + P, :]).then_inc(xr_in[t % 2], 16)
                for t in range(NT):
                    sp.wait_ge(xnew_ready, t + 1)
                    sp.dma_start(g["out"][0, P * t:P * t + P, :], xn[:, t, :]).then_inc(x_stored, 16)
                sp.wait_ge(x_stored, 16 * NT)
                for t in range(NT):
                    sp.wait_ge(xn_ready, t + 1)
                    sp.dma_start(g["xn2_dram"][P * t:P * t + P, :], xn[:, t, :]).then_inc(xn_stored, 16)
                sp.wait_ge(xn_stored, 16 * NT)

            @block.tensor
            def _(pe):
                pe.wait_ge(a_in, 16)
                pe.wait_ge(b_in, 32)

                def logits(t):
                    pe.wait_ge(h_ready, KD * (t + 1))
                    for k in range(KD):
                        mm = pe.matmul(pj[:, (O + NT) % 4, 0, NE * t:NE * t + NE], h2[:, t % 2, k, :], router[:, k, :],
                                       start=k == 0, stop=k == KD - 1)
                    mm.then_inc(job, 1)

                for i, (kind, j, h) in enumerate(jobs):
                    q = i % 4 if kind != "h" else (O + 1 + j % 3) % 4
                    b = pj[:, q]
                    if kind != "h" and i >= 4:
                        pe.wait_ge(read, i - 3)
                    if kind == "h":
                        pe.wait_ge(read, O if j < 3 else O + j - 2)
                    if kind == "m":
                        for br, (w, y) in enumerate(((wa, ya), (wb, yb))):
                            for c in range(NCH):
                                mm = pe.matmul(b[:, br], w[:, c, P * j:P * j + P], y[:, c, 512 * h:512 * h + 512],
                                               start=c == 0, stop=c == NCH - 1)
                    elif kind == "o":
                        if j == 0:
                            pe.wait_ge(o_in, 16)
                            pe.wait_ge(mt_ready, M)
                        for h_ in range(2):
                            for k in range(KD):
                                mm = pe.matmul(b[:, h_], mT[:, k, P * j:P * j + P], wo[:, k, 512 * h_:512 * h_ + 512],
                                               start=k == 0, stop=k == KD - 1)
                    else:
                        pe.wait_ge(xn_ready, j + 1)
                        for k in range(KD):
                            mm = pe.transpose(b[:, k // 4, P * (k % 4):P * (k % 4) + P], xn[:, j, P * k:P * k + P],
                                              ident[:])
                    mm.then_inc(job, 1)
                    if kind == "h":
                        if j == 0:
                            pe.wait_ge(r_in, 16)
                        logits(j)
                pe.wait_ge(sm_step, 6)
                for t in range(NT):
                    mm = pe.transpose(pj[0:NE, (O + 1) % 4, t // 4, P * (t % 4):P * (t % 4) + P], ex[:, t, :], ident[:])
                mm.then_inc(aff_t, 1)

            @block.scalar
            def _(act):
                for t in range(NT):
                    act.wait_ge(xnew_ready, t + 1)
                    if t:
                        act.wait_ge(sq_ready, t)
                    act.activation(junk, xn[:, t, :], ACT.Square, accum_out=ss[:, t:t + 1]).then_inc(sq_ready, 1)
                act.wait_ge(v_step, 1)
                act.activation(rt[:], ss[:], ACT.Sqrt).then_inc(rt_ready, 1)
                act.wait_ge(sm_step, 3)
                act.activation(ex[:], lg[:], ACT.Exp).then_inc(exp_done, 1)

            @block.vector
            def _(dve):
                for i in range(M):
                    j, h = divmod(i, 2)
                    b = pj[:, i % 4]
                    dve.wait_ge(job, i + 1)
                    dve.wait_ge(gates_in[i % 2], 16 * (i // 2 + 1))
                    part = slice(512 * h, 512 * h + 512)
                    if i >= 2:
                        dve.wait_ge(mt_ready, i - 1)
                    dve.tensor_tensor(ta[:, i % 2], gates[:, i % 2, 0], b[:, 0], ALU.mult).then_inc(mul, 1)
                    dve.tensor_tensor(tb[:, i % 2], gates[:, i % 2, 1], b[:, 1], ALU.mult).then_inc(read, 1)
                    dve.wait_ge(mul, i + 1)
                    dve.wait_ge(read, i + 1)
                    dve.tensor_tensor(mT[:, j, part], ta[:, i % 2], tb[:, i % 2], ALU.add).then_inc(mt_ready, 1)
                for t in range(NT):
                    i = M + t
                    dve.wait_ge(job, i + 1)
                    dve.tensor_tensor(xn[:, t, :], pj[:, i % 4].rearrange("p a n -> p (a n)"), g["g1row"][:], ALU.mult)\
                       .then_inc(read, 1)
                    dve.wait_ge(read, i + 1)
                    dve.wait_ge(xr_in[t % 2], 16 * (t // 2 + 1))
                    dve.tensor_tensor(xn[:, t, :], xn[:, t, :], x[:, t % 2], ALU.add).then_inc(xnew_ready, 1)
                dve.wait_ge(sq_ready, NT)
                dve.tensor_scalar(ss[:], ss[:], 1.0 / D, EPS, ALU.mult, ALU.add).then_inc(v_step, 1)
                inverse_root(dve, rt_ready, v_step, 1, ss[:], rt[:], rs[:], tmp[:])
                dve.wait_ge(x_stored, 16 * NT)
                for t in range(NT):
                    dve.tensor_scalar(xn[:, t, :], xn[:, t, :], rs[:, t:t + 1], None, ALU.mult).then_inc(xn_ready, 1)
                for t in range(NT):
                    b = pj[:, (O + 1 + t % 3) % 4]
                    dve.wait_ge(job, O + 2 * t + 1)
                    if t >= 2:
                        dve.wait_ge(job, O + 2 * (t - 1))
                    for k in range(KD):
                        ins = dve.tensor_scalar(h2[:, t % 2, k, :], b[:, k // 4, P * (k % 4):P * (k % 4) + P],
                                                A2[:, k:k + 1], mod[:, 24 + k, 0:1], ALU.mult, ALU.add)
                        ins.then_inc(h_ready, 1)
                        if k == KD - 1:
                            dve.wait_ge(h_ready, KD * (t + 1))
                            dve.tensor_copy(tmp[:, 0:1], rs[:, 0:1]).then_inc(read, 1)
                dve.wait_ge(job, O + 2 * NT)
                lp = pj[:, (O + NT) % 4, 0, 0:NT * NE].rearrange("p (t e) -> p t e", e=NE)
                dve.tensor_reduce(mxl[:], lp, AX, ALU.max).then_inc(sm_step, 1)
                dve.wait_ge(sm_step, 1)
                dve.tensor_copy(lg[:], lp).then_inc(sm_step, 1)
                dve.wait_ge(sm_step, 2)
                dve.tensor_tensor(lg[:], lg[:], mxl[:].unsqueeze(2).broadcast_to([P, NT, NE]), ALU.subtract)\
                   .then_inc(sm_step, 1)
                dve.wait_ge(exp_done, 1)
                dve.tensor_reduce(sm[:], ex[:], AX, ALU.add).then_inc(sm_step, 1)
                dve.wait_ge(sm_step, 4)
                dve.reciprocal(sm[:], sm[:]).then_inc(sm_step, 1)
                dve.wait_ge(sm_step, 5)
                dve.tensor_tensor(ex[:], ex[:], sm[:].unsqueeze(2).broadcast_to([P, NT, NE]), ALU.mult)\
                   .then_inc(sm_step, 1)
                dve.wait_ge(aff_t, 1)
                dve.tensor_copy(g["affT"][:], pj[0:NE, (O + 1) % 4].rearrange("p a n -> p (a n)")).then_inc(aff_ready, 1)


def choice(g):
    nc, sem = g["nc"], g["sem"]
    aff, ident = g["affT"], g["ident"]
    R = CAP // 8
    with ExitStack() as s:
        sb, ps = g["scope"](s)
        vals, idx = sb("vals", [NE, CAP]), sb("idx_rows", [NE, CAP], U32)
        idx_f = sb("idx_f", [NE, CAP])
        p_c = ps("p_c", [P, 2, 512])
        best, found, gone = sem("best"), sem("found"), sem("gone")
        as_float, turned, kept = sem("as_float"), sem("turned"), sem("kept")

        with nc.Block() as block:
            @block.vector
            def _(dve):
                for r in range(R):
                    at = slice(8 * r, 8 * r + 8)
                    if r:
                        dve.wait_ge(gone, r)
                    dve.max(vals[:, at], aff[:]).then_inc(best, 1)
                    dve.wait_ge(best, r + 1)
                    dve.max_index(idx[:, at], vals[:, at], aff[:]).then_inc(found, 1)
                    dve.wait_ge(found, r + 1)
                    dve.match_replace(aff[:], vals[:, at], aff[:], -1.0).then_inc(gone, 1)
                dve.tensor_copy(idx_f[:], idx[:]).then_inc(as_float, 1)
                dve.wait_ge(turned, 1)
                dve.tensor_copy(g["gate"][:], p_c[:, 0, 0:NE]).then_inc(kept, 1)
                dve.tensor_copy(g["idx"][:], p_c[:, 1, 0:NE]).then_inc(kept, 1)
                dve.wait_ge(kept, 2)

            @block.tensor
            def _(pe):
                pe.wait_ge(as_float, 1)
                pe.transpose(p_c[:, 0, 0:NE], vals[:], ident[0:NE, 0:NE])
                pe.transpose(p_c[:, 1, 0:NE], idx_f[:], ident[0:NE, 0:NE]).then_inc(turned, 1)


FQ = FF // 512
EU = 4 * FQ + 2 * FQ
RAW, PARTS = 6, 4
AHEAD = 3
TURNS = FQ + 2
TURN_AT = {5: 0, 9: 1, 13: 2, 16: (3, 4), 17: 5}


def experts(g):
    nc, sem, A = g["nc"], g["sem"], g["A"]
    ident, A2, mod, g2row = g["ident"], g["A2"], g["mod"], g["g2row"]
    idx, gate = g["idx"], g["gate"]
    with ExitStack() as s:
        sb, ps = g["scope"](s)
        ring = sb("ring", [P, RAW, 2048])
        r_hi, r_lo = sb("r_hi", [P, PARTS, 2048], F32R), sb("r_lo", [P, PARTS, 2048], F32R)
        xe = sb("xe", [P, D])
        xf = sb("xf", [P, 2, 4, P])
        x_hi, x_lo = sb("x_hi", [P, KD, P], F32R), sb("x_lo", [P, KD, P], F32R)
        sg, au = sb("sg", [P, 512]), sb("au", [P, 512])
        a_hi, a_lo = sb("a_hi", [P, FF // P, P], F32R), sb("a_lo", [P, FF // P, P], F32R)
        ys, yo = sb("ys", [P, D]), sb("yo", [P, 2, D])
        idx_e = sb("idx_e", [P, 1], U32)
        idx_s = sb("idx_s", [P, 2], U32)
        gate_e = sb("gate_e", [P, 1])
        p_a = ps("p_a", [P, 2, 512])
        p_b = ps("p_b", [P, 512])
        p_y = ps("p_y2", [P, D])
        p_t = ps("p_t2", [P, 2, 512])
        raw_in = [sem(f"raw_in{i}") for i in range(RAW)]
        hi_ready, lo_ready, unit_done = sem("hi_ready"), sem("lo_ready"), sem("unit_done")
        idx_ready, gathered, gate_ready = sem("idx_ready"), sem("gathered"), sem("gate_ready")
        turn, turn_f, turn_hi, turn_lo = sem("turn"), sem("turn_f"), sem("turn_hi"), sem("turn_lo")
        sg_ready, au_step, au_ready = sem("sg_ready"), sem("au_step"), sem("au_ready")
        ys_ready, yo_ready, added = sem("ys_ready"), sem("yo_ready"), sem("added")
        pool_passed = sem("pool_passed")

        def source(e, i):
            if i < 4 * FQ:
                c, q = divmod(i, 4)
                w = A["w_gate"] if q < 2 else A["w_up"]
                return w[0][bass.ds(e, 1), 512 * (q % 2):512 * (q % 2) + 512, 512 * c:512 * c + 512]\
                    .rearrange("e (k p) n -> p (e k) n", p=P)
            j = i - 4 * FQ
            return A["w_down"][0][bass.ds(e, 1), 256 * j:256 * j + 256, :].rearrange("e (k p) n -> p (e k) n", p=P)

        def each_expert(eng, body, first=True, last=True):
            body(0, True, False)
            with eng.Fori(1, NE - 1) as e:
                body(e, False, False)
            body(NE - 1, False, True)

        with nc.Block() as block:
            @block.sync
            def _(sp):
                def body(e, first, last):
                    for i in range(EU):
                        if not (first and i < RAW):
                            sp.wait_ge(lo_ready, EU * e + i - RAW + 1)
                        n = 4 if i < 4 * FQ else 2
                        sp.dma_start(ring[:, i % RAW].rearrange("p (k n) -> p k n", k=n), source(e, i))\
                          .then_inc(raw_in[i % RAW], 16)
                each_expert(sp, body)

            @block.gpsimd
            def _(pool):
                def gather(e):
                    pool.wait_ge(idx_ready, e + 1)
                    pool.sem_inc(pool_passed, 1)
                    pool.indirect_dma_start(out=xe[:], out_offset=None, in_=g["xn2_dram"][:, :],
                                            in_offset=bass.IndirectOffsetOnAxis(ap=idx_e[:, 0:1], axis=0))\
                        .then_inc(gathered, 16)

                def body(e, first, last):
                    if not last:
                        gather(e + 1)
                    pool.wait_ge(yo_ready, e + 1)
                    if not first:
                        pool.wait_ge(added, 16 * e)
                    pool.sem_inc(pool_passed, 1)
                    pool.indirect_dma_start(out=g["out"][0], in_=yo[:, 0], in_offset=None,
                                            out_offset=bass.IndirectOffsetOnAxis(ap=idx_s[:, 0:1], axis=0),
                                            compute_op=ALU.add).then_inc(added, 16)
                gather(0)
                each_expert(pool, body)
                pool.wait_ge(added, 16 * NE)

            @block.scalar
            def _(act):
                def high_part(e, i, before=None):
                    act.wait_ge(raw_in[i % RAW], 16 * (EU // RAW * e + i // RAW + 1))
                    if not before:
                        act.wait_ge(unit_done, EU * e + i - PARTS + 1)
                    act.activation(r_hi[:, i % PARTS], ring[:, i % RAW], ACT.Copy).then_inc(hi_ready, 1)

                def turn_x(e, q):
                    act.wait_ge(turn_f, 2 * e + q + 1)
                    act.activation(x_hi[:, 4 * q:4 * q + 4, :], xf[:, q], ACT.Copy).then_inc(turn_hi, 1)

                def body(e, first, last):
                    for i in range(EU):
                        if not (last and i + AHEAD >= EU):
                            high_part(e, i + AHEAD, first and i + AHEAD < PARTS)
                        if i < 4 * FQ and i % 4 == 3:
                            c = i // 4
                            act.wait_ge(unit_done, EU * e + i - 1)
                            if not (first and c == 0):
                                act.wait_ge(au_step, 2 * (FQ * e + c))
                            act.activation(sg[:], p_a[:, c % 2], ACT.Sigmoid).then_inc(sg_ready, 1)
                        for q in np.atleast_1d(TURN_AT.get(i, [])).astype(int).tolist():
                            if q in (3, 4):
                                if not last:
                                    turn_x(e + 1, q - 3)
                                continue
                            c = min(q, 3)
                            act.wait_ge(turn, turns(e, q, last))
                            act.activation(a_hi[:, 4 * c:4 * c + 4, :].rearrange("p k m -> p (k m)"), p_t[:, q % 2],
                                           ACT.Copy).then_inc(turn_hi, 1)
                        if i == EU - 1:
                            act.wait_ge(unit_done, EU * e + EU)
                            act.wait_ge(gate_ready, e + 1)
                            if not first:
                                act.wait_ge(yo_ready, e)
                            act.activation(ys[:], p_y[:], ACT.Copy, scale=gate_e[:, 0:1]).then_inc(ys_ready, 1)
                for i in range(AHEAD):
                    high_part(0, i, True)
                for q in range(2):
                    turn_x(0, q)
                each_expert(act, body)

            @block.vector
            def _(dve):
                def low_part(e, i):
                    dve.wait_ge(hi_ready, EU * e + i + 1)
                    dve.tensor_tensor(r_lo[:, i % PARTS], ring[:, i % RAW], r_hi[:, i % PARTS].bitcast(F32),
                                      ALU.subtract).then_inc(lo_ready, 1)

                def take_index(e, first):
                    if not first:
                        dve.wait_ge(gathered, 16 * e)
                    dve.tensor_copy(idx_e[:, 0:1], idx[:, bass.ds(e, 1)]).then_inc(idx_ready, 1)

                def turn_x(e, q, n, bank):
                    dve.wait_ge(turn, n + 1)
                    for k in range(4):
                        ins = dve.tensor_scalar(xf[:, q, k, :], p_t[:, bank, P * k:P * k + P],
                                                A2[:, 4 * q + k:4 * q + k + 1], mod[:, 24 + 4 * q + k, 0:1],
                                                ALU.mult, ALU.add)
                    ins.then_inc(turn_f, 1)
                    dve.wait_ge(turn_hi, n + 1)
                    dve.tensor_tensor(x_lo[:, 4 * q:4 * q + 4, :], xf[:, q], x_hi[:, 4 * q:4 * q + 4, :].bitcast(F32),
                                      ALU.subtract).then_inc(turn_lo, 1)

                def body(e, first, last):
                    for i in range(EU):
                        if not (last and i + AHEAD >= EU):
                            low_part(e, i + AHEAD)
                        if i == 0 and not last:
                            take_index(e + 1, False)
                        if i == 1:
                            if not first:
                                dve.wait_ge(ys_ready, e)
                                dve.wait_ge(added, 16 * e)
                            dve.tensor_copy(gate_e[:, 0:1], gate[:, bass.ds(e, 1)]).then_inc(gate_ready, 1)
                            dve.tensor_copy(idx_s[:, 0:1], idx[:, bass.ds(e, 1)])
                        if i < 4 * FQ and i % 4 == 3:
                            c = i // 4
                            dve.wait_ge(sg_ready, FQ * e + c + 1)
                            if not (first and c == 0):
                                dve.wait_ge(turn, turns(e, c - 1, last) if c else turns_before(e))
                            dve.tensor_tensor(au[:], sg[:], p_a[:, c % 2], ALU.mult).then_inc(au_step, 1)
                            dve.wait_ge(au_step, 2 * (FQ * e + c) + 1)
                            dve.wait_ge(unit_done, EU * e + i + 1)
                            dve.tensor_tensor(au[:], au[:], p_b[:], ALU.mult).then_inc(au_step, 1)
                        for q in np.atleast_1d(TURN_AT.get(i, [])).astype(int).tolist():
                            if q in (3, 4):
                                if not last:
                                    turn_x(e + 1, q - 3, turns(e, q, last) - 1, q % 2)
                                continue
                            c = min(q, 3)
                            n = turns(e, q, last)
                            dve.wait_ge(turn_hi, n)
                            dve.tensor_tensor(a_lo[:, 4 * c:4 * c + 4, :].rearrange("p k m -> p (k m)"), p_t[:, q % 2],
                                              a_hi[:, 4 * c:4 * c + 4, :].rearrange("p k m -> p (k m)").bitcast(F32),
                                              ALU.subtract).then_inc(turn_lo, 1)
                        if i == EU - 1:
                            dve.wait_ge(ys_ready, e + 1)
                            dve.tensor_tensor(yo[:, 0], ys[:], g2row[:], ALU.mult).then_inc(yo_ready, 1)
                take_index(0, True)
                for i in range(AHEAD):
                    low_part(0, i)
                for q in range(2):
                    turn_x(0, q, q, q)
                each_expert(dve, body)

            @block.tensor
            def _(pe):
                def turn_x(e, q, n, bank):
                    if q == 0:
                        pe.wait_ge(gathered, 16 * (e + 1))
                    if not (isinstance(n, int) and n < 2):
                        pe.wait_ge(turn_lo, n - 1)
                    for k in range(4):
                        mm = pe.transpose(p_t[:, bank, P * k:P * k + P], xe[:, P * (4 * q + k):P * (4 * q + k) + P],
                                          ident[:])
                    mm.then_inc(turn, 1)

                def turn_a(e, q, n):
                    c = min(q, 3)
                    pe.wait_ge(au_step, 2 * (FQ * e + c + 1))
                    pe.wait_ge(turn_lo, n - 1)
                    for k in range(4):
                        mm = pe.transpose(p_t[:, q % 2, P * k:P * k + P], au[:, P * k:P * k + P], ident[:])
                    mm.then_inc(turn, 1)

                def body(e, first, last):
                    for i in range(EU):
                        pe.wait_ge(lo_ready, EU * e + i + 1)
                        hi, lo = r_hi[:, i % PARTS], r_lo[:, i % PARTS]
                        if i < 4 * FQ:
                            c, q = divmod(i, 4)
                            out = p_a[:, c % 2] if q < 2 else p_b[:]
                            if i == 0:
                                pe.wait_ge(turn_lo, turns_before(e))
                            if q == 0 and not (first and c < 2):
                                pe.wait_ge(au_step, 2 * (FQ * e + c - 1))
                            if q == 2 and not (first and c == 0):
                                pe.wait_ge(au_step, 2 * (FQ * e + c))
                            for k in range(4):
                                kk = 4 * (q % 2) + k
                                mm = three(pe, out, x_hi[:, kk, :], x_lo[:, kk, :], hi[:, 512 * k:512 * k + 512],
                                           lo[:, 512 * k:512 * k + 512], kk == 0, kk == KD - 1)
                        else:
                            j = i - 4 * FQ
                            if j == 0 and not first:
                                pe.wait_ge(ys_ready, e)
                            if j % 2 == 0:
                                c = j // 2
                                pe.wait_ge(turn_lo, turns(e, c if c < 3 else 5, last))
                            for k in range(2):
                                kk = 2 * j + k
                                for h in range(2):
                                    at = slice(D * k + 512 * h, D * k + 512 * h + 512)
                                    mm = three(pe, p_y[:, 512 * h:512 * h + 512], a_hi[:, kk, :], a_lo[:, kk, :],
                                               hi[:, at], lo[:, at], kk == 0, kk == FF // P - 1)
                        mm.then_inc(unit_done, 1)
                        for q in np.atleast_1d(TURN_AT.get(i, [])).astype(int).tolist():
                            n = turns(e, q, last) - 1
                            if q in (3, 4):
                                if not last:
                                    turn_x(e + 1, q - 3, n, q % 2)
                            else:
                                turn_a(e, q, n)
                for q in range(2):
                    turn_x(0, q, q, q)
                each_expert(pe, body)


def turns_before(e):
    return TURNS * e + 2


def turns(e, q, last):
    return TURNS * e + q + 3 - (2 if last and q == 5 else 0)


INPUTS = ["x", "c", "ctx", "c_ctx", "ada_w", "ada_b", "norm1", "norm2", "w_in", "conv_w", "conv_b", "filt_w1",
          "filt_b1", "filt_w2", "filt_b2", "filt_w3", "filt_b3", "filt_freq", "filt_out", "hyena_bias", "q_norm",
          "k_norm", "attn_sink", "w_branch_a", "w_branch_b", "w_out", "router", "w_gate", "w_up", "w_down"]


def kernel(**inputs):
    from concourse import bacc
    from concourse.bass_utils import run_bass_kernel_spmd

    nc = bacc.Bacc("TRN2", target_bir_lowering=False, num_devices=1)
    arrays = {f"in_{n}": np.ascontiguousarray(inputs[n]) for n in INPUTS}
    arrays.update({f"in_{n}": a for n, a in shape_constants().items()})
    A = {n[3:]: nc.dram_tensor(n, a.shape, mybir.dt.from_np(a.dtype), kind="ExternalInput").ap()
         for n, a in arrays.items()}
    out = nc.dram_tensor("out_x", (1, L, D), F32, kind="ExternalOutput").ap()
    build(nc, A, out)
    r = run_bass_kernel_spmd(nc, [arrays], core_ids=[0])
    return r.results[0]["out_x"]
```

```python
from contextlib import ExitStack

import numpy as np

import concourse.bass as bass
from concourse import mybir

P = 128
D = 1024
L = 1024
LC = 256
KD = D // P
NT = L // P
NTC = LC // P
NTA = NT + NTC
LA = L + LC
HY = 512
NCH = HY // P
NH = 8
NKV = 2
HD = 64
OFF_Q = 3 * HY
OFF_G = OFF_Q + NH * HD + 2 * NKV * HD
QKV = OFF_G - OFF_Q
NE = 16
CAP = 2 * L // NE
FF = 2048
BANDS = 16
EMB = 1 + 2 * BANDS
FH = 64
EPS = 1e-6
NEG = -1e30
GRID_W = 64
NG = NH + NKV
GRP = NH // NKV
ROT = HD // 2

F32 = mybir.dt.float32
F32R = mybir.dt.float32r
BF16 = mybir.dt.bfloat16
I32 = mybir.dt.int32
U32 = mybir.dt.uint32
ALU = mybir.AluOpType
ACT = mybir.ActivationFunctionType
AX = mybir.AxisListType.X

UW = 256
QKV_UNITS = QKV // UW
HY_UNITS = OFF_Q // UW
G_UNITS = 2 * D // UW
UNITS = QKV_UNITS + HY_UNITS + G_UNITS

FQ = FF // 512
EU = 4 * FQ + 2 * FQ
RAW, PARTS = 12, 4
AHEAD = 3
TURNS = FQ + 2
TURN_AT = {5: 0, 9: 1, 13: 2, 16: (3, 4), 17: 5}


def unit_column(u):
    if u < QKV_UNITS:
        return OFF_Q + u * UW
    if u < QKV_UNITS + HY_UNITS:
        return (u - QKV_UNITS) * UW
    return OFF_G + (u - QKV_UNITS - HY_UNITS) * UW


def shape_constants():
    f = np.float32
    t = np.linspace(0.0, 1.0, L, dtype=f)[:, None]
    w = (f(2.0 * np.pi) * np.arange(L, dtype=f)[:, None] / f(L)).astype(f)
    fr = np.linspace(1e-4, BANDS - 1, BANDS, dtype=f)[None, :]
    feat = np.concatenate([t, np.cos((fr * w).astype(f)), -np.sin((fr * w).astype(f))], axis=-1).astype(f)
    lo, hi = np.log(1e-2) / 1.5, np.log(1e-2) / 0.3
    deltas = np.linspace(lo, hi, HY, dtype=f)
    decay = np.exp(-t * np.abs(deltas)).astype(f)
    order = np.concatenate([np.arange(0, L, 2), np.arange(1, L, 2)])
    row = np.repeat(np.arange(L // GRID_W, dtype=f), GRID_W)
    col = np.tile(np.arange(GRID_W, dtype=f), L // GRID_W)
    inv = (f(10000.0) ** (-np.arange(0, ROT, 2, dtype=f) / f(ROT))).astype(f)
    ang = np.concatenate([row[:, None] * inv, col[:, None] * inv], axis=-1).astype(f)
    fq = np.pi * (2 * np.arange(L // 2)[:, None] + 1) / (2 * L)
    j = np.arange(L // 2)[None, :]
    ce, se = np.cos(fq * 2 * j), np.sin(fq * 2 * j)
    co, so = np.cos(fq * (2 * j + 1)), np.sin(fq * (2 * j + 1))
    fourier = np.stack([ce.T, co, se.T, so, ce, se]).astype(f)
    return {
        "feat": np.ascontiguousarray(feat[order].T),
        "decay": np.ascontiguousarray(decay[order] / f(L)),
        "rope_cos": np.cos(ang).astype(f),
        "rope_sin": np.sin(ang).astype(f),
        "fourier": fourier,
    }


def build(nc, A, out):
    root = ExitStack()
    with root:
        def sem(name):
            return root.enter_context(nc.semaphore(name))

        def scope(stack):
            def sb(name, shape, dt=F32):
                return stack.enter_context(nc.sbuf_tensor(name, shape, dt))

            def ps(name, shape, dt=F32):
                return stack.enter_context(nc.psum_tensor(name, shape, dt))
            return sb, ps

        g = {"nc": nc, "sem": sem, "scope": scope, "A": A, "out": out}
        sb, _ = scope(root)
        g["z_dram"] = nc.dram_tensor("z_dram", [OFF_Q, L], F32).ap()
        g["gate_dram"] = nc.dram_tensor("gate_dram", [2 * D, L], F32).ap()
        g["yb_dram"] = nc.dram_tensor("yb_dram", [NH * HD, L], F32).ap()
        g["xn2_dram"] = nc.dram_tensor("xn2_dram", [L, D], F32).ap()
        g["ident"] = sb("ident", [P, P])
        g["ones"] = sb("ones", [P, P])
        g["cols1"] = sb("cols1", [P, 80])
        g["cols2"] = sb("cols2", [P, 56])
        g["A2"] = sb("A2", [P, KD])
        g["mod"] = sb("mod", [P, 48, 2])
        g["g1row"] = sb("g1row", [P, D])
        g["g2row"] = sb("g2row", [P, D])
        with ExitStack() as s12:
            sb12, _ = scope(s12)
            g["qkv"] = sb12("qkv", [P, NTA, QKV])
            g["sil"] = sb12("sil", [P, 2, KD])
            with ExitStack() as s:
                sbh, _ = scope(s)
                g["h_hi"] = sbh("h_hi", [P, KD, LA], F32R)
                g["h_lo"] = sbh("h_lo", [P, KD, LA], F32R)
                modulation(g)
                projection(g)
            attention(g)
        with ExitStack() as s:
            sby, _ = scope(s)
            g["ya"] = sby("ya", [P, NCH, L])
            hyena(g)
            g["late"] = root.enter_context(nc.sbuf_tensor("late", [P, L], F32, side="right"))
            g["affT"] = g["late"][0:NE, :]
            g["ring"] = root.enter_context(nc.sbuf_tensor("ring", [P, RAW, 2048], F32, side="right"))
            g["raw_in"] = [sem(f"raw_in{i}") for i in range(RAW)]
            merge(g)
        with ExitStack() as s:
            sbe, _ = scope(s)
            g["idx"] = sbe("idx", [P, NE], U32)
            g["gate"] = sbe("gate", [P, NE])
            choice(g)
            experts(g)


def modulation(g):
    nc, sem, A = g["nc"], g["sem"], g["A"]
    ident, ones, cols1, cols2, mod = g["ident"], g["ones"], g["cols1"], g["cols2"], g["mod"]
    h_hi, h_lo, sil = g["h_hi"], g["h_lo"], g["sil"]
    GROUPS = [(h, k) for h in range(3) for k in range(KD)]
    SECTIONS = 2 * D // 512
    with ExitStack() as s:
        sb, ps = g["scope"](s)
        rows1, rows2 = sb("rows1", [80, P]), sb("rows2", [56, P])
        sig = sb("sig", [P, 2 * KD])
        ada = sb("ada", [P, 2, KD, 512])
        mod_rows = sb("mod_rows", [2, SECTIONS, 512])
        x = sb("x_in", [P, NTA, D])
        ss, rt, r0, tt = (sb(n, [P, NTA]) for n in ("ss", "rt", "r0", "tt"))
        scale = sb("mod_scale", [P, KD, 2])
        hf = sb("hf", [P, 3, 512])
        junk = hf[:].rearrange("p a n -> p (a n)")[:, 0:D]
        p_rows = ps("p_rows", [P, 512])
        p_mod = ps("p_mod", [P, 512])
        p_x = ps("p_x", [P, 3, 512])
        p_sec = ps("p_sec", [P, 2, 512])
        rows_in, rows2_in = sem("rows_in"), sem("rows2_in")
        ada_in = [sem(f"ada_in{i}") for i in range(2)]
        x_in = [sem(f"x_in{i}") for i in range(NTA // 2)]
        consts = sem("consts")
        rows_t, cols_ready = sem("rows_t"), sem("cols_ready")
        sig_ready, sil_ready = sem("sig_ready"), sem("sil_ready")
        section_done, section_copied, mod_t = sem("section_done"), sem("section_copied"), sem("mod_t")
        mod_ready = sem("mod_ready")
        ss_ready, root_ready, norm_step, xn_ready = sem("ss_ready"), sem("root_ready"), sem("norm_step"), sem("xn_ready")
        x_t, h_f, hi_ready, lo_ready = sem("x_t"), sem("h_f"), sem("h_hi_ready"), sem("h_lo_ready")

        def tokens(h):
            return (512 * h, 512) if h < 2 else (L, LC)

        with nc.Block() as block:
            @block.sync
            def _(sp):
                at = 0
                for name, n in (("ada_b", 48), ("norm1", 8), ("norm2", 8), ("c", 8)):
                    sp.dma_start(rows1[at:at + n, :], A[name].rearrange("o (j p) -> (o j) p", p=P)).then_inc(rows_in, 16)
                    at += n
                sp.dma_start(rows1[at:at + 8, :], A["c_ctx"].rearrange("(j p) -> j p", p=P)).then_inc(rows_in, 16)
                sp.dma_start(rows2[0:36, :], A["conv_w"].rearrange("o r (j p) -> (o r j) p", p=P)).then_inc(rows2_in, 16)
                sp.dma_start(rows2[36:48, :], A["conv_b"].rearrange("o (j p) -> (o j) p", p=P)).then_inc(rows2_in, 16)
                sp.dma_start(rows2[48:56, :], A["hyena_bias"].rearrange("o r (j p) -> (o r j) p", p=P)).then_inc(rows2_in, 16)
                for s_ in range(SECTIONS):
                    if s_ >= 2:
                        sp.wait_ge(section_done, s_ - 1)
                    sp.dma_start(ada[:, s_ % 2], A["ada_w"][0][:, 512 * s_:512 * s_ + 512]
                                 .rearrange("(k p) n -> p k n", p=P)).then_inc(ada_in[s_ % 2], 16)

            @block.gpsimd
            def _(pool):
                pool.memset(ident[:], 0.0).then_inc(consts, 1)
                pool.memset(ones[:], 1.0).then_inc(consts, 1)
                pool.wait_ge(consts, 2)
                pool.affine_select(out=ident[:], in_=ident[:], compare_op=ALU.not_equal, fill=1.0, base=0,
                                   pattern=[[-1, P]], channel_multiplier=1).then_inc(consts, 1)

            @block.scalar
            def _(act):
                for i in range(NTA // 2):
                    src = A["x"][0, 2 * P * i:2 * P * i + 2 * P, :] if 2 * i < NT else A["ctx"][0]
                    act.dma_start(x[:, 2 * i:2 * i + 2, :], src.rearrange("(t p) d -> p t d", p=P)).then_inc(x_in[i], 16)
                act.wait_ge(cols_ready, 1)
                act.activation(sig[:], cols1[:, 64:80], ACT.Sigmoid).then_inc(sig_ready, 1)
                for t in range(NTA):
                    act.wait_ge(x_in[t // 2], 16)
                    if t:
                        act.wait_ge(ss_ready, t)
                    act.activation(junk, x[:, t, :], ACT.Square, accum_out=ss[:, t:t + 1]).then_inc(ss_ready, 1)
                act.wait_ge(norm_step, 1)
                act.activation(rt[:], ss[:], ACT.Sqrt).then_inc(root_ready, 1)
                for s_ in range(SECTIONS):
                    act.wait_ge(section_done, s_ + 1)
                    act.activation(mod_rows[:, s_, :], p_sec[0:2, s_ % 2, :], ACT.Copy).then_inc(section_copied, 1)
                for i, (h, k) in enumerate(GROUPS):
                    a, n = tokens(h)
                    act.wait_ge(h_f, i + 1)
                    act.activation(h_hi[:, k, a:a + n], hf[:, i % 3, :n], ACT.Copy).then_inc(hi_ready, 1)

            @block.vector
            def _(dve):
                dve.wait_ge(rows_t, 1)
                dve.tensor_copy(cols1[:], p_rows[:, 0:80]).then_inc(cols_ready, 1)
                dve.tensor_copy(cols2[:], p_rows[:, 80:136]).then_inc(cols_ready, 1)
                dve.wait_ge(sig_ready, 1)
                dve.wait_ge(cols_ready, 2)
                dve.tensor_tensor(sil[:].rearrange("p s k -> p (s k)"), cols1[:, 64:80], sig[:], ALU.mult)\
                   .then_inc(sil_ready, 1)
                dve.wait_ge(ss_ready, NTA)
                dve.tensor_scalar(ss[:], ss[:], 1.0 / D, EPS, ALU.mult, ALU.add).then_inc(norm_step, 1)
                inverse_root(dve, root_ready, norm_step, 1, ss[:], rt[:], r0[:], tt[:])
                for t in range(NTA):
                    dve.tensor_scalar(x[:, t, :], x[:, t, :], r0[:, t:t + 1], None, ALU.mult).then_inc(xn_ready, 1)
                dve.wait_ge(mod_t, 1)
                for v in range(2):
                    dve.tensor_tensor(mod[:, 0:16, v], p_mod[:, v:32:2], cols1[:, 0:16], ALU.add).then_inc(mod_ready, 1)
                dve.wait_ge(mod_ready, 2)
                for v in range(2):
                    dve.scalar_tensor_tensor(out=scale[:, :, v], in0=mod[:, 8:16, v], scalar=1.0,
                                             in1=cols1[:, 48:56], op0=ALU.add, op1=ALU.mult).then_inc(mod_ready, 1)
                dve.wait_ge(mod_ready, 4)

                def modulate(i):
                    h, k = GROUPS[i]
                    v, n = int(h == 2), tokens(h)[1]
                    dve.wait_ge(x_t, i + 1)
                    if i >= 3:
                        dve.wait_ge(lo_ready, i - 2)
                    dve.tensor_scalar(hf[:, i % 3, :n], p_x[:, i % 3, :n], scale[:, k, v:v + 1], mod[:, k, v:v + 1],
                                      ALU.mult, ALU.add).then_inc(h_f, 1)

                def low_part(i):
                    h, k = GROUPS[i]
                    a, n = tokens(h)
                    dve.wait_ge(hi_ready, i + 1)
                    dve.tensor_tensor(h_lo[:, k, a:a + n], hf[:, i % 3, :n], h_hi[:, k, a:a + n].bitcast(F32),
                                      ALU.subtract).then_inc(lo_ready, 1)

                for i in range(len(GROUPS)):
                    modulate(i)
                    if i:
                        low_part(i - 1)
                low_part(len(GROUPS) - 1)

            @block.tensor
            def _(pe):
                pe.wait_ge(consts, 3)
                pe.wait_ge(rows_in, 80)
                pe.wait_ge(rows2_in, 48)
                pe.transpose(p_rows[:, 0:80], rows1[:], ident[0:80, 0:80])
                pe.transpose(p_rows[:, 80:136], rows2[:], ident[0:56, 0:56]).then_inc(rows_t, 1)
                pe.wait_ge(sil_ready, 1)
                for s_ in range(SECTIONS):
                    pe.wait_ge(ada_in[s_ % 2], 16 * (s_ // 2 + 1))
                    if s_ >= 2:
                        pe.wait_ge(section_copied, s_ - 1)
                    for k in range(KD):
                        mm = pe.matmul(p_sec[0:2, s_ % 2, :], sil[:, :, k], ada[:, s_ % 2, k, :],
                                       start=k == 0, stop=k == KD - 1)
                    mm.then_inc(section_done, 1)
                pe.wait_ge(section_copied, SECTIONS)
                for c in range(4 * SECTIONS):
                    mm = pe.transpose(p_mod[:, 2 * c:2 * c + 2], mod_rows[:, c // 4, P * (c % 4):P * (c % 4) + P],
                                      ident[0:2, 0:2])
                mm.then_inc(mod_t, 1)
                for i, (h, k) in enumerate(GROUPS):
                    if i >= 3:
                        pe.wait_ge(h_f, i - 2)
                    tiles = range(4 * h, min(4 * h + 4, NTA))
                    pe.wait_ge(xn_ready, tiles[-1] + 1)
                    for n, t in enumerate(tiles):
                        mm = pe.transpose(p_x[:, i % 3, P * n:P * n + P], x[:, t, P * k:P * k + P], ident[:])
                    mm.then_inc(x_t, 1)


def three(pe, out, a_hi, a_lo, b_hi, b_lo, start, stop):
    pe.matmul(out, a_hi, b_hi, start=start, stop=False)
    pe.matmul(out, a_hi, b_lo, start=False, stop=False)
    return pe.matmul(out, a_lo, b_hi, start=False, stop=stop)


def projection(g):
    nc, sem, A = g["nc"], g["sem"], g["A"]
    h_hi, h_lo, qkv, cols2 = g["h_hi"], g["h_lo"], g["qkv"], g["cols2"]
    ident, ones, sil, mod, cols1 = g["ident"], g["ones"], g["sil"], g["mod"], g["cols1"]
    groups = []
    for u in range(UNITS):
        if u < QKV_UNITS:
            groups += [(u, t, None) for t in range(NTA if u == QKV_UNITS - 1 else NT)]
        else:
            groups += [(u, c, h) for c in range(2) for h in range(2)]
    first = {}
    for i, (u, _, _) in enumerate(groups):
        first.setdefault(u, i)
    first[UNITS] = len(groups)
    BANKS = 6
    with ExitStack() as s:
        sb, ps = g["scope"](s)
        w = sb("w_raw", [P, 2, KD, UW])
        w_hi = sb("w_hi", [P, 2, KD, UW], F32R)
        w_lo = sb("w_lo", [P, 2, KD, UW], F32R)
        ub = sb("ub", [P, L + 2])
        work = sb("work", [P, 4 * NG * ROT])
        t1 = work[:, 0:L]
        zs = sb("zs", [P, 2, L])
        gs = zs
        ada = sb("ada_rest", [P, KD, UW])
        acc = sb("ada_acc", [P, 2, UW])
        diag = sb("diag", [P, 2, P])
        wrow = sb("wrow", [P, NG, HD])
        cos, sin = sb("cos", [P, NT, ROT]), sb("sin", [P, NT, ROT])
        sq = work[:, 0:NG * HD]
        ssq, root, rstd, tmp = (sb(n, [P, NTA, NG]) for n in ("ssq", "q_root", "rstd", "q_tmp"))
        xn = sb("xn", [P, NG, HD])
        rope = [work[:, NG * ROT * i:NG * ROT * (i + 1)].rearrange("p (h d) -> p h d", d=ROT) for i in range(4)]
        p_mod = ps("p_mod2", [P, 512])
        p_g = ps("p_g", [P, 512])
        pz = ps("p_z", [P, BANKS, 512])
        w_in = [sem(f"w_in{i}") for i in range(2)]
        w_hi_ready, w_lo_ready = sem("w_hi_ready"), sem("w_lo_ready")
        group_done, evacuated = sem("group_done"), sem("evacuated")
        ada_in, acc_step, acc_ready, sums_done = sem("ada2_in"), sem("acc_step"), sem("acc_ready"), sem("sums_done")
        mod_ready, diag_ready, g_done, g_copied = sem("mod2_ready"), sem("diag_ready"), sem("g_done"), sem("g_copied")
        small_in, sq_ready, ssq_ready = sem("small_in"), sem("sq_ready"), sem("ssq_ready")
        q_root, q_step, rope_step, qn_ready = sem("q_root_ready"), sem("q_step"), sem("rope_step"), sem("qn_ready")
        padded, conv_step, z_ready = sem("padded"), sem("conv_step"), sem("z_ready")
        z_stored = [sem(f"z_stored{i}") for i in range(2)]
        g_stored = [sem(f"g_stored{i}") for i in range(2)]
        NZ, NGT = 2 * HY_UNITS, 2 * G_UNITS
        ADA = 4 * D // UW

        with nc.Block() as block:
            @block.sync
            def _(sp):
                def load(u):
                    if u >= 2:
                        sp.wait_ge(w_lo_ready, u - 1)
                    c = unit_column(u)
                    sp.dma_start(w[:, u % 2], A["w_in"][0][:, c:c + UW].rearrange("(k p) n -> p k n", p=P))\
                      .then_inc(w_in[u % 2], 16)
                load(0)
                load(1)
                for i in range(NG):
                    w_ = A["q_norm"] if i < NH else A["k_norm"]
                    sp.dma_start(wrow[:, i, :], w_[0, :].partition_broadcast(P)).then_inc(small_in, 16)
                sp.dma_start(cos[:], A["rope_cos"].rearrange("(t p) d -> p t d", p=P)).then_inc(small_in, 16)
                sp.dma_start(sin[:], A["rope_sin"].rearrange("(t p) d -> p t d", p=P)).then_inc(small_in, 16)
                for u in range(UNITS):
                    if u + 2 < UNITS:
                        load(u + 2)
                    if u < ADA:
                        if u:
                            sp.wait_ge(acc_ready, u)
                        c = 2 * D + UW * u
                        sp.dma_start(ada[:], A["ada_w"][0][:, c:c + UW].rearrange("(k p) n -> p k n", p=P))\
                          .then_inc(ada_in, 16)
                    if QKV_UNITS <= u < QKV_UNITS + HY_UNITS:
                        for c in range(2):
                            i = 2 * (u - QKV_UNITS) + c
                            sp.wait_ge(z_ready, i + 1)
                            sp.dma_start(g["z_dram"][P * i:P * i + P, :], zs[:, i % 2, :]).then_inc(z_stored[i % 2], 16)
                for i in range(2):
                    sp.wait_ge(z_stored[i], 16 * (NZ // 2))

            @block.scalar
            def _(act):
                def high_part(u):
                    act.wait_ge(w_in[u % 2], 16 * (u // 2 + 1))
                    if u >= 2:
                        act.wait_ge(group_done, first[u - 1])
                    act.activation(w_hi[:, u % 2], w[:, u % 2], ACT.Copy).then_inc(w_hi_ready, 1)

                high_part(0)
                act.wait_ge(padded, 1)
                for u in range(UNITS):
                    if u + 1 < UNITS:
                        high_part(u + 1)
                    if u == QKV_UNITS + 1:
                        act.wait_ge(q_step, 1)
                        act.activation(root[:], ssq[:], ACT.Sqrt).then_inc(q_root, 1)
                    for i in range(first[u], first[u + 1]):
                        _, c, h = groups[i]
                        act.wait_ge(group_done, i + 1)
                        src = pz[:, i % BANKS, :]
                        if u < QKV_UNITS:
                            act.activation(qkv[:, c, UW * u:UW * u + UW], src[:, 0:UW], ACT.Copy).then_inc(evacuated, 1)
                        elif u < QKV_UNITS + HY_UNITS:
                            n = 2 * (u - QKV_UNITS) + c
                            if n:
                                act.wait_ge(z_ready, n)
                            act.activation(ub[:, 1 + 512 * h:513 + 512 * h], src, ACT.Copy).then_inc(evacuated, 1)
                        else:
                            n = 2 * (u - QKV_UNITS - HY_UNITS) + c
                            if n < 2 and h == 0:
                                act.wait_ge(z_stored[n % 2], 16 * (NZ // 2))
                            if n >= 2 and h == 0:
                                act.wait_ge(g_stored[n % 2], 16 * (n // 2))
                            act.activation(gs[:, n % 2, 512 * h:512 * h + 512], src, ACT.Sigmoid).then_inc(evacuated, 1)
                            if h == 1:
                                act.wait_ge(evacuated, i + 1)
                                act.dma_start(g["gate_dram"][P * n:P * n + P, :], gs[:, n % 2, :])\
                                   .then_inc(g_stored[n % 2], 16)
                for i in range(2):
                    act.wait_ge(g_stored[i], 16 * (NGT // 2))

            @block.vector
            def _(dve):
                def low_part(u):
                    dve.wait_ge(w_hi_ready, u + 1)
                    dve.tensor_tensor(w_lo[:, u % 2], w[:, u % 2], w_hi[:, u % 2].bitcast(F32), ALU.subtract)\
                       .then_inc(w_lo_ready, 1)

                def ada_part(m):
                    dve.wait_ge(ada_in, 16 * (m + 1))
                    if m >= 2:
                        dve.wait_ge(sums_done, m - 1)
                    a = acc[:, m % 2]
                    dve.tensor_scalar(a, ada[:, 0, :], sil[:, 0, 0:1], None, ALU.mult).then_inc(acc_step, 1)
                    for k in range(1, KD):
                        dve.wait_ge(acc_step, (KD - 1) * m + k)
                        dve.scalar_tensor_tensor(out=a, in0=ada[:, k, :], scalar=sil[:, 0, k:k + 1], in1=a,
                                                 op0=ALU.mult, op1=ALU.add)\
                           .then_inc(acc_step if k < KD - 1 else acc_ready, 1)

                def head_squares(i):
                    a = 0 if i < NT else NH
                    w_ = (NG - a) * HD
                    src = qkv[:, i, HD * a:HD * NG]
                    if i:
                        dve.wait_ge(ssq_ready, i + 1)
                    dve.tensor_tensor(sq[:, 0:w_], src, src, ALU.mult).then_inc(sq_ready, 1)
                    dve.wait_ge(sq_ready, i + 1)
                    dve.tensor_reduce(ssq[:, i, a:NG], sq[:, 0:w_].rearrange("p (h d) -> p h d", d=HD), AX, ALU.add)\
                       .then_inc(ssq_ready, 1)

                rope_steps = 0

                def norm_heads(i):
                    nonlocal rope_steps
                    x = qkv[:, i, 0:NG * HD].rearrange("p (h d) -> p h d", d=HD)
                    r_ = rstd[:, i, :].unsqueeze(2).broadcast_to([P, NG, HD])
                    if i:
                        dve.wait_ge(qn_ready, i)
                    if i < NT:
                        def pairs(t, spec):
                            return t[:, 0:NH].rearrange(spec, s=NKV, g=GRP)
                        dve.tensor_tensor(pairs(xn, "p (g s) d -> p s g d"), pairs(x, "p (s g) d -> p s g d"),
                                          pairs(r_, "p (s g) d -> p s g d"), ALU.mult)
                    dve.tensor_tensor(xn[:, NH:], x[:, NH:], r_[:, NH:], ALU.mult).then_inc(rope_step, 1)
                    rope_steps += 1
                    dve.wait_ge(rope_step, rope_steps)
                    if i >= NT:
                        dve.tensor_tensor(x[:, NH:], xn[:, NH:], wrow[:, NH:], ALU.mult).then_inc(qn_ready, 1)
                        return
                    dve.tensor_tensor(xn[:], xn[:], wrow[:], ALU.mult).then_inc(rope_step, 1)
                    rope_steps += 1
                    dve.wait_ge(rope_step, rope_steps)
                    dve.wait_ge(z_ready, min(2 * (i + 1), NZ))
                    c = cos[:, i, :].unsqueeze(1).broadcast_to([P, NG, ROT])
                    s_ = sin[:, i, :].unsqueeze(1).broadcast_to([P, NG, ROT])
                    even, odd = xn[:, :, 0:HD:2], xn[:, :, 1:HD:2]
                    for r, a, b in zip(rope, (even, odd, even, odd), (c, s_, s_, c)):
                        dve.tensor_tensor(r, a, b, ALU.mult).then_inc(rope_step, 1)
                    rope_steps += 4
                    dve.wait_ge(rope_step, rope_steps)
                    dve.tensor_tensor(x[:, :, 0:HD:2], rope[0], rope[1], ALU.subtract)
                    dve.tensor_tensor(x[:, :, 1:HD:2], rope[2], rope[3], ALU.add).then_inc(qn_ready, 1)

                dve.memset(ub[:], 0.0).then_inc(padded, 1)
                dve.memset(ssq[:], 1.0).then_inc(ssq_ready, 1)
                dve.wait_ge(ssq_ready, 1)
                low_part(0)
                for u in range(UNITS):
                    if u + 1 < UNITS:
                        low_part(u + 1)
                    if u < ADA:
                        ada_part(u)
                    if u == QKV_UNITS:
                        dve.wait_ge(small_in, 16 * (NG + 2))
                        dve.wait_ge(evacuated, first[QKV_UNITS])
                        for i in range(NTA):
                            head_squares(i)
                        dve.wait_ge(ssq_ready, NTA + 1)
                        dve.tensor_scalar(ssq[:], ssq[:], 1.0 / HD, EPS, ALU.mult, ALU.add).then_inc(q_step, 1)
                    if u == QKV_UNITS + 1:
                        inverse_root(dve, q_root, q_step, 1, ssq[:], root[:], rstd[:], tmp[:])
                    if QKV_UNITS < u <= QKV_UNITS + NTA:
                        norm_heads(u - QKV_UNITS - 1)
                    if not QKV_UNITS <= u < QKV_UNITS + HY_UNITS:
                        continue
                    for c in range(2):
                        n = 2 * (u - QKV_UNITS) + c
                        b = ub[:]
                        dve.wait_ge(evacuated, first[u] + 2 * c + 2)
                        if n >= 2:
                            dve.wait_ge(z_stored[n % 2], 16 * (n // 2))
                        if n:
                            dve.wait_ge(z_ready, n)
                        if n >= 2:
                            dve.wait_ge(qn_ready, min(u - QKV_UNITS, NT))
                        dve.tensor_scalar(t1, b[:, 1:L + 1], cols2[:, 12 + n:13 + n], cols2[:, 36 + n:37 + n],
                                          ALU.mult, ALU.add).then_inc(conv_step, 1)
                        dve.wait_ge(conv_step, 2 * n + 1)
                        dve.scalar_tensor_tensor(out=t1, in0=b[:, 0:L], scalar=cols2[:, n:n + 1], in1=t1,
                                                 op0=ALU.mult, op1=ALU.add).then_inc(conv_step, 1)
                        dve.wait_ge(conv_step, 2 * n + 2)
                        dve.scalar_tensor_tensor(out=zs[:, n % 2, :], in0=b[:, 2:L + 2], scalar=cols2[:, 24 + n:25 + n],
                                                 in1=t1, op0=ALU.mult, op1=ALU.add).then_inc(z_ready, 1)
                dve.wait_ge(sums_done, ADA)
                dve.tensor_tensor(mod[:, 16:48, 0], p_mod[:, 0:32], cols1[:, 16:48], ALU.add).then_inc(mod_ready, 1)
                dve.wait_ge(mod_ready, 1)
                dve.scalar_tensor_tensor(out=g["A2"][:], in0=mod[:, 32:40, 0], scalar=1.0, in1=cols1[:, 56:64],
                                         op0=ALU.add, op1=ALU.mult).then_inc(mod_ready, 1)
                for i in range(2 * KD):
                    if i >= 2:
                        dve.wait_ge(g_done, i - 1)
                    c = (16 if i < KD else 40) + i % KD
                    dve.tensor_scalar(diag[:, i % 2, :], ident[:], mod[:, c, 0:1], None, ALU.mult).then_inc(diag_ready, 1)
                    if i % 4 == 3:
                        row = g["g1row"] if i < KD else g["g2row"]
                        dve.wait_ge(g_done, i + 1)
                        q = i // 4
                        dve.tensor_copy(row[:, 512 * (q % 2):512 * (q % 2) + 512], p_g[:]).then_inc(g_copied, 1)

            @block.tensor
            def _(pe):
                def column_sums(m):
                    pe.wait_ge(acc_ready, m + 1)
                    for c in range(2):
                        mm = pe.matmul(p_mod[:, 2 * m + c:2 * m + c + 1], acc[:, m % 2, P * c:P * c + P], ones[:, 0:1],
                                       start=True, stop=True)
                    mm.then_inc(sums_done, 1)

                for u in range(UNITS):
                    if 1 <= u <= ADA:
                        column_sums(u - 1)
                    pe.wait_ge(w_lo_ready, u + 1)
                    b = u % 2
                    for i in range(first[u], first[u + 1]):
                        _, c, h = groups[i]
                        if i >= BANKS:
                            pe.wait_ge(evacuated, i - BANKS + 1)
                        for k in range(KD):
                            if h is None:
                                mm = three(pe, pz[:, i % BANKS, 0:UW],
                                           h_hi[:, k, P * c:P * c + P], h_lo[:, k, P * c:P * c + P],
                                           w_hi[:, b, k, :], w_lo[:, b, k, :], k == 0, k == KD - 1)
                            else:
                                mm = three(pe, pz[:, i % BANKS, :],
                                           w_hi[:, b, k, P * c:P * c + P], w_lo[:, b, k, P * c:P * c + P],
                                           h_hi[:, k, 512 * h:512 * h + 512], h_lo[:, k, 512 * h:512 * h + 512],
                                           k == 0, k == KD - 1)
                        mm.then_inc(group_done, 1)
                for i in range(2 * KD):
                    pe.wait_ge(diag_ready, i + 1)
                    if i >= 4 and i % 4 == 0:
                        pe.wait_ge(g_copied, i // 4)
                    pe.matmul(p_g[:, P * (i % 4):P * (i % 4) + P], ones[:], diag[:, i % 2, :], start=True, stop=True)\
                      .then_inc(g_done, 1)


def inverse_root(dve, act_root, step, at, v, root, r, tmp, roots=1):
    dve.wait_ge(act_root, roots)
    dve.reciprocal(r, root).then_inc(step, 1)
    dve.wait_ge(step, at + 1)
    dve.tensor_tensor(tmp, r, r, ALU.mult).then_inc(step, 1)
    dve.wait_ge(step, at + 2)
    dve.tensor_tensor(tmp, tmp, v, ALU.mult).then_inc(step, 1)
    dve.wait_ge(step, at + 3)
    dve.tensor_scalar(tmp, tmp, -0.5, 1.5, ALU.mult, ALU.add).then_inc(step, 1)
    dve.wait_ge(step, at + 4)
    dve.tensor_tensor(r, r, tmp, ALU.mult).then_inc(step, 1)
    dve.wait_ge(step, at + 5)


def attention(g):
    nc, sem, A = g["nc"], g["sem"], g["A"]
    qkv, ident, ones = g["qkv"], g["ident"], g["ones"]
    U = NT * NH
    G = NT * NKV
    SC = HD ** -0.5
    QB = 3
    TB = 3
    with ExitStack() as s:
        sb, ps = g["scope"](s)
        nsink = sb("nsink", [P, NH])
        q_hi, q_lo = (sb(n, [P, QB, NKV, GRP, P], F32R) for n in ("q_hi", "q_lo"))
        k_hi, k_lo = (sb(n, [P, LA], F32R) for n in ("k_hi", "k_lo"))
        v_hi, v_lo = (sb(n, [P, NTA, P], F32R) for n in ("v_hi", "v_lo"))
        negI, m_prev, m_next = (sb(n, [P, P], BF16) for n in ("negI", "m_prev", "m_next"))
        mx, nm, rs = (sb(n, [P, U]) for n in ("mx", "nm", "rs"))
        es0, es, r = (sb(n, [P, 2, GRP]) for n in ("es0", "es", "r_sum"))
        probs = sb("probs", [P, 3, 640])
        pT_hi, pT_lo = (sb(n, [P, 2, 5, GRP, P], F32R) for n in ("pT_hi", "pT_lo"))
        diag = sb("r_diag", [P, GRP, P])
        o_raw = sb("o_raw", [P, 2, 512])
        yb = sb("yb", [P, 2, 512])
        p_s = ps("p_s", [P, 2, 1024])
        p_t = ps("p_turned", [P, TB, 512])
        p_o = ps("p_o", [P, 512])
        p_r = p_o
        small_in, masks, mask_step = sem("sink_in"), sem("masks"), sem("mask_step")
        w_ready, v_hi_ready, v_lo_ready = sem("sink_ready"), sem("v_hi_ready"), sem("v_lo_ready")
        q_lo_zero = sem("q_lo_zero")
        turned, t_hi, t_lo = sem("tile_turned"), sem("turned_hi"), sem("turned_lo")
        s_done, max_ready, shift_ready, exp_ready = sem("s_done"), sem("max_ready"), sem("shift_ready"), sem("exp_ready")
        pv_done = sem("pv_done")
        es0_ready, es_ready, r_step = sem("es0_ready"), sem("es_ready"), sem("r_step")
        diag_ready, r_done, o_copied, yb_ready = sem("r_diag_ready"), sem("r_done"), sem("o_copied"), sem("yb_ready")
        y_stored = [sem(f"y_stored{i}") for i in range(2)]
        ORDER = [NT, NT + 1] + list(range(NT))

        def blocks(n):
            return list(range(max(0, n - 1), min(NT - 1, n + 1) + 1))

        def window(n):
            return 512 - P * len(blocks(n)), 512

        def chunks(n):
            a = window(n)[0]
            return [(a + P * i, w) for i, w in enumerate(blocks(n))] + [(512, NT), (512 + P, NT + 1)]

        def at_unit(u):
            n, h = divmod(u, NH)
            return n + 4 if h == 2 and n + 4 < NTA else None

        banks = []

        def add_tile(i):
            banks.extend([("q", i), ("k", i)] if ORDER[i] < NT else [("k", i)])

        for i in range(4):
            add_tile(i)
        for u in range(U):
            if (i := at_unit(u)) is not None:
                add_tile(i)
            banks.extend([("w", u), ("c", u)])
        n_bank = {b: n for n, b in enumerate(banks)}

        def parts(u):
            c = len(blocks(u // NH))
            return ("w", slice(0, c)), ("c", slice(c, c + 2))

        with nc.Block() as block:
            @block.sync
            def _(sp):
                sp.dma_start(nsink[:], A["attn_sink"][0, :].partition_broadcast(P)).then_inc(small_in, 16)
                for G_ in range(G):
                    n, kv = divmod(G_, NKV)
                    sp.wait_ge(yb_ready, G_ + 1)
                    at = slice(HD * kv, HD * kv + HD)
                    dst = g["yb_dram"][HD * GRP * kv:HD * GRP * (kv + 1), P * n:P * n + P]
                    sp.dma_start(dst.rearrange("(j d) t -> d j t", d=HD),
                                 yb[at, G_ % 2].rearrange("d (j t) -> d j t", j=GRP)).then_inc(y_stored[G_ % 2], 16)
                for i in range(2):
                    sp.wait_ge(y_stored[i], 16 * (G // 2))

            @block.gpsimd
            def _(pool):
                pool.memset(q_hi[:].rearrange("p b s j t -> p (b s j t)").bitcast(F32), 0.0).then_inc(mask_step, 1)
                pool.memset(negI[:], 0.0).then_inc(mask_step, 1)
                pool.memset(m_prev[:], 0.0).then_inc(mask_step, 1)
                pool.memset(m_next[:], 0.0).then_inc(mask_step, 1)
                pool.wait_ge(mask_step, 4)
                pool.affine_select(out=negI[:], in_=negI[:], compare_op=ALU.not_equal, fill=NEG, base=0,
                                   pattern=[[-1, P]], channel_multiplier=1).then_inc(masks, 1)
                pool.affine_select(out=m_prev[:], in_=m_prev[:], compare_op=ALU.is_ge, fill=1.0, base=0,
                                   pattern=[[1, P]], channel_multiplier=-1).then_inc(masks, 1)
                pool.affine_select(out=m_next[:], in_=m_next[:], compare_op=ALU.is_ge, fill=1.0, base=0,
                                   pattern=[[-1, P]], channel_multiplier=1).then_inc(masks, 1)

            def key_columns(t):
                return slice(P * t, P * t + P)

            @block.scalar
            def _(act):
                def high_qk(i):
                    t = ORDER[i]
                    if t < NT:
                        n = n_bank[("q", i)]
                        act.wait_ge(turned, n + 1)
                        if t >= QB:
                            act.wait_ge(s_done, NH * (t - QB + 1))
                        for kv in range(NKV):
                            at = slice(HD * kv, HD * kv + HD)
                            ins = act.activation(q_hi[at, t % QB, kv],
                                                 p_t[at, n % TB].rearrange("p (j t) -> p j t", j=GRP), ACT.Copy)
                        ins.then_inc(t_hi, 1)
                    n = n_bank[("k", i)]
                    act.wait_ge(turned, n + 1)
                    act.activation(k_hi[:, key_columns(t)], p_t[:, n % TB, 0:P], ACT.Copy).then_inc(t_hi, 1)

                act.activation(v_hi[:], qkv[:, :, HD * NG:], ACT.Copy).then_inc(v_hi_ready, 1)
                for i in range(4):
                    if i == 2:
                        act.wait_ge(mask_step, 4)
                    high_qk(i)

                def high_probs(u):
                    h = u % NH
                    if u >= 2 * GRP and u % GRP == 0:
                        act.wait_ge(pv_done, u // GRP - 1)
                    for part, cs in parts(u):
                        n = n_bank[(part, u)]
                        act.wait_ge(turned, n + 1)
                        act.activation(pT_hi[:, (u // GRP) % 2, cs, h % GRP, :],
                                       p_t[:, n % TB, 0:P * (cs.stop - cs.start)].rearrange("p (c t) -> p c t", t=P),
                                       ACT.Copy).then_inc(t_hi, 1)

                def sink_term(G_):
                    act.wait_ge(es0_ready, G_ + 1)
                    act.activation(es[:, G_ % 2], es0[:, G_ % 2], ACT.Exp).then_inc(es_ready, 1)

                def copy_output(G_):
                    at = slice(HD * (G_ % NKV), HD * (G_ % NKV) + HD)
                    act.wait_ge(pv_done, G_ + 1)
                    if G_ >= 2:
                        act.wait_ge(yb_ready, G_ - 1)
                    act.activation(o_raw[at, G_ % 2], p_o[at, :], ACT.Copy).then_inc(o_copied, 1)

                for u in range(U):
                    n = u // NH
                    a = window(n)[0]
                    if u:
                        high_probs(u - 1)
                    act.wait_ge(shift_ready, u + 1)
                    if u >= 3:
                        act.wait_ge(turned, n_bank[("c", u - 3)] + 1)
                    act.activation(probs[:, u % 3, 0:768 - a], p_s[:, u % 2, a:768], ACT.Exp, bias=nm[:, u:u + 1],
                                   scale=SC, accum_out=rs[:, u:u + 1]).then_inc(exp_ready, 1)
                    if (i := at_unit(u)) is not None:
                        high_qk(i)
                    if u % GRP == GRP - 1:
                        sink_term(u // GRP)
                    if u % GRP == 1 and u > GRP:
                        copy_output(u // GRP - 1)
                high_probs(U - 1)
                copy_output(G - 1)

            @block.vector
            def _(dve):
                dve.memset(q_lo[:].rearrange("p b s j t -> p (b s j t)").bitcast(F32), 0.0).then_inc(q_lo_zero, 1)
                dve.wait_ge(small_in, 16)
                dve.tensor_scalar(nsink[:], nsink[:], -1.0, None, ALU.mult).then_inc(w_ready, 1)
                dve.wait_ge(v_hi_ready, 1)
                dve.tensor_tensor(v_lo[:], qkv[:, :, HD * NG:], v_hi[:].bitcast(F32), ALU.subtract).then_inc(v_lo_ready, 1)
                dve.wait_ge(q_lo_zero, 1)

                def low_qk(i):
                    t = ORDER[i]
                    if t < NT:
                        n = n_bank[("q", i)]
                        dve.wait_ge(t_hi, n + 1)
                        for kv in range(NKV):
                            at = slice(HD * kv, HD * kv + HD)
                            ins = dve.tensor_tensor(q_lo[at, t % QB, kv],
                                                    p_t[at, n % TB].rearrange("p (j t) -> p j t", j=GRP),
                                                    q_hi[at, t % QB, kv].bitcast(F32), ALU.subtract)
                        ins.then_inc(t_lo, 1)
                    n = n_bank[("k", i)]
                    dve.wait_ge(t_hi, n + 1)
                    dve.tensor_tensor(k_lo[:, key_columns(t)], p_t[:, n % TB, 0:P],
                                      k_hi[:, key_columns(t)].bitcast(F32), ALU.subtract).then_inc(t_lo, 1)

                for i in range(4):
                    low_qk(i)
                dve.wait_ge(w_ready, 1)

                def low_probs(u):
                    h = u % NH
                    for part, cs in parts(u):
                        n = n_bank[(part, u)]
                        dve.wait_ge(t_hi, n + 1)
                        dve.tensor_tensor(pT_lo[:, (u // GRP) % 2, cs, h % GRP, :],
                                          p_t[:, n % TB, 0:P * (cs.stop - cs.start)].rearrange("p (c t) -> p c t", t=P),
                                          pT_hi[:, (u // GRP) % 2, cs, h % GRP, :].bitcast(F32),
                                          ALU.subtract).then_inc(t_lo, 1)

                def divide_1(G_):
                    dve.wait_ge(es_ready, G_ + 1)
                    dve.tensor_tensor(r[:, G_ % 2], rs[:, GRP * G_:GRP * G_ + GRP], es[:, G_ % 2], ALU.add).then_inc(r_step, 1)
                    dve.wait_ge(r_step, 2 * G_ + 1)
                    dve.reciprocal(r[:, G_ % 2], r[:, G_ % 2]).then_inc(r_step, 1)
                    dve.wait_ge(r_step, 2 * G_ + 2)
                    if G_:
                        dve.wait_ge(r_done, G_)
                    dve.tensor_tensor(diag[:], ident[:].unsqueeze(1).broadcast_to([P, GRP, P]),
                                      r[:, G_ % 2].unsqueeze(2).broadcast_to([P, GRP, P]), ALU.mult).then_inc(diag_ready, 1)

                def divide_2(G_):
                    at = slice(HD * (G_ % NKV), HD * (G_ % NKV) + HD)
                    dve.wait_ge(r_done, G_ + 1)
                    dve.wait_ge(o_copied, G_ + 1)
                    if G_ >= 2:
                        dve.wait_ge(y_stored[G_ % 2], 16 * (G_ // 2))
                    dve.tensor_tensor(yb[at, G_ % 2], o_raw[at, G_ % 2], p_r[at, :], ALU.mult).then_inc(yb_ready, 1)

                def shift(u):
                    n, h = divmod(u, NH)
                    dve.wait_ge(s_done, u + 1)
                    dve.reduce_max(mx[:, u:u + 1], p_s[:, u % 2, window(n)[0]:768], AX).then_inc(max_ready, 1)
                    dve.wait_ge(max_ready, u + 1)
                    dve.tensor_scalar(nm[:, u:u + 1], mx[:, u:u + 1], -SC, nsink[:, h:h + 1], ALU.mult, ALU.min)\
                       .then_inc(shift_ready, 1)

                shift(0)
                for u in range(U):
                    if u:
                        low_probs(u - 1)
                    if (i := at_unit(u)) is not None:
                        low_qk(i)
                    if u + 1 < U:
                        shift(u + 1)
                    if u % GRP == GRP - 1:
                        G_ = u // GRP
                        at = GRP * (G_ % NKV)
                        dve.wait_ge(shift_ready, u + 1)
                        if G_ >= 2:
                            dve.wait_ge(es_ready, G_ - 1)
                        dve.tensor_tensor(es0[:, G_ % 2], nm[:, GRP * G_:GRP * G_ + GRP], nsink[:, at:at + GRP],
                                          ALU.subtract).then_inc(es0_ready, 1)
                    if u % GRP == 1 and u > GRP:
                        divide_1(u // GRP - 1)
                    if u % GRP == 3 and u > GRP:
                        divide_2(u // GRP - 1)
                low_probs(U - 1)
                divide_1(G - 1)
                divide_2(G - 1)

            @block.tensor
            def _(pe):
                def free_bank(n):
                    if n >= TB:
                        pe.wait_ge(t_lo, n - TB + 1)
                    return p_t[:, n % TB]

                def turn_qk(i):
                    t = ORDER[i]
                    q = qkv[:, t, 0:HD * NG]
                    if t < NT:
                        bank = free_bank(n_bank[("q", i)])
                        for j in range(GRP):
                            mm = pe.transpose(bank[:, P * j:P * j + P], q[:, P * j:P * j + P], ident[:])
                        mm.then_inc(turned, 1)
                    bank = free_bank(n_bank[("k", i)])
                    pe.transpose(bank[:, 0:P], q[:, 512:640], ident[:]).then_inc(turned, 1)

                for i in range(4):
                    turn_qk(i)
                pe.wait_ge(masks, 3)

                def scores(u):
                    n, h = divmod(u, NH)
                    kv, j = divmod(h, GRP)
                    bank, b, (a, _) = p_s[:, u % 2], blocks(n), window(n)
                    qh, ql = q_hi[:, n % QB, kv, j, :], q_lo[:, n % QB, kv, j, :]
                    if h == 0:
                        pe.wait_ge(t_lo, n_bank[("k", min(n + 3, NTA - 1))] + 1)
                    if u >= 2:
                        pe.wait_ge(exp_ready, u - 1)
                    ks = slice(P * b[0], P * b[-1] + P)
                    three(pe, bank[:, a:512], qh, ql, k_hi[:, ks], k_lo[:, ks], True, False)
                    if b[0] < n:
                        pe.matmul(bank[:, a:a + P], negI[:], m_prev[:], start=False, stop=b[-1] == n)
                    if b[-1] > n:
                        pe.matmul(bank[:, 512 - P:512], negI[:], m_next[:], start=False, stop=True)
                    three(pe, bank[:, 512:768], qh, ql, k_hi[:, L:], k_lo[:, L:], True, True).then_inc(s_done, 1)

                def transpose_probs(u):
                    a = window(u // NH)[0]
                    pe.wait_ge(exp_ready, u + 1)
                    for part, cs in parts(u):
                        bank = free_bank(n_bank[(part, u)])
                        for i, (c, _) in enumerate(chunks(u // NH)[cs]):
                            mm = pe.transpose(bank[:, P * i:P * i + P], probs[:, u % 3, c - a:c - a + P], ident[:])
                        mm.then_inc(turned, 1)

                def values(G_):
                    n = G_ // NKV
                    pe.wait_ge(t_lo, n_bank[("c", GRP * G_ + GRP - 1)] + 1)
                    if G_ == 0:
                        pe.wait_ge(v_lo_ready, 1)
                    else:
                        pe.wait_ge(yb_ready, G_)
                    cs = chunks(n)
                    for i, (_, t) in enumerate(cs):
                        mm = three(pe, p_o[:], v_hi[:, t, :], v_lo[:, t, :],
                                   pT_hi[:, G_ % 2, i].rearrange("p j t -> p (j t)"),
                                   pT_lo[:, G_ % 2, i].rearrange("p j t -> p (j t)"), i == 0, i == len(cs) - 1)
                    mm.then_inc(pv_done, 1)

                def spread(G_):
                    pe.wait_ge(diag_ready, G_ + 1)
                    pe.wait_ge(o_copied, G_ + 1)
                    pe.matmul(p_r[:], ones[:], diag[:].rearrange("p j t -> p (j t)"), start=True, stop=True)\
                      .then_inc(r_done, 1)

                scores(0)
                for u in range(U):
                    if u + 1 < U:
                        scores(u + 1)
                    if (i := at_unit(u)) is not None:
                        turn_qk(i)
                    transpose_probs(u)
                    if u % GRP == 0 and u:
                        values(u // GRP - 1)
                    if u % GRP == 2 and u > GRP:
                        spread(u // GRP - 1)
                values(G - 1)
                spread(G - 1)


def hyena(g):
    nc, sem, A = g["nc"], g["sem"], g["A"]
    ident, cols2, ya = g["ident"], g["cols2"], g["ya"]
    T = L // P
    HT = T // 2
    FC = L // 2 // P
    ORD = 2
    TWO_PI = 2.0 * np.pi
    C1 = 6.28125
    C2 = TWO_PI - C1
    MAGIC = 1.5 * 2.0 ** 23
    with ExitStack() as outer:
        sbo, _ = g["scope"](outer)
        hid = sbo("hid", [FH, L])
        fpm = sbo("fpm", [FH, ORD, 2, HY])
        with ExitStack() as s:
            sb, ps = g["scope"](s)
            feat = sb("feat", [EMB, L])
            w1, w2, w3 = sb("fw1", [EMB, FH]), sb("fw2", [FH, FH]), sb("fw3", [FH, FH])
            vec = sb("fvec", [FH, 4])
            fout = sb("fout", [FH, ORD, 2, HY])
            un, kn = sb("un", [FH, L]), sb("kn", [FH, L])
            p_f = ps("p_f", [FH, 2, 512])
            f_in, fz_ready, f_step, sin_ready = sem("f_in"), sem("fz_ready"), sem("f_step"), sem("sin_ready")
            with nc.Block() as block:
                @block.sync
                def _(sp):
                    sp.dma_start(feat[:], A["feat"]).then_inc(f_in, 16)
                    for t, n in ((w1, "filt_w1"), (w2, "filt_w2"), (w3, "filt_w3")):
                        sp.dma_start(t[:], A[n][0]).then_inc(f_in, 16)
                    for i, n in enumerate(("filt_b1", "filt_b2", "filt_b3", "filt_freq")):
                        sp.dma_start(vec[:, i:i + 1], A[n].rearrange("o h -> h o")).then_inc(f_in, 16)
                    sp.dma_start(fout[:].rearrange("h a b c -> h (a b c)"), A["filt_out"][0]).then_inc(f_in, 16)

                @block.tensor
                def _(pe):
                    pe.wait_ge(f_in, 16 * 9)
                    for layer, (w, src) in enumerate(((w1, feat), (w2, hid), (w3, hid))):
                        for h in range(2):
                            if layer:
                                pe.wait_ge(sin_ready, 2 * (layer - 1) + h + 1)
                            pe.matmul(p_f[:, h, :], w[:], src[:, 512 * h:512 * h + 512], start=True, stop=True)\
                              .then_inc(fz_ready, 1)

                @block.vector
                def _(dve):
                    dve.wait_ge(f_in, 16 * 9)
                    dve.tensor_tensor(fpm[:, :, 0, :], fout[:, :, 0, :], fout[:, :, 1, :], ALU.add)
                    dve.tensor_tensor(fpm[:, :, 1, :], fout[:, :, 0, :], fout[:, :, 1, :], ALU.subtract)
                    n = 0
                    for layer in range(3):
                        for h in range(2):
                            u, k = un[:, 512 * h:512 * h + 512], kn[:, 512 * h:512 * h + 512]
                            dve.wait_ge(fz_ready, 2 * layer + h + 1)
                            if layer:
                                dve.wait_ge(sin_ready, 2 * (layer - 1) + h + 1)
                            for op in (
                                lambda: dve.tensor_scalar(u, p_f[:, h, :], vec[:, layer:layer + 1], vec[:, 3:4],
                                                          ALU.add, ALU.mult),
                                lambda: dve.tensor_scalar(k, u, 1.0 / TWO_PI, MAGIC, ALU.mult, ALU.add),
                                lambda: dve.tensor_scalar(k, k, -MAGIC, None, ALU.add),
                                lambda: dve.scalar_tensor_tensor(out=u, in0=k, scalar=-C1, in1=u,
                                                                 op0=ALU.mult, op1=ALU.add),
                                lambda: dve.scalar_tensor_tensor(out=u, in0=k, scalar=-C2, in1=u,
                                                                 op0=ALU.mult, op1=ALU.add),
                                lambda: dve.tensor_scalar(u, u, 3.1415925, -3.1415925, ALU.min, ALU.max),
                            ):
                                op().then_inc(f_step, 1)
                                n += 1
                                dve.wait_ge(f_step, n)

                @block.scalar
                def _(act):
                    for i in range(6):
                        half = slice(512 * (i % 2), 512 * (i % 2) + 512)
                        act.wait_ge(f_step, 6 * (i + 1))
                        act.activation(hid[:, half], un[:, half], ACT.Sin).then_inc(sin_ready, 1)

        with ExitStack() as s:
            sb, ps = g["scope"](s)
            four = sb("four", [P, 4, FC, 512])
            pm = sb("pm", [P, 2, T, HY])
            ut = sb("ut", [P, T, HY])
            spec = sb("spec", [P, 4, FC, HY])
            gate = sb("gate_in", [P, 2, L])
            decay = sb("decay_in", [P, 2, HY])
            cp = sb("cp", [P, 4, HY])
            KX = sb("kx", [P, 8, HY])
            Y = sb("yspec", [P, 4, HY])
            t_a, t_b = sb("t_a", [P, 2, HY]), sb("t_b", [P, 2, HY])
            pj = ps("p_j", [P, 4, 2, 512])
            v_in, four_in, four2_in = sem("v_in"), sem("four_in"), sem("four2_in")
            four_back_in = sem("four_back_in")
            decay_in = [sem(f"decay_in{i}") for i in range(2)]
            gate_in = [sem(f"gate_in{i}") for i in range(2)]
            job, a_done, v_done = sem("job"), sem("act_read"), sem("dve_read")
            step = sem("spectral_step")
            jobs = []
            EARLY = T // 2
            for o in range(ORD):
                jobs += [("filter", o, c) for c in range(EARLY if o else 0, T)]
                jobs += [("turn", o, c) for c in range(HT)]
                jobs += [(k, o, c) for c in range(FC) for k in ("Kc", "Ks", "Xc", "Xs")]
                if o + 1 < ORD:
                    jobs += [("filter", o + 1, c) for c in range(EARLY)]
                jobs += [("back", o, c) for c in range(NCH)]
            n_job = {j: i for i, j in enumerate(jobs)}
            acts = {j: i + 1 for i, j in enumerate([j for j in jobs if j[0] not in ("filter", "back")])}
            dves = {j: i + 1 for i, j in enumerate([j for j in jobs if j[0] != "turn"])}

            def spectral_steps(o):
                return (o + 1) * (3 + FC * (4 + 10)) + o * 2 * NCH

            def free(pe, i):
                if i >= 4:
                    j = jobs[i - 4]
                    pe.wait_ge(*((a_done, acts[j]) if j[0] == "turn" else (v_done, dves[j])))

            with nc.Block() as block:
                @block.sync
                def _(sp):
                    def load_decay(i):
                        c = i % T
                        if i >= 2:
                            sp.wait_ge(v_done, dves[("filter", (i - 2) // T, (i - 2) % T)])
                        sp.dma_start(decay[:, i % 2], A["decay"][P * c:P * c + P, :]).then_inc(decay_in[i % 2], 16)

                    def load_gate(i):
                        o, c = divmod(i, NCH)
                        if i >= 2:
                            sp.wait_ge(v_done, dves[("back", (i - 2) // NCH, (i - 2) % NCH)])
                        at = HY * (o + 1) + P * c
                        sp.dma_start(gate[:, i % 2], g["z_dram"][at:at + P, :]).then_inc(gate_in[i % 2], 16)

                    def load_fourier(rows, s_):
                        for to, m in rows:
                            sp.dma_start(four[:, to], A["fourier"][m].rearrange("(c p) n -> p c n", p=P)).then_inc(s_, 16)

                    load_decay(0)
                    load_decay(1)
                    sp.dma_start(ya[:], g["z_dram"][0:HY, :].rearrange("(c p) t -> p c t", p=P)).then_inc(v_in, 16)
                    load_fourier(((0, 0), (1, 1), (2, 2), (3, 3)), four_in)
                    load_gate(0)
                    load_gate(1)
                    for c in range(2, T):
                        load_decay(c)
                    for o in range(ORD):
                        sp.wait_ge(job, n_job[("Xs", o, FC - 1)] + 1)
                        load_fourier(((0, 4), (2, 5)), four_back_in)
                        if o + 1 < ORD:
                            for c in range(EARLY):
                                load_decay((o + 1) * T + c)
                        for c in range(NCH):
                            if o * NCH + c >= 2:
                                load_gate(o * NCH + c)
                        if o + 1 < ORD:
                            sp.wait_ge(job, n_job[("back", o, NCH - 1)] + 1)
                            load_fourier(((0, 0), (2, 2)), four2_in)
                            for c in range(EARLY, T):
                                load_decay((o + 1) * T + c)

                @block.scalar
                def _(act):
                    for i, j in enumerate(jobs):
                        kind, o, c = j
                        if kind in ("filter", "back"):
                            continue
                        act.wait_ge(job, i + 1)
                        b = pj[:, i % 4]
                        if kind == "turn":
                            act.activation(ut[:, c:T:HT, :], b, ACT.Copy).then_inc(a_done, 1)
                        else:
                            q = ("Kc", "Ks", "Xc", "Xs").index(kind)
                            if o or c:
                                before = (kind, o, c - 1) if c else (kind, o - 1, FC - 1)
                                act.wait_ge(v_done, dves[before])
                            act.activation(cp[:, q], b[:, 0, :], ACT.Copy).then_inc(a_done, 1)

                @block.vector
                def _(dve):
                    steps = 0

                    def done(*instructions):
                        nonlocal steps
                        for i in instructions:
                            i.then_inc(step, 1)
                        steps += len(instructions)
                        dve.wait_ge(step, steps)

                    def tt(out, a, b, op):
                        return dve.tensor_tensor(out, a, b, op)

                    for i, j in enumerate(jobs):
                        kind, o, c = j
                        b = pj[:, i % 4]
                        if kind == "filter":
                            n = o * T + c
                            dve.wait_ge(job, i + 1)
                            dve.wait_ge(decay_in[n % 2], 16 * (n // 2 + 1))
                            if c == 0:
                                done(tt(pm[:, 0, c], b[:, 0], decay[:, n % 2], ALU.mult),
                                     tt(pm[:, 1, c], b[:, 1], decay[:, n % 2], ALU.mult))
                                done(tt(t_a[0:1, 0], pm[0:1, 0, 0], pm[0:1, 1, 0], ALU.add))
                                dve.tensor_scalar(pm[0:1, 0, 0], t_a[0:1, 0], 0.5, None, ALU.mult).then_inc(v_done, 1)
                            else:
                                tt(pm[:, 0, c], b[:, 0], decay[:, n % 2], ALU.mult)
                                tt(pm[:, 1, c], b[:, 1], decay[:, n % 2], ALU.mult).then_inc(v_done, 1)
                        elif kind == "back":
                            n = o * NCH + c
                            dve.wait_ge(job, i + 1)
                            dve.wait_ge(gate_in[n % 2], 16 * (n // 2 + 1))
                            bias = cols2[:, 48 + 4 * o + c:49 + 4 * o + c]
                            y = [ya[:, c, q:L:2] for q in range(2)]
                            done(*[dve.scalar_tensor_tensor(out=y[q], in0=y[q], scalar=bias, in1=b[:, q],
                                                            op0=ALU.mult, op1=ALU.add) for q in range(2)])
                            tt(ya[:, c, :], ya[:, c, :], gate[:, n % 2, :], ALU.mult).then_inc(v_done, 1)
                        elif kind in ("Kc", "Ks", "Xc", "Xs"):
                            q = ("Kc", "Ks", "Xc", "Xs").index(kind)
                            dve.wait_ge(a_done, acts[j])
                            even, odd = cp[:, q], b[:, 1]
                            tt(KX[:, 2 * q], even, odd, ALU.add).then_inc(step, 1)
                            if kind[1] == "c":
                                tt(KX[:, 2 * q + 1], even, odd, ALU.subtract).then_inc(v_done, 1)
                            else:
                                tt(KX[:, 2 * q + 1], odd, even, ALU.subtract).then_inc(v_done, 1)
                            steps += 1
                            if kind == "Xs":
                                dve.wait_ge(step, steps)
                                dve.wait_ge(v_done, dves[j])
                                kr, ki, xr, xi = (KX[:, 2 * z:2 * z + 2] for z in range(4))
                                yr, yi = Y[:, 0:2], Y[:, 2:4]
                                done(tt(t_a[:], xr, kr, ALU.mult), tt(t_b[:], xi, ki, ALU.mult))
                                done(tt(yr, t_a[:], t_b[:], ALU.subtract))
                                done(tt(t_a[:], xr, ki, ALU.mult), tt(t_b[:], xi, kr, ALU.mult))
                                done(tt(yi, t_a[:], t_b[:], ALU.add))
                                done(tt(spec[:, 0, c], Y[:, 0], Y[:, 1], ALU.add),
                                     tt(spec[:, 1, c], Y[:, 2], Y[:, 3], ALU.subtract),
                                     tt(spec[:, 2, c], Y[:, 0], Y[:, 1], ALU.subtract),
                                     tt(spec[:, 3, c], Y[:, 2], Y[:, 3], ALU.add))

                @block.tensor
                def _(pe):
                    for i, j in enumerate(jobs):
                        kind, o, c = j
                        b = pj[:, i % 4]
                        free(pe, i)
                        if kind == "filter":
                            for m in range(2):
                                mm = pe.matmul(b[:, m], hid[:, P * c:P * c + P], fpm[:, o, m, :], start=True, stop=True)
                        elif kind == "turn":
                            if c == 0:
                                if o == 0:
                                    pe.wait_ge(v_in, 16)
                                else:
                                    pe.wait_ge(v_done, dves[("back", o - 1, NCH - 1)])
                            for m in range(2):
                                at = 2 * P * c + m
                                for h in range(NCH):
                                    mm = pe.transpose(b[:, m, P * h:P * h + P], ya[:, h, at:at + 2 * P - 1:2], ident[:])
                        elif kind == "back":
                            if c == 0:
                                pe.wait_ge(four_back_in, 32 * (o + 1))
                                pe.wait_ge(step, spectral_steps(o))
                            for m in range(2):
                                for z in range(2):
                                    for f in range(FC):
                                        mm = pe.matmul(b[:, m], spec[:, 2 * m + z, f, P * c:P * c + P],
                                                       four[:, 2 * z + m, f, :], start=z == 0 and f == 0,
                                                       stop=z == 1 and f == FC - 1)
                        else:
                            if c == 0 and kind == "Kc":
                                if o == 0:
                                    pe.wait_ge(four_in, 64)
                                else:
                                    pe.wait_ge(four2_in, 32 * o)
                                pe.wait_ge(v_done, dves[("filter", o, T - 1)])
                            if c == 0 and kind == "Xc":
                                pe.wait_ge(a_done, acts[("turn", o, HT - 1)])
                            z = int(kind[1] == "s")
                            for m in range(2):
                                src = pm[:, z] if kind[0] == "K" else ut
                                for t in range(HT):
                                    mm = pe.matmul(b[:, m], four[:, 2 * z + m, t, P * c:P * c + P],
                                                   src[:, HT * m + t, :], start=t == 0, stop=t == HT - 1)
                        mm.then_inc(job, 1)


def merge(g):
    nc, sem, A = g["nc"], g["sem"], g["A"]
    ya, ident, mod, A2, ring = g["ya"], g["ident"], g["mod"], g["A2"], g["ring"]
    XB = 3

    def slots(a, b):
        return ring[:, a:b].rearrange("p s n -> p (s n)").rearrange("p (k n) -> p k n", n=D)

    with ExitStack() as s:
        sb, ps = g["scope"](s)
        wa, wb, mT, wo = slots(0, 2), slots(2, 4), slots(4, 8), slots(8, 12)
        yb = sb("yb_in", [P, NCH, L])
        gates = sb("gates_in", [P, 2, 2, 512])
        ta, tb = sb("m_a", [P, 2, 512]), sb("m_b", [P, 2, 512])
        x = sb("x_res", [P, 2, D])
        xnew = sb("x_new", [P, XB, D])
        xn = sb("x_normed", [P, 2, D])
        junk = sb("squares", [P, D])
        ss, rt, rs, tmp = (sb(n, [P, NT]) for n in ("ss2", "rt2", "rs2", "tmp2"))
        router = sb("router_w", [P, KD, NE])
        h2 = sb("h2", [P, 2, KD, P])
        lg, ex = sb("lg", [P, NT, NE]), sb("ex", [P, NT, NE])
        mxl, sm = sb("mxl", [P, NT]), sb("sml", [P, NT])
        pj = ps("p_m", [P, 4, 2, 512])
        a_in, b_in, o_in, r_in = sem("wa_in"), sem("wb_in"), sem("wo_in"), sem("router_in")
        gates_in = [sem(f"gates_in{i}") for i in range(2)]
        xr_in = [sem(f"xr_in{i}") for i in range(2)]
        job, read = sem("m_job"), sem("m_read")
        mul, mt_ready = sem("m_mul"), sem("mt_ready")
        xnew_ready, sq_ready = sem("xnew_ready"), sem("sq2_ready")
        v_step, rt_ready, xn_ready = sem("v2_step"), sem("rt2_ready"), sem("xn2_ready")
        h_ready = sem("h2_ready")
        sm_step, exp_done = sem("sm_step"), sem("ex_ready")
        aff_t = sem("aff_t")
        x_stored = [sem(f"x_stored{i}") for i in range(XB)]
        xn_stored = [sem(f"xn_stored{i}") for i in range(2)]
        M = 2 * KD
        jobs = [("m", i) for i in range(M)]
        for t in range(NT):
            jobs.append(("o", t))
            if t >= 2:
                jobs.append(("l", t - 2))
            if t >= 1:
                jobs.append(("h", t - 1))
        jobs += [("l", NT - 2), ("h", NT - 1), ("l", NT - 1)]
        n_job = {j: i + 1 for i, j in enumerate(jobs)}
        logit_bank = pj[:, 3, 0, 0:NT * NE].rearrange("p (t e) -> p t e", e=NE)

        with nc.Block() as block:
            @block.sync
            def _(sp):
                sp.dma_start(wa, A["w_branch_a"][0].rearrange("(c p) n -> p c n", p=P)).then_inc(a_in, 16)
                sp.dma_start(yb[:], g["yb_dram"].rearrange("(c p) t -> p c t", p=P)).then_inc(b_in, 16)
                sp.dma_start(wb, A["w_branch_b"][0].rearrange("(c p) n -> p c n", p=P)).then_inc(b_in, 16)
                for i in range(M):
                    if i >= 2:
                        sp.wait_ge(mt_ready, i - 1)
                    j, h = divmod(i, 2)
                    sp.dma_start(gates[:, i % 2], g["gate_dram"][:, 512 * h:512 * h + 512]
                                 .rearrange("(v c p) t -> c p v t", v=2, p=P)[j]).then_inc(gates_in[i % 2], 16)
                    if i == 1:
                        sp.dma_start(wo, A["w_out"][0].rearrange("(c p) n -> p c n", p=P)).then_inc(o_in, 16)
                        sp.dma_start(router[:], A["router"][0].rearrange("(c p) n -> p c n", p=P)).then_inc(r_in, 16)
                for t in range(NT):
                    if t >= 2:
                        sp.wait_ge(xnew_ready, t - 1)
                    sp.dma_start(x[:, t % 2], A["x"][0, P * t:P * t + P, :]).then_inc(xr_in[t % 2], 16)
                    if t == 1:
                        sp.wait_ge(job, n_job[("m", M - 1)])
                        for i in range(4):
                            load_unit(sp, g, 0, i)
                    if t >= 1:
                        sp.wait_ge(xnew_ready, t)
                        sp.dma_start(g["out"][0, P * (t - 1):P * t, :], xnew[:, (t - 1) % XB, :])\
                          .then_inc(x_stored[(t - 1) % XB], 16)
                sp.wait_ge(job, n_job[("o", NT - 1)])
                sp.wait_ge(xnew_ready, NT)
                sp.dma_start(g["out"][0, L - P:L, :], xnew[:, (NT - 1) % XB, :]).then_inc(x_stored[(NT - 1) % XB], 16)
                for i in range(4, RAW):
                    load_unit(sp, g, 0, i)
                for i in range(XB):
                    sp.wait_ge(x_stored[i], 16 * len(range(i, NT, XB)))

            @block.tensor
            def _(pe):
                pe.wait_ge(a_in, 16)
                for kind, t in jobs:
                    if kind == "m":
                        j, h = divmod(t, 2)
                        if t >= 4:
                            pe.wait_ge(read, t - 3)
                        for br, (w, y) in enumerate(((wa, ya), (wb, yb))):
                            if t == 0 and br == 1:
                                pe.wait_ge(b_in, 32)
                            for c in range(NCH):
                                mm = pe.matmul(pj[:, t % 4, br], w[:, c, P * j:P * j + P],
                                               y[:, c, 512 * h:512 * h + 512], start=c == 0, stop=c == NCH - 1)
                    elif kind == "o":
                        if t == 0:
                            pe.wait_ge(o_in, 16)
                            pe.wait_ge(mt_ready, M)
                        if t >= 2:
                            pe.wait_ge(read, M + t - 1)
                        for h in range(2):
                            for k in range(KD):
                                mm = pe.matmul(pj[:, t % 2, h], mT[:, k, P * t:P * t + P],
                                               wo[:, k, 512 * h:512 * h + 512], start=k == 0, stop=k == KD - 1)
                    elif kind == "h":
                        pe.wait_ge(xn_ready, t + 1)
                        if t:
                            pe.wait_ge(h_ready, KD * t)
                        for k in range(KD):
                            mm = pe.transpose(pj[:, 2, k // 4, P * (k % 4):P * (k % 4) + P], xn[:, t % 2, P * k:P * k + P],
                                              ident[:])
                    else:
                        if t == 0:
                            pe.wait_ge(r_in, 16)
                        pe.wait_ge(h_ready, KD * (t + 1))
                        for k in range(KD):
                            mm = pe.matmul(pj[:, 3, 0, NE * t:NE * t + NE], h2[:, t % 2, k, :], router[:, k, :],
                                           start=k == 0, stop=k == KD - 1)
                    mm.then_inc(job, 1)
                pe.wait_ge(sm_step, 6)
                for t in range(NT):
                    mm = pe.transpose(pj[0:NE, 2, t // 4, P * (t % 4):P * (t % 4) + P], ex[:, t, :], ident[:])
                mm.then_inc(aff_t, 1)

            @block.scalar
            def _(act):
                for t in range(NT):
                    act.wait_ge(xnew_ready, t + 1)
                    if t:
                        act.wait_ge(sq_ready, t)
                    act.activation(junk[:], xnew[:, t % XB, :], ACT.Square, accum_out=ss[:, t:t + 1]).then_inc(sq_ready, 1)
                    act.wait_ge(v_step, 6 * t + 1)
                    act.activation(rt[:, t:t + 1], ss[:, t:t + 1], ACT.Sqrt).then_inc(rt_ready, 1)
                    act.wait_ge(xn_ready, t + 1)
                    act.dma_start(g["xn2_dram"][P * t:P * t + P, :], xn[:, t % 2, :]).then_inc(xn_stored[t % 2], 16)
                act.wait_ge(sm_step, 3)
                act.activation(ex[:], lg[:], ACT.Exp).then_inc(exp_done, 1)
                for i in range(2):
                    act.wait_ge(xn_stored[i], 16 * (NT // 2))

            @block.vector
            def _(dve):
                for i in range(M):
                    j, h = divmod(i, 2)
                    b = pj[:, i % 4]
                    dve.wait_ge(job, i + 1)
                    dve.wait_ge(gates_in[i % 2], 16 * (i // 2 + 1))
                    part = slice(512 * h, 512 * h + 512)
                    if i >= 2:
                        dve.wait_ge(mt_ready, i - 1)
                    dve.tensor_tensor(ta[:, i % 2], gates[:, i % 2, 0], b[:, 0], ALU.mult).then_inc(mul, 1)
                    dve.tensor_tensor(tb[:, i % 2], gates[:, i % 2, 1], b[:, 1], ALU.mult).then_inc(read, 1)
                    dve.wait_ge(mul, i + 1)
                    dve.wait_ge(read, i + 1)
                    dve.tensor_tensor(mT[:, j, part], ta[:, i % 2], tb[:, i % 2], ALU.add).then_inc(mt_ready, 1)

                def new_rows(t):
                    xt, c = xnew[:, t % XB, :], slice(t, t + 1)
                    dve.wait_ge(job, n_job[("o", t)])
                    if t >= XB:
                        dve.wait_ge(x_stored[t % XB], 16 * (t // XB))
                        dve.wait_ge(xn_ready, t - XB + 1)
                    dve.tensor_tensor(xt, pj[:, t % 2].rearrange("p a n -> p (a n)"), g["g1row"][:], ALU.mult)\
                       .then_inc(read, 1)
                    dve.wait_ge(read, M + t + 1)
                    dve.wait_ge(xr_in[t % 2], 16 * (t // 2 + 1))
                    dve.tensor_tensor(xt, xt, x[:, t % 2], ALU.add).then_inc(xnew_ready, 1)
                    dve.wait_ge(sq_ready, t + 1)
                    dve.tensor_scalar(ss[:, c], ss[:, c], 1.0 / D, EPS, ALU.mult, ALU.add).then_inc(v_step, 1)
                    inverse_root(dve, rt_ready, v_step, 6 * t + 1, ss[:, c], rt[:, c], rs[:, c], tmp[:, c], t + 1)
                    dve.wait_ge(xnew_ready, t + 1)
                    if t >= 2:
                        dve.wait_ge(xn_stored[t % 2], 16 * (t // 2))
                        dve.wait_ge(job, n_job[("h", t - 2)])
                    dve.tensor_scalar(xn[:, t % 2, :], xt, rs[:, c], None, ALU.mult).then_inc(xn_ready, 1)

                def modulated(t):
                    dve.wait_ge(job, n_job[("h", t)])
                    if t >= 2:
                        dve.wait_ge(job, n_job[("l", t - 2)])
                    for k in range(KD):
                        dve.tensor_scalar(h2[:, t % 2, k, :], pj[:, 2, k // 4, P * (k % 4):P * (k % 4) + P],
                                          A2[:, k:k + 1], mod[:, 24 + k, 0:1], ALU.mult, ALU.add).then_inc(h_ready, 1)

                for t in range(NT):
                    new_rows(t)
                    if t:
                        modulated(t - 1)
                modulated(NT - 1)
                dve.wait_ge(job, n_job[("l", NT - 1)])
                dve.tensor_reduce(mxl[:], logit_bank, AX, ALU.max).then_inc(sm_step, 1)
                dve.wait_ge(sm_step, 1)
                dve.tensor_copy(lg[:], logit_bank).then_inc(sm_step, 1)
                dve.wait_ge(sm_step, 2)
                dve.tensor_tensor(lg[:], lg[:], mxl[:].unsqueeze(2).broadcast_to([P, NT, NE]), ALU.subtract)\
                   .then_inc(sm_step, 1)
                dve.wait_ge(exp_done, 1)
                dve.tensor_reduce(sm[:], ex[:], AX, ALU.add).then_inc(sm_step, 1)
                dve.wait_ge(sm_step, 4)
                dve.reciprocal(sm[:], sm[:]).then_inc(sm_step, 1)
                dve.wait_ge(sm_step, 5)
                dve.tensor_tensor(ex[:], ex[:], sm[:].unsqueeze(2).broadcast_to([P, NT, NE]), ALU.mult)\
                   .then_inc(sm_step, 1)
                dve.wait_ge(aff_t, 1)
                dve.tensor_copy(g["affT"], pj[0:NE, 2].rearrange("p a n -> p (a n)"))


def load_unit(sp, g, e, i):
    if i < 4 * FQ:
        n = 4
        c, q = divmod(i, 4)
        w = g["A"]["w_gate"] if q < 2 else g["A"]["w_up"]
        rows, columns = slice(512 * (q % 2), 512 * (q % 2) + 512), slice(512 * c, 512 * c + 512)
    else:
        n = 2
        j = i - 4 * FQ
        w, rows, columns = g["A"]["w_down"], slice(256 * j, 256 * j + 256), slice(0, D)
    src = w[0][bass.ds(e, 1), rows, columns].rearrange("e (k p) n -> p (e k) n", p=P)
    sp.dma_start(g["ring"][:, i % RAW].rearrange("p (k n) -> p k n", k=n), src).then_inc(g["raw_in"][i % RAW], 16)


def choice(g):
    nc, sem = g["nc"], g["sem"]
    aff, ident = g["affT"], g["ident"]
    R = CAP // 8
    with ExitStack() as s:
        sb, ps = g["scope"](s)
        vals, idx = sb("vals", [NE, CAP]), sb("idx_rows", [NE, CAP], U32)
        idx_f = sb("idx_f", [NE, CAP])
        p_c = ps("p_c", [P, 2, 512])
        best, found, gone = sem("best"), sem("found"), sem("gone")
        as_float, turned, kept = sem("as_float"), sem("turned"), sem("kept")

        with nc.Block() as block:
            @block.vector
            def _(dve):
                for r in range(R):
                    at = slice(8 * r, 8 * r + 8)
                    if r:
                        dve.wait_ge(gone, r)
                    dve.max(vals[:, at], aff).then_inc(best, 1)
                    dve.wait_ge(best, r + 1)
                    dve.max_index(idx[:, at], vals[:, at], aff).then_inc(found, 1)
                    dve.wait_ge(found, r + 1)
                    dve.match_replace(aff, vals[:, at], aff, -1.0).then_inc(gone, 1)
                dve.tensor_copy(idx_f[:], idx[:]).then_inc(as_float, 1)
                dve.wait_ge(turned, 1)
                dve.tensor_copy(g["gate"][:], p_c[:, 0, 0:NE]).then_inc(kept, 1)
                dve.tensor_copy(g["idx"][:], p_c[:, 1, 0:NE]).then_inc(kept, 1)
                dve.wait_ge(kept, 2)

            @block.tensor
            def _(pe):
                pe.wait_ge(as_float, 1)
                pe.transpose(p_c[:, 0, 0:NE], vals[:], ident[0:NE, 0:NE])
                pe.transpose(p_c[:, 1, 0:NE], idx_f[:], ident[0:NE, 0:NE]).then_inc(turned, 1)


def experts(g):
    nc, sem, A = g["nc"], g["sem"], g["A"]
    ident, A2, mod, g2row = g["ident"], g["A2"], g["mod"], g["g2row"]
    idx, gate, ring, raw_in = g["idx"], g["gate"], g["ring"], g["raw_in"]
    with ExitStack() as s:
        sb, ps = g["scope"](s)
        r_hi, r_lo = sb("r_hi", [P, PARTS, 2048], F32R), sb("r_lo", [P, PARTS, 2048], F32R)
        xf = sb("xf", [P, 2, 4, P])
        x_hi, x_lo = sb("x_hi", [P, KD, P], F32R), sb("x_lo", [P, KD, P], F32R)
        sg, au = sb("sg", [P, 512]), sb("au", [P, 512])
        a_hi, a_lo = sb("a_hi", [P, FF // P, P], F32R), sb("a_lo", [P, FF // P, P], F32R)
        xe, yo = g["g1row"], g["late"]
        idx_e = sb("idx_e", [P, 1], U32)
        idx_s = sb("idx_s", [P, 2], U32)
        gate_e = sb("gate_e", [P, 1])
        p_a = ps("p_a", [P, 2, 512])
        p_b = ps("p_b", [P, 512])
        p_y = ps("p_y2", [P, D])
        p_t = ps("p_t2", [P, 2, 512])
        hi_ready, lo_ready, unit_done = sem("hi_ready"), sem("lo_ready"), sem("unit_done")
        idx_ready, gathered, gate_ready = sem("idx_ready"), sem("gathered"), sem("gate_ready")
        turn, turn_f, turn_hi, turn_lo = sem("turn"), sem("turn_f"), sem("turn_hi"), sem("turn_lo")
        sg_ready, au_step = sem("sg_ready"), sem("au_step")
        yo_ready, added = sem("yo_ready"), sem("added")
        pool_passed = sem("pool_passed")

        def each_expert(eng, body, first=True, last=True):
            body(0, True, False)
            with eng.Fori(1, NE - 1) as e:
                body(e, False, False)
            body(NE - 1, False, True)

        with nc.Block() as block:
            @block.sync
            def _(sp):
                def body(e, first, last):
                    for i in range(EU):
                        if first and i < RAW:
                            continue
                        sp.wait_ge(lo_ready, EU * e + i - RAW + 1)
                        load_unit(sp, g, e, i)
                each_expert(sp, body)

            @block.gpsimd
            def _(pool):
                def gather(e):
                    pool.wait_ge(idx_ready, e + 1)
                    pool.sem_inc(pool_passed, 1)
                    pool.indirect_dma_start(out=xe[:], out_offset=None, in_=g["xn2_dram"][:, :],
                                            in_offset=bass.IndirectOffsetOnAxis(ap=idx_e[:, 0:1], axis=0))\
                        .then_inc(gathered, 16)

                def body(e, first, last):
                    if not last:
                        gather(e + 1)
                    pool.wait_ge(yo_ready, e + 1)
                    if not first:
                        pool.wait_ge(added, 16 * e)
                    pool.sem_inc(pool_passed, 1)
                    pool.indirect_dma_start(out=g["out"][0], in_=yo[:], in_offset=None,
                                            out_offset=bass.IndirectOffsetOnAxis(ap=idx_s[:, 0:1], axis=0),
                                            compute_op=ALU.add).then_inc(added, 16)
                gather(0)
                each_expert(pool, body)
                pool.wait_ge(added, 16 * NE)

            @block.scalar
            def _(act):
                def high_part(e, i, before=None):
                    act.wait_ge(raw_in[i % RAW], 16 * (EU // RAW * e + i // RAW + 1))
                    if not before:
                        act.wait_ge(unit_done, EU * e + i - PARTS + 1)
                    act.activation(r_hi[:, i % PARTS], ring[:, i % RAW], ACT.Copy).then_inc(hi_ready, 1)

                def turn_x(e, q):
                    act.wait_ge(turn_f, 2 * e + q + 1)
                    act.activation(x_hi[:, 4 * q:4 * q + 4, :], xf[:, q], ACT.Copy).then_inc(turn_hi, 1)

                def body(e, first, last):
                    for i in range(EU):
                        if not (last and i + AHEAD >= EU):
                            high_part(e, i + AHEAD, first and i + AHEAD < PARTS)
                        if i < 4 * FQ and i % 4 == 3:
                            c = i // 4
                            act.wait_ge(unit_done, EU * e + i - 1)
                            if not (first and c == 0):
                                act.wait_ge(au_step, 2 * (FQ * e + c))
                            act.activation(sg[:], p_a[:, c % 2], ACT.Sigmoid).then_inc(sg_ready, 1)
                        for q in np.atleast_1d(TURN_AT.get(i, [])).astype(int).tolist():
                            if q in (3, 4):
                                if not last:
                                    turn_x(e + 1, q - 3)
                                continue
                            c = min(q, 3)
                            act.wait_ge(turn, turns(e, q, last))
                            act.activation(a_hi[:, 4 * c:4 * c + 4, :].rearrange("p k m -> p (k m)"), p_t[:, q % 2],
                                           ACT.Copy).then_inc(turn_hi, 1)
                for i in range(AHEAD):
                    high_part(0, i, True)
                for q in range(2):
                    turn_x(0, q)
                each_expert(act, body)

            @block.vector
            def _(dve):
                def low_part(e, i):
                    dve.wait_ge(hi_ready, EU * e + i + 1)
                    dve.tensor_tensor(r_lo[:, i % PARTS], ring[:, i % RAW], r_hi[:, i % PARTS].bitcast(F32),
                                      ALU.subtract).then_inc(lo_ready, 1)

                def take_index(e, first):
                    if not first:
                        dve.wait_ge(gathered, 16 * e)
                    dve.tensor_copy(idx_e[:, 0:1], idx[:, bass.ds(e, 1)]).then_inc(idx_ready, 1)

                def turn_x(e, q, n, bank):
                    dve.wait_ge(turn, n + 1)
                    for k in range(4):
                        ins = dve.tensor_scalar(xf[:, q, k, :], p_t[:, bank, P * k:P * k + P],
                                                A2[:, 4 * q + k:4 * q + k + 1], mod[:, 24 + 4 * q + k, 0:1],
                                                ALU.mult, ALU.add)
                    ins.then_inc(turn_f, 1)
                    dve.wait_ge(turn_hi, n + 1)
                    dve.tensor_tensor(x_lo[:, 4 * q:4 * q + 4, :], xf[:, q], x_hi[:, 4 * q:4 * q + 4, :].bitcast(F32),
                                      ALU.subtract).then_inc(turn_lo, 1)

                def body(e, first, last):
                    for i in range(EU):
                        if not (last and i + AHEAD >= EU):
                            low_part(e, i + AHEAD)
                        if i == 0 and not last:
                            take_index(e + 1, False)
                        if i == EU // 2:
                            if not first:
                                dve.wait_ge(yo_ready, e)
                                dve.wait_ge(added, 16 * e)
                            dve.tensor_copy(gate_e[:, 0:1], gate[:, bass.ds(e, 1)]).then_inc(gate_ready, 1)
                            dve.tensor_copy(idx_s[:, 0:1], idx[:, bass.ds(e, 1)])
                        if i < 4 * FQ and i % 4 == 3:
                            c = i // 4
                            dve.wait_ge(sg_ready, FQ * e + c + 1)
                            if not (first and c == 0):
                                dve.wait_ge(turn, turns(e, c - 1, last) if c else turns_before(e))
                            dve.tensor_tensor(au[:], sg[:], p_a[:, c % 2], ALU.mult).then_inc(au_step, 1)
                            dve.wait_ge(au_step, 2 * (FQ * e + c) + 1)
                            dve.wait_ge(unit_done, EU * e + i + 1)
                            dve.tensor_tensor(au[:], au[:], p_b[:], ALU.mult).then_inc(au_step, 1)
                        for q in np.atleast_1d(TURN_AT.get(i, [])).astype(int).tolist():
                            if q in (3, 4):
                                if not last:
                                    turn_x(e + 1, q - 3, turns(e, q, last) - 1, q % 2)
                                continue
                            c = min(q, 3)
                            n = turns(e, q, last)
                            dve.wait_ge(turn_hi, n)
                            dve.tensor_tensor(a_lo[:, 4 * c:4 * c + 4, :].rearrange("p k m -> p (k m)"), p_t[:, q % 2],
                                              a_hi[:, 4 * c:4 * c + 4, :].rearrange("p k m -> p (k m)").bitcast(F32),
                                              ALU.subtract).then_inc(turn_lo, 1)
                        if i == EU - 1:
                            dve.wait_ge(unit_done, EU * e + EU)
                            dve.wait_ge(gate_ready, e + 1)
                            dve.scalar_tensor_tensor(out=yo[:], in0=p_y[:], scalar=gate_e[:, 0:1], in1=g2row[:],
                                                     op0=ALU.mult, op1=ALU.mult).then_inc(yo_ready, 1)
                take_index(0, True)
                for i in range(AHEAD):
                    low_part(0, i)
                for q in range(2):
                    turn_x(0, q, q, q)
                each_expert(dve, body)

            @block.tensor
            def _(pe):
                def turn_x(e, q, n, bank):
                    if q == 0:
                        pe.wait_ge(gathered, 16 * (e + 1))
                    if not (isinstance(n, int) and n < 2):
                        pe.wait_ge(turn_lo, n - 1)
                    for k in range(4):
                        mm = pe.transpose(p_t[:, bank, P * k:P * k + P], xe[:, P * (4 * q + k):P * (4 * q + k) + P],
                                          ident[:])
                    mm.then_inc(turn, 1)

                def turn_a(e, q, n):
                    c = min(q, 3)
                    pe.wait_ge(au_step, 2 * (FQ * e + c + 1))
                    pe.wait_ge(turn_lo, n - 1)
                    for k in range(4):
                        mm = pe.transpose(p_t[:, q % 2, P * k:P * k + P], au[:, P * k:P * k + P], ident[:])
                    mm.then_inc(turn, 1)

                def body(e, first, last):
                    for i in range(EU):
                        pe.wait_ge(lo_ready, EU * e + i + 1)
                        hi, lo = r_hi[:, i % PARTS], r_lo[:, i % PARTS]
                        if i < 4 * FQ:
                            c, q = divmod(i, 4)
                            out = p_a[:, c % 2] if q < 2 else p_b[:]
                            if i == 0:
                                pe.wait_ge(turn_lo, turns_before(e))
                            if q == 0 and not (first and c < 2):
                                pe.wait_ge(au_step, 2 * (FQ * e + c - 1))
                            if q == 2 and not (first and c == 0):
                                pe.wait_ge(au_step, 2 * (FQ * e + c))
                            for k in range(4):
                                kk = 4 * (q % 2) + k
                                mm = three(pe, out, x_hi[:, kk, :], x_lo[:, kk, :], hi[:, 512 * k:512 * k + 512],
                                           lo[:, 512 * k:512 * k + 512], kk == 0, kk == KD - 1)
                        else:
                            j = i - 4 * FQ
                            if j == 0 and not first:
                                pe.wait_ge(yo_ready, e)
                            if j % 2 == 0:
                                c = j // 2
                                pe.wait_ge(turn_lo, turns(e, c if c < 3 else 5, last))
                            for k in range(2):
                                kk = 2 * j + k
                                for h in range(2):
                                    at = slice(D * k + 512 * h, D * k + 512 * h + 512)
                                    mm = three(pe, p_y[:, 512 * h:512 * h + 512], a_hi[:, kk, :], a_lo[:, kk, :],
                                               hi[:, at], lo[:, at], kk == 0, kk == FF // P - 1)
                        mm.then_inc(unit_done, 1)
                        for q in np.atleast_1d(TURN_AT.get(i, [])).astype(int).tolist():
                            n = turns(e, q, last) - 1
                            if q in (3, 4):
                                if not last:
                                    turn_x(e + 1, q - 3, n, q % 2)
                            else:
                                turn_a(e, q, n)
                for q in range(2):
                    turn_x(0, q, q, q)
                each_expert(pe, body)


def turns_before(e):
    return TURNS * e + 2


def turns(e, q, last):
    return TURNS * e + q + 3 - (2 if last and q == 5 else 0)


INPUTS = ["x", "c", "ctx", "c_ctx", "ada_w", "ada_b", "norm1", "norm2", "w_in", "conv_w", "conv_b", "filt_w1",
          "filt_b1", "filt_w2", "filt_b2", "filt_w3", "filt_b3", "filt_freq", "filt_out", "hyena_bias", "q_norm",
          "k_norm", "attn_sink", "w_branch_a", "w_branch_b", "w_out", "router", "w_gate", "w_up", "w_down"]


def kernel(**inputs):
    from concourse import bacc
    from concourse.bass_utils import run_bass_kernel_spmd

    nc = bacc.Bacc("TRN2", target_bir_lowering=False, num_devices=1)
    arrays = {f"in_{n}": np.ascontiguousarray(inputs[n]) for n in INPUTS}
    arrays.update({f"in_{n}": a for n, a in shape_constants().items()})
    A = {n[3:]: nc.dram_tensor(n, a.shape, mybir.dt.from_np(a.dtype), kind="ExternalInput").ap()
         for n, a in arrays.items()}
    out = nc.dram_tensor("out_x", (1, L, D), F32, kind="ExternalOutput").ap()
    build(nc, A, out)
    r = run_bass_kernel_spmd(nc, [arrays], core_ids=[0])
    return r.results[0]["out_x"]
```
